# Optimizing a Trainium2 kernel written in Bass

```python
import math
import jax
import jax.numpy as jnp
from jax import lax
import numpy as np

D_MODEL = 1024
BATCH = 1
SEQ = 256
DEPTH = 1

N_META = 16
N_HEADS = 16
N_KV_HEADS = 4
HEAD_DIM = 64
Q_PER_KV = N_HEADS // N_KV_HEADS
Q_DIM = N_HEADS * HEAD_DIM
KV_DIM = N_KV_HEADS * HEAD_DIM
WINDOW = 128
ATT_BLOCK = 128
N_BUCKETS = 32
MAX_DISTANCE = 128
SSM_EXPAND = 2
D_INNER = SSM_EXPAND * D_MODEL
SSM_HEAD_DIM = 64
N_SSM_HEADS = D_INNER // SSM_HEAD_DIM
N_GROUPS = 4
HEADS_PER_GROUP = N_SSM_HEADS // N_GROUPS
D_STATE = 128
CONV_WIDTH = 4
CONV_DIM = D_INNER + 2 * N_GROUPS * D_STATE
CHUNK = 128
DT_MIN = 0.001
DT_MAX = 0.1
N_EXPERTS = 32
TOP_K = 4
D_FF = D_MODEL
SWIGLU_ALPHA = 1.702
SWIGLU_LIMIT = 7.0
MOE_BLOCK = 256
N_BRANCHES = 2
EPS = 1e-5
IN_SIZES = (Q_DIM, KV_DIM, KV_DIM, D_INNER, CONV_DIM, N_SSM_HEADS, N_BRANCHES * D_MODEL)
IN_DIM = sum(IN_SIZES)

kernel_name = "hybrid_swa_ssd_moe_block"

def rms_norm(x, g):
    xf = x.astype(jnp.float32)
    y = xf * lax.rsqrt(jnp.mean(xf * xf, axis=-1, keepdims=True) + EPS)
    return (y * g.astype(jnp.float32)).astype(x.dtype)

def t5_bucket(dist):
    n = jnp.maximum(dist, 0)
    max_exact = N_BUCKETS // 2
    nf = jnp.maximum(n, 1).astype(jnp.float32)
    large = max_exact + (jnp.log(nf / max_exact) / math.log(MAX_DISTANCE / max_exact)
                         * (N_BUCKETS - max_exact)).astype(jnp.int32)
    large = jnp.minimum(large, N_BUCKETS - 1)
    return jnp.where(n < max_exact, n, large)

def sink_softmax(logits, sinks):
    sink = jnp.broadcast_to(sinks, logits.shape[:-1] + (1,))
    p = jax.nn.softmax(jnp.concatenate([logits, sink], axis=-1), axis=-1)
    return p[..., :-1]

def sliding_window_attention(q, k, v, sinks, rel_bias):
    Bsz, L = q.shape[0], q.shape[1]
    S = L - N_META
    nb = S // ATT_BLOCK
    ctx = N_META + 2 * ATT_BLOCK
    scale = HEAD_DIM ** -0.5
    sinks_f = sinks.astype(jnp.float32).reshape(N_KV_HEADS, Q_PER_KV)[:, :, None, None]
    table = rel_bias.astype(jnp.float32)

    qm = q[:, :N_META].reshape(Bsz, N_META, N_KV_HEADS, Q_PER_KV, HEAD_DIM)
    km, vm = k[:, :N_META], v[:, :N_META]
    im = jnp.arange(N_META, dtype=jnp.int32)
    dist_m = im[:, None] - im[None, :]
    bias_m = table[t5_bucket(dist_m)].reshape(N_META, N_META, N_KV_HEADS, Q_PER_KV).transpose(2, 3, 0, 1)
    lm = jnp.einsum('bqkgd,bskd->bkgqs', qm, km).astype(jnp.float32) * scale + bias_m
    lm = jnp.where(dist_m >= 0, lm, -jnp.inf)
    pm = sink_softmax(lm, sinks_f)
    om = jnp.einsum('bkgqs,bskd->bqkgd', pm.astype(v.dtype), vm).reshape(Bsz, N_META, Q_DIM)

    qr = q[:, N_META:].reshape(Bsz, nb, ATT_BLOCK, N_KV_HEADS, Q_PER_KV, HEAD_DIM)

    def with_context(t, t_meta):
        t = t.reshape(Bsz, nb, ATT_BLOCK, N_KV_HEADS, HEAD_DIM)
        prev = jnp.concatenate([jnp.zeros_like(t[:, :1]), t[:, :-1]], axis=1)
        meta = jnp.broadcast_to(t_meta[:, None], (Bsz, nb, N_META, N_KV_HEADS, HEAD_DIM))
        return jnp.concatenate([meta, prev, t], axis=2)

    kc = with_context(k[:, N_META:], km)
    vc = with_context(v[:, N_META:], vm)

    n_idx = jnp.arange(nb, dtype=jnp.int32)[:, None]
    j = jnp.arange(ATT_BLOCK, dtype=jnp.int32)[None, :]
    kpos = jnp.concatenate([
        jnp.broadcast_to(jnp.arange(N_META, dtype=jnp.int32)[None, :], (nb, N_META)),
        N_META + (n_idx - 1) * ATT_BLOCK + j,
        N_META + n_idx * ATT_BLOCK + j], axis=1)
    qpos = N_META + n_idx * ATT_BLOCK + j
    dist = qpos[:, :, None] - kpos[:, None, :]
    is_meta_slot = (jnp.arange(ctx) < N_META)[None, None, :]
    valid = is_meta_slot | ((dist >= 0) & (dist < WINDOW) & (kpos[:, None, :] >= N_META))
    bias = table[t5_bucket(dist)].reshape(nb, ATT_BLOCK, ctx, N_KV_HEADS, Q_PER_KV).transpose(0, 3, 4, 1, 2)

    logits = jnp.einsum('bnqkgd,bnskd->bnkgqs', qr, kc).astype(jnp.float32) * scale + bias[None]
    logits = jnp.where(valid[None, :, None, None], logits, -jnp.inf)
    p = sink_softmax(logits, sinks_f)
    o = jnp.einsum('bnkgqs,bnskd->bnqkgd', p.astype(v.dtype), vc).reshape(Bsz, S, Q_DIM)
    return jnp.concatenate([om, o], axis=1)

def causal_depthwise_conv(u, w, b):
    y = lax.conv_general_dilated(
        u, w[:, None, :].astype(u.dtype), window_strides=(1,), padding=[(CONV_WIDTH - 1, 0)],
        dimension_numbers=('NWC', 'WIO', 'NWC'), feature_group_count=u.shape[-1])
    return y + b.astype(u.dtype)

def ssd_scan(x, dt, A, Bm, Cm):
    Bsz, Lp = x.shape[0], x.shape[1]
    nc = Lp // CHUNK
    xc = x.reshape(Bsz, nc, CHUNK, N_GROUPS, HEADS_PER_GROUP, SSM_HEAD_DIM)
    dtc = dt.reshape(Bsz, nc, CHUNK, N_GROUPS, HEADS_PER_GROUP)
    Bc = Bm.reshape(Bsz, nc, CHUNK, N_GROUPS, D_STATE)
    Cc = Cm.reshape(Bsz, nc, CHUNK, N_GROUPS, D_STATE)
    a = jnp.moveaxis(dtc * A.reshape(N_GROUPS, HEADS_PER_GROUP), 2, -1)
    a_cs = jnp.cumsum(a, axis=-1)
    xdt = xc * dtc[..., None]

    causal = jnp.tril(jnp.ones((CHUNK, CHUNK), dtype=bool))
    decay = jnp.exp(jnp.where(causal, a_cs[..., :, None] - a_cs[..., None, :], -jnp.inf))
    cb = jnp.einsum('bclgn,bcsgn->bcgls', Cc, Bc)
    y_diag = jnp.einsum('bcgls,bcgrls,bcsgrp->bclgrp', cb, decay, xdt)

    decay_to_end = jnp.exp(a_cs[..., -1:] - a_cs)
    states = jnp.einsum('bclgn,bcgrl,bclgrp->bcgrpn', Bc, decay_to_end, xdt)
    chunk_decay = jnp.exp(a_cs[..., -1])

    def step(h, inp):
        s_c, d_c = inp
        return h * d_c[..., None, None] + s_c, h

    h0 = jnp.zeros((Bsz, N_GROUPS, HEADS_PER_GROUP, SSM_HEAD_DIM, D_STATE), jnp.float32)
    _, h_in = lax.scan(step, h0, (jnp.moveaxis(states, 1, 0), jnp.moveaxis(chunk_decay, 1, 0)))
    h_in = jnp.moveaxis(h_in, 0, 1)
    y_off = jnp.einsum('bclgn,bcgrpn,bcgrl->bclgrp', Cc, h_in, jnp.exp(a_cs))
    return (y_diag + y_off).reshape(Bsz, Lp, N_SSM_HEADS, SSM_HEAD_DIM)

def ssd_mixer(z, xbc, dt_raw, conv_w, conv_b, dt_bias, a_log, d_skip, norm_g):
    Bsz, L = z.shape[0], z.shape[1]
    xbc = jax.nn.silu(causal_depthwise_conv(xbc, conv_w, conv_b)).astype(jnp.float32)
    xs = xbc[..., :D_INNER].reshape(Bsz, L, N_SSM_HEADS, SSM_HEAD_DIM)
    Bm = xbc[..., D_INNER:D_INNER + N_GROUPS * D_STATE].reshape(Bsz, L, N_GROUPS, D_STATE)
    Cm = xbc[..., D_INNER + N_GROUPS * D_STATE:].reshape(Bsz, L, N_GROUPS, D_STATE)
    dt = jax.nn.softplus(dt_raw.astype(jnp.float32) + dt_bias.astype(jnp.float32))
    A = -jnp.exp(a_log.astype(jnp.float32))
    pad = CHUNK - N_META

    def padl(t):
        return jnp.pad(t, [(0, 0), (pad, 0)] + [(0, 0)] * (t.ndim - 2))

    y = ssd_scan(padl(xs), padl(dt), A, padl(Bm), padl(Cm))[:, pad:]
    y = y + d_skip.astype(jnp.float32)[:, None] * xs
    y = y.reshape(Bsz, L, D_INNER) * jax.nn.silu(z.astype(jnp.float32))
    yg = y.reshape(Bsz, L, N_GROUPS, D_INNER // N_GROUPS)
    yg = yg * lax.rsqrt(jnp.mean(yg * yg, axis=-1, keepdims=True) + EPS)
    y = yg.reshape(Bsz, L, D_INNER) * norm_g.astype(jnp.float32)
    return y.astype(z.dtype)

def swiglu_clamped(hh):
    x_glu = jnp.minimum(hh[..., ::2], SWIGLU_LIMIT)
    x_lin = jnp.clip(hh[..., 1::2], -SWIGLU_LIMIT, SWIGLU_LIMIT)
    return x_glu * jax.nn.sigmoid(SWIGLU_ALPHA * x_glu) * (x_lin + 1.0)

def moe_ffn(u, w_router, b_router, w1, b1, w2, b2):
    T = u.shape[0]
    logits = (u @ w_router + b_router).astype(jnp.float32)
    top_vals, top_idx = lax.top_k(logits, TOP_K)
    top_w = jax.nn.softmax(top_vals, axis=-1).astype(u.dtype)
    n_assign = T * TOP_K
    flat_e = top_idx.reshape(-1)
    flat_tok = jnp.repeat(jnp.arange(T, dtype=jnp.int32), TOP_K)
    flat_w = top_w.reshape(-1)
    order = jnp.argsort(flat_e)
    sorted_e = flat_e[order]
    counts = jnp.bincount(flat_e, length=N_EXPERTS)
    padded = (counts + MOE_BLOCK - 1) // MOE_BLOCK * MOE_BLOCK
    start = jnp.cumsum(counts) - counts
    pend = jnp.cumsum(padded)
    pstart = pend - padded
    dest = jnp.arange(n_assign, dtype=jnp.int32) + (pstart - start)[sorted_e]
    n_rows = -(-(n_assign + N_EXPERTS * (MOE_BLOCK - 1)) // MOE_BLOCK) * MOE_BLOCK
    n_blocks = n_rows // MOE_BLOCK
    row_tok = jnp.zeros((n_rows,), jnp.int32).at[dest].set(flat_tok[order])
    row_w = jnp.zeros((n_rows,), u.dtype).at[dest].set(flat_w[order])
    block_e = jnp.minimum(
        jnp.searchsorted(pend, jnp.arange(n_blocks, dtype=jnp.int32) * MOE_BLOCK, side='right'),
        N_EXPERTS - 1)

    def body(acc, inp):
        tok, wt, e = inp
        hb = swiglu_clamped(u[tok] @ w1[e] + b1[e])
        yb = (hb @ w2[e] + b2[e]) * wt[:, None]
        return acc.at[tok].add(yb), None

    out, _ = lax.scan(body, jnp.zeros_like(u),
                      (row_tok.reshape(n_blocks, MOE_BLOCK), row_w.reshape(n_blocks, MOE_BLOCK), block_e))
    return out

def setup_inputs(seed: int = 0) -> dict:
    key = jax.random.key(seed)
    ks = jax.random.split(key, 24)

    def nrm(k, shape, scale):
        return jax.random.normal(k, shape, jnp.float32) * scale

    def gain(k, shape):
        return 1.0 + nrm(k, shape, 0.02)

    dt0 = jnp.exp(jax.random.uniform(ks[8], (DEPTH, N_SSM_HEADS), jnp.float32)
                  * (math.log(DT_MAX) - math.log(DT_MIN)) + math.log(DT_MIN))
    return {
        "x": nrm(ks[0], (BATCH, SEQ, D_MODEL), 1.0),
        "meta_tokens": nrm(ks[1], (N_META, D_MODEL), 1.0),
        "rel_bias": nrm(ks[2], (N_BUCKETS, N_HEADS), 0.5),
        "norm_mix_g": gain(ks[3], (DEPTH, D_MODEL)),
        "w_in": nrm(ks[4], (DEPTH, D_MODEL, IN_DIM), D_MODEL ** -0.5),
        "attn_sinks": nrm(ks[5], (DEPTH, N_HEADS), 0.5),
        "conv_w": nrm(ks[6], (DEPTH, CONV_WIDTH, CONV_DIM), CONV_WIDTH ** -0.5),
        "conv_b": nrm(ks[7], (DEPTH, CONV_DIM), 0.01),
        "dt_bias": dt0 + jnp.log(-jnp.expm1(-dt0)),
        "a_log": jnp.log(jax.random.uniform(ks[9], (DEPTH, N_SSM_HEADS), jnp.float32, 1.0, 16.0)),
        "d_skip": gain(ks[10], (DEPTH, N_SSM_HEADS)),
        "ssm_norm_g": gain(ks[11], (DEPTH, D_INNER)),
        "w_attn_br": nrm(ks[12], (DEPTH, Q_DIM, D_MODEL), Q_DIM ** -0.5),
        "w_ssm_br": nrm(ks[13], (DEPTH, D_INNER, D_MODEL), D_INNER ** -0.5),
        "w_out": nrm(ks[14], (DEPTH, D_MODEL, D_MODEL), D_MODEL ** -0.5),
        "norm_ffn_g": gain(ks[15], (DEPTH, D_MODEL)),
        "w_router": nrm(ks[16], (DEPTH, D_MODEL, N_EXPERTS), D_MODEL ** -0.5),
        "b_router": nrm(ks[17], (DEPTH, N_EXPERTS), 0.01),
        "w_exp_in": nrm(ks[18], (DEPTH, N_EXPERTS, D_MODEL, 2 * D_FF), D_MODEL ** -0.5),
        "b_exp_in": nrm(ks[19], (DEPTH, N_EXPERTS, 2 * D_FF), 0.01),
        "w_exp_out": nrm(ks[20], (DEPTH, N_EXPERTS, D_FF, D_MODEL), D_FF ** -0.5),
        "b_exp_out": nrm(ks[21], (DEPTH, N_EXPERTS, D_MODEL), 0.01),
        "norm_final_g": gain(ks[22], (D_MODEL,)),
    }

def reference(x, meta_tokens, rel_bias, norm_mix_g, w_in, attn_sinks, conv_w, conv_b, dt_bias, a_log,
              d_skip, ssm_norm_g, w_attn_br, w_ssm_br, w_out, norm_ffn_g, w_router, b_router,
              w_exp_in, b_exp_in, w_exp_out, b_exp_out, norm_final_g):
    Bsz = x.shape[0]
    meta = jnp.broadcast_to(meta_tokens[None].astype(x.dtype), (Bsz, N_META, D_MODEL))
    h = jnp.concatenate([meta, x], axis=1)
    L = h.shape[1]
    splits = np.cumsum(IN_SIZES)[:-1].tolist()
    for layer in range(DEPTH):
        u = rms_norm(h, norm_mix_g[layer])
        q, k, v, z, xbc, dt_raw, gate_logits = jnp.split(u @ w_in[layer], splits, axis=-1)
        y_attn = sliding_window_attention(
            q.reshape(Bsz, L, N_HEADS, HEAD_DIM), k.reshape(Bsz, L, N_KV_HEADS, HEAD_DIM),
            v.reshape(Bsz, L, N_KV_HEADS, HEAD_DIM), attn_sinks[layer], rel_bias)
        y_ssm = ssd_mixer(z, xbc, dt_raw, conv_w[layer], conv_b[layer], dt_bias[layer], a_log[layer],
                          d_skip[layer], ssm_norm_g[layer])
        gates = jax.nn.sigmoid(gate_logits.astype(jnp.float32)).astype(h.dtype).reshape(Bsz, L, N_BRANCHES, D_MODEL)
        merged = gates[:, :, 0] * (y_attn @ w_attn_br[layer]) + gates[:, :, 1] * (y_ssm @ w_ssm_br[layer])
        h = h + merged @ w_out[layer]
        u = rms_norm(h, norm_ffn_g[layer]).reshape(Bsz * L, D_MODEL)
        h = h + moe_ffn(u, w_router[layer], b_router[layer], w_exp_in[layer], b_exp_in[layer],
                        w_exp_out[layer], b_exp_out[layer]).reshape(Bsz, L, D_MODEL)
    h = rms_norm(h, norm_final_g)
    return h[:, N_META:]


_drawn_inputs = setup_inputs


def setup_inputs(seed=0):
    import zlib

    import numpy as np

    out = dict(_drawn_inputs(seed))
    spreads = {}
    factors = {'attn_sinks': 8.0, 'b_exp_in': 8.0, 'b_exp_out': 8.0, 'norm_final_g': 2.83}
    for name, (base, spread) in spreads.items():
        noise = np.random.default_rng([zlib.crc32(name.encode()), seed]).standard_normal(out[name].shape)
        drawn = base * np.exp(spread * noise) if base else spread * noise
        out[name] = jnp.asarray(drawn.astype(out[name].dtype))
    for name, factor in factors.items():
        out[name] = (out[name] * factor).astype(out[name].dtype)
    return out
```

```python
import math
from contextlib import ExitStack

import numpy as np

import concourse.bass as bass
from concourse import mybir

F32 = mybir.dt.float32
BF16 = mybir.dt.bfloat16
U32 = mybir.dt.uint32
I32 = mybir.dt.int32
ALU = mybir.AluOpType
ACT = mybir.ActivationFunctionType
AX = mybir.AxisListType.X

P = 128
D = 1024
KT = D // P
META = 16
SEQ = 256
NT = META + SEQ
BLK = 128
HEADS, KV, HD = 16, 4, 64
NB, MAXD, WINDOW = 32, 128, 128
DI = 2048
SH = 32
G = 4
HPG = SH // G
NS = 128
CW = 4
E = 32
FF = 1024
CAP = 64
PASSES = SEQ // CAP
EPS = 1e-5
ALPHA, LIMIT = 1.702, 7.0
COL_Q, COL_K, COL_V, COL_Z = 0, 1024, 1280, 1536
COL_X = COL_Z + DI
COL_B = COL_X + DI
COL_C = COL_B + G * NS
COL_DT = COL_C + G * NS
COL_G = COL_DT + SH
SLOTS = 12
SLOT = 2048
NEG = -1e30
VL = 400
LK = NT + META + BLK


def distance_one_hots():
    x = np.arange(VL)
    dist = NT - 1 - x
    n = np.maximum(dist, 0)
    exact = NB // 2
    nf = np.maximum(n, 1).astype(np.float32)
    large = exact + (np.log(nf / np.float32(exact)) / np.float32(math.log(MAXD / exact))
                     * np.float32(NB - exact)).astype(np.int32)
    bucket = np.where(n < exact, n, np.minimum(large, NB - 1))
    oh = np.zeros((NB + 1, 2, VL), np.float32)
    oh[bucket, :, x] = 1.0
    oh[NB, 1, :] = np.where((dist >= 0) & (dist < WINDOW), 0.0, NEG)
    return oh


class Chain:

    def __init__(self, eng, sem, base=0):
        self.eng, self.sem, self.base, self.n = eng, sem, base, 0

    def link(self, ins):
        self.n += 1
        ins.then_inc(self.sem, 1)
        self.eng.wait_ge(self.sem, self.base + self.n)


def hybrid_layer(nc, x, meta, rel, g_mix, w_in, sinks, conv_w, conv_b, dt_bias, a_log, d_skip, g_ssm,
                 w_att, w_ssm, w_out, g_ffn, w_rt, b_rt, w1, b1, w2, b2, g_fin, c_sq, c_oh, out):
    ctx = ExitStack()
    with ctx:
        def sb(name, shape, dt=F32):
            return ctx.enter_context(nc.sbuf_tensor(name, shape, dt))

        def sem(name):
            return ctx.enter_context(nc.semaphore(name))

        ring = sb("ring", [P, SLOTS, SLOT])
        squares = sb("squares", [P, 5, P])
        ident, tri_le, tri_gt, ones, iota2 = (squares[:, i, :] for i in range(5))
        wdt = sb("wdt", [P, KT, SH])
        wrt = sb("wrt", [P, KT, E])
        rows = sb("rows", [P, 2, P])
        cols = sb("cols", [P, 152])
        col_cw, col_cb = cols[:, 0:96], cols[:, 96:120]
        col_gmix, col_gffn, col_gssm = cols[:, 120:128], cols[:, 128:136], cols[:, 136:152]
        dtb, alog, dskip, brt = (sb(n, [P, 32]) for n in ("dtb", "alog", "dskip", "brt"))
        sink_nat, sink_p = sb("sink_nat", [P, HEADS]), sb("sink_p", [P, HEADS])
        half_neg = sb("half_neg", [P, 8])
        ssq, rstd = sb("ssq", [P, 8]), sb("rstd", [P, 8])
        dts = sb("dts", [P, 7, 96])
        dt, aa = dts[:, 0, :], dts[:, 1, :]
        decays = sb("decays", [P, 3, 3, SH])
        stats = sb("stats", [P, 6, 4])
        tab = sb("tab", [NB + 1, 2, HEADS])
        arena = sb("arena", [P, 25024])

        def at(off, *shape, dt=F32):
            n = int(np.prod(shape))
            words = n if dt != BF16 else n // 2
            v = arena[:, off:off + words]
            if dt != F32:
                v = v.bitcast(dt)
            if len(shape) == 1:
                return v
            names = "abcd"[:len(shape)]
            return v.rearrange(f"p ({' '.join(names)}) -> p {' '.join(names)}",
                               **{names[i]: shape[i] for i in range(len(shape))})

        uT = at(0, KT, NT)
        yaT = at(2176, KT, SEQ)
        bT, cT = at(4224, G, NT), at(5312, G, NT)
        xTC = at(6400, 2, DI)
        bTC = at(10496, 2, G * NS)
        R = 11520
        qT = at(R, KT, SEQ)
        kz = at(R + 2048, KV, NT)
        vTC = at(R + 3136, 3, KV * HD)
        toep = at(R + 3904, HEADS, LK)
        xin = at(R + 3904, 3, D)
        logit = at(R + 10560, 2, 2, LK)
        ohs = at(R + 10560, 2, VL)
        avec = at(R + 11360, 2, VL)
        pT = at(R + 12224, 2, 640)
        zy = at(R, 2, DI)
        hst = at(R + 4096, G, HPG * HD)
        S0 = R + 6144
        xpre, cv, sg = at(S0, 2, 276), at(S0 + 552, 2, NT), at(S0 + 1096, 2, NT)
        xs = at(S0 + 1640, 3, NT)
        xm, xdec0 = at(S0 + 2456, 512), at(S0 + 2968, 512)
        ztmp = at(S0 + 3480, 2, 512)
        au = at(S0, 2, HPG, BLK)
        em = at(S0 + 2048, 2, HPG, BLK)
        cbm = at(S0 + 4096, 2, BLK)
        xdt = at(S0 + 4352, 2, HPG, HD)
        xdec = at(S0 + 5376, HPG, HD)
        ysum = at(S0 + 5888, HPG, HD)
        sq_scratch = at(R + 12544, 512)
        yT = at(S0, 16, SEQ)
        mT = at(6400, KT, SEQ)
        gsig = at(8448, 2, 512)
        gmul = at(9472, 2, 512)
        acc = at(0, 2, D)
        xres = at(4224, 2, D)
        un = at(8448, 2, D)
        u2T = at(2176, KT, SEQ)
        upart = at(R + 10240, 3, 2, D, dt=BF16)
        ures = at(6400, 2, D)
        b1raw = at(R, 2 * FF)
        b1res = at(R + 5120, 1024)
        b1all = at(R + 2048, 2 * FF, dt=BF16)
        b1mid, b1lo = at(R + 3072, 2 * FF, dt=BF16), at(R + 4096, 2 * FF, dt=BF16)
        b2sb = at(4224, D)
        X0 = R + 5120
        s2 = at(X0, SEQ)
        usel = at(X0 + 256, KT, CAP)
        glu, sig, lin, hsw = (at(X0 + 768 + 512 * i, 2, 256) for i in range(4))
        hT = at(X0 + 2816, 2, 2, P)
        wT = at(X0 + 3328, SEQ)
        rt = at(X0 + 3584, 16, 64)
        ysb = at(6400, 2, 512)
        gfin = at(7424, D)
        gwt = at(10496, 2, P)
        gsel = at(10752, 2, CAP, dt=BF16)
        bsel = at(10816, CAP, dt=BF16)
        pos = at(10880, 2, 40)
        wtok = at(10960, 2, 40)
        ident3 = at(11040, 40)
        ofl = at(11080, 8)
        maskb = at(11088, 2, E, dt=BF16)
        tri_lt_b, ones_b = at(11120, P, dt=BF16), at(11184, P, dt=BF16)
        topv, negm, wsum = at(11248, 2, 8), at(11264, 2, 1), at(11268, 2, 1)
        topi = at(11272, 2, 8).bitcast(U32)
        topf, tope = at(11288, 2, 8), at(11304, 2, 8)

        bank = [ctx.enter_context(nc.psum_tensor(f"bank{i}", [P, 512], F32)) for i in range(8)]
        toep_rows = nc.dram_tensor("toep_rows", (P, HEADS, 2, VL), F32, kind="Internal").ap()

        slot_loaded = [sem(f"slot_loaded{i}") for i in range(SLOTS)]
        slot_used = sem("slot_used")
        x_in, const_in, vec_in, row_in, rel_in = (sem(n) for n in ("x_in", "const_in", "vec_in", "row_in", "rel_in"))
        toep_out, toep_in, xres_in, b1_in, b1_spread, b2_in, gfin_in, out_done = (sem(n) for n in (
            "toep_out", "toep_in", "xres_in", "b1_in", "b1_spread", "b2_in", "gfin_in", "out_done"))
        dve_chain, act_chain = sem("dve_chain"), sem("act_chain")
        zeros_set, sq_done, ssq_ready, rstd_ready, un_ready, acc_final, tail_chain = (sem(n) for n in (
            "zeros_set", "sq_done", "ssq_ready", "rstd_ready", "un_ready", "acc_final", "tail_chain"))
        tile_ready, tile_saved = sem("tile_ready"), sem("tile_saved")
        rows_T, cols_saved, tab_ready, avec_ready, avec_saved = (sem(n) for n in (
            "rows_T", "cols_saved", "tab_ready", "avec_ready", "avec_saved"))
        a_ready, cum_ready, decay_ready, alog_exp, nabs_ready, dt_exp = (sem(n) for n in (
            "a_ready", "cum_ready", "decay_ready", "alog_exp", "nabs_ready", "dt_exp"))
        qk_ready, logit_done, max_ready, exp_ready, p_ready, pt_ready, ptm_saved, ptb_saved, pv_ready, ya_saved = (
            sem(n) for n in ("qk_ready", "logit_done", "max_ready", "exp_ready", "p_ready", "pt_ready",
                             "ptm_saved", "ptb_saved", "pv_ready", "ya_saved"))
        conv_ready, csig_ready, xs_ready, tr_ready, tr_saved, xdec0_ready, st0_ready, st0_saved, z_done = (
            sem(n) for n in ("conv_ready", "csig_ready", "xs_ready", "tr_ready", "tr_saved", "xdec0_ready",
                             "st0_ready", "st0_saved", "z_done"))
        au_ready, seg_ready, e_ready, m_ready, y_ready, y_done, yn_ready = (sem(n) for n in (
            "au_ready", "seg_ready", "e_ready", "m_ready", "y_ready", "y_done", "yn_ready"))
        gate_ready, branch_ready, gsig_ready, m_done, h_ready, h_done = (sem(n) for n in (
            "gate_ready", "branch_ready", "gsig_ready", "m_done", "h_ready", "h_done"))
        lg_ready, topexp_in, topexp_ready, mask_ready, rank_ready, wT_ready, wT_saved, b2_ready, route_done = (
            sem(n) for n in ("lg_ready", "topexp_in", "topexp_ready", "mask_ready", "rank_ready", "wT_ready",
                             "wT_saved", "b2_ready", "route_done"))
        b1_ready, flag_ready = sem("b1_ready"), sem("flag_ready")
        g_ready, gat_ready, s2_ready, s2_saved, usel_ready, glu_ready, esig_ready, hs_ready, hT_ready, hT_saved = (
            sem(n) for n in ("g_ready", "gat_ready", "s2_ready", "s2_saved", "usel_ready", "glu_ready",
                             "esig_ready", "hs_ready", "hT_ready", "hT_saved"))
        ye_saved, sc_ready, sc_added, fin_ready = (sem(n) for n in ("ye_saved", "sc_ready", "sc_added", "fin_ready"))

        def cols_of(w, c0, kt=KT, k0=0, n=256):
            return w[k0 * P:(k0 + kt) * P, c0:c0 + n].rearrange("(k p) c -> p k c", p=P)

        def slot_view(s, *shape):
            names = "abc"[:len(shape)]
            return ring[:, s, 0:int(np.prod(shape))].rearrange(
                f"p ({' '.join(names)}) -> p {' '.join(names)}", **{names[i]: shape[i] for i in range(len(shape))})

        chunks = []

        def add(*parts):
            chunks.append(parts)
            return len(chunks) - 1

        K8 = (lambda s: slot_view(s, KT, 256))
        ck = add((K8, cols_of(w_in, COL_K)))
        cvv = add((K8, cols_of(w_in, COL_V)))
        cq = []
        for j in range(2):
            for r in range(0, 4, 2):
                parts = []
                for half in range(2):
                    c0 = COL_Q + (8 * j + 4 * half + r) * HD
                    for i in range(2):
                        parts.append((lambda s, half=half, i=i: slot_view(s, KT, 2, 128)[:, :, i, HD * half:HD * half + HD],
                                      cols_of(w_in, c0 + HD * i, n=HD)))
                cq.append(add(*parts))
        conv_tiles = [16 + i for i in range(8)] + list(range(16))
        cx = [add((K8, cols_of(w_in, COL_X + conv_tiles[2 * i] * P))) for i in range(12)]
        cz = [[add((lambda s: slot_view(s, 4, 512), cols_of(w_in, COL_Z + 512 * n, kt=4, k0=4 * h, n=512)))
               for h in range(2)] for n in range(4)]
        cbr = []
        w_att_v = w_att.rearrange("(j h r d) c -> h j d r c", j=2, h=2, r=4)
        for dp in range(4):
            c0 = dp * 256
            g0 = add((K8, cols_of(w_in, COL_G + c0)))
            g1 = add((K8, cols_of(w_in, COL_G + D + c0)))
            parts = []
            for half in range(2):
                for j in range(2):
                    parts.append((lambda s, half=half, j=j: slot_view(s, KT, 256)[64 * half:64 * half + 64, 4 * j:4 * j + 4, :],
                                  w_att_v[half, j, :, :, c0:c0 + 256]))
            at_ = add(*parts)
            s0 = add((K8, cols_of(w_ssm, c0)))
            s1 = add((K8, cols_of(w_ssm, c0, k0=8)))
            cbr.append((g0, g1, at_, s0, s1))
        co = [add((lambda s: slot_view(s, 2, 1024), cols_of(w_out, 0, kt=2, k0=2 * i, n=1024))) for i in range(4)]
        FRONT = len(chunks)
        loaded_at, seen = [], [0] * SLOTS
        for n, parts in enumerate(chunks):
            seen[n % SLOTS] += 16 * len(parts)
            loaded_at.append(seen[n % SLOTS])

        def arrived(eng, n):
            eng.wait_ge(slot_loaded[n % SLOTS], loaded_at[n])

        T_U, T_K, T_V, T_Q, T_DT = 0, 8, 10, 13, 21
        T_X = 24
        T_Z = T_X + 24
        T_Y = T_Z + 8
        T_END = T_Y + 16

        released = [None] * FRONT
        released[ck], released[cvv] = (tile_ready, T_K + 2), (tile_ready, T_V + 3)
        for i, n in enumerate(cq):
            released[n] = (tile_ready, T_Q + 2 * i + 2)
        for i, n in enumerate(cx):
            released[n] = (tile_ready, T_X + 2 * i + 2)
        for i, pair in enumerate(cz):
            for n in pair:
                released[n] = (tile_ready, T_Z + 2 * i + 2)
        for dp, five in enumerate(cbr):
            for i, n in enumerate(five):
                released[n] = (gate_ready if i < 2 else branch_ready, 2 * dp + 2)
        for n in co:
            released[n] = (h_ready, 1)

        def slot_of(i):
            return (FRONT + i) % SLOTS

        def expert_arrived(eng, i, t):
            eng.wait_ge(slot_loaded[slot_of(i)], t * 16 + (seen[slot_of(i)] + 16))

        w1_v = w1.rearrange("e (s k p) (h c) -> e h s p k c", p=P, k=2, h=2)
        w2_v = w2.rearrange("e (h c b p) n -> e h b p c n", p=P, h=2, c=2)

        def expert_sources(e):
            one = bass.ds(e, 1)
            src = [w1_v[one, h, s].rearrange("e p k c -> p (e k) c") for h in range(2) for s in range(4)]
            src += [w2_v[one, h, b].rearrange("e p c n -> p (e c) n") for h in range(2) for b in range(2)]
            return src

        block = ctx.enter_context(nc.Block())

        @block.sync
        def _(sp):
            sp.dma_start(xin[:, 1:3, :], x.rearrange("(c p) d -> p c d", p=P)).then_inc(x_in, 16)
            sp.dma_start(xin[0:META, 0, :], meta).then_inc(x_in, 16)
            for n, parts in enumerate(chunks):
                if n >= SLOTS:
                    sp.wait_ge(*released[n - SLOTS])
                for dst, src in parts:
                    sp.dma_start(dst(n % SLOTS), src).then_inc(slot_loaded[n % SLOTS], 16)

            def expert(t, e):
                for i, src in enumerate(expert_sources(e)):
                    if isinstance(t, int):
                        sp.wait_ge(*released[FRONT + i - SLOTS])
                    else:
                        sp.wait_ge(slot_used, t * 12 + (i + 1 - SLOTS))
                    sp.dma_start(slot_view(slot_of(i), 2, 1024), src).then_inc(slot_loaded[slot_of(i)], 16)

            expert(0, 0)
            with sp.Fori(1, E) as e:
                expert(e, e)
            sp.wait_ge(flag_ready, 1)
            more = sp.value_load(ofl[0:1, 0:1].bitcast(I32), min_val=0, max_val=1)
            with sp.If(more):
                with sp.Fori(1, PASSES) as b:
                    with sp.Fori(0, E) as e:
                        expert(b * E + e, e)
            for c in range(2):
                sp.wait_ge(fin_ready, c + 1)
                sp.dma_start(out[c * P:(c + 1) * P, :], un[:, c, :]).then_inc(out_done, 16)
            sp.wait_ge(out_done, 32)

        @block.gpsimd
        def _(pool):
            pool.dma_start(ohs[0:NB + 1, :, :], c_oh).then_inc(rel_in, 16)
            pool.dma_start(tab[0:NB, 0, :], rel).then_inc(rel_in, 16)
            widths = (3, 8, 2, 2)

            def rsqrt(n):
                pool.wait_ge(ssq_ready, n + 1)
                pool.tensor_tensor(rstd[:, 0:widths[n]], ssq[:, 0:widths[n]], half_neg[:, 0:widths[n]],
                                   ALU.pow).then_inc(rstd_ready, 1)

            rsqrt(0)
            pool.wait_ge(avec_saved, 1)
            pool.dma_start(toep_rows.rearrange("q h a v -> h q (a v)"),
                           avec[0:HEADS, :, :].rearrange("p a v -> p (a v)").unsqueeze(1).to_broadcast([HEADS, P, 2 * VL])
                           ).then_inc(toep_out, 16)
            pool.wait_ge(toep_out, 16)
            pool.wait_ge(tile_ready, T_U + 8)
            RP = HEADS * 2 * VL

            def toeplitz(x0, half, n):
                return bass.AP(toep_rows.tensor, half * VL + x0, [[RP - 1, P], [2 * VL, HEADS], [1, n]])

            with nc.allow_non_contiguous_dma(reason="short runs of the bias"):
                pool.dma_start(toep[:, :, 0:META], toeplitz(127, 0, META)).then_inc(toep_in, 16)
                pool.dma_start(toep[:, :, META:NT], toeplitz(127 + META, 1, SEQ)).then_inc(toep_in, 16)
                pool.dma_start(toep[:, :, NT:NT + META], toeplitz(255, 0, META)).then_inc(toep_in, 16)
                pool.dma_start(toep[:, :, NT + META:LK], toeplitz(255 + META, 1, BLK)).then_inc(toep_in, 16)
            for n in range(1, 4):
                rsqrt(n)
                if n == 1:
                    pool.wait_ge(y_done, 8)
                    pool.dma_start(xres, x.rearrange("(c p) d -> p c d", p=P)).then_inc(xres_in, 16)
                    pool.wait_ge(tile_ready, T_END)
                    pool.dma_start(b1raw[0:E, :], b1).then_inc(b1_in, 16)
                    pool.wait_ge(b1_ready, 1)
                    pool.dma_start(b1all[E:2 * E, :], b1mid[0:E, :]).then_inc(b1_spread, 16)
                    pool.dma_start(b1all[2 * E:3 * E, :], b1lo[0:E, :]).then_inc(b1_spread, 16)
                if n == 2:
                    pool.wait_ge(h_done, 4)
                    pool.dma_start(b2sb[0:E, :], b2).then_inc(b2_in, 16)
                    pool.wait_ge(route_done, 1)
                    pool.dma_start(gfin, bass.AP(g_fin.tensor, 0, [[0, P], [1, D]])).then_inc(gfin_in, 16)

        @block.scalar
        def _(act):
            sc = nc.scalar
            ch = Chain(act, act_chain)
            act.dma_start(squares[:, :, :], c_sq).then_inc(const_in, 16)
            act.dma_start(rows[0:96, 0, :], conv_w.rearrange("w (i c) -> (w i) c", c=P)).then_inc(row_in, 16)
            act.dma_start(rows[96:120, 0, :], conv_b.rearrange("(i c) -> i c", c=P)).then_inc(row_in, 16)
            act.dma_start(rows[0:8, 1, :], g_mix.rearrange("(i c) -> i c", c=P)).then_inc(row_in, 16)
            act.dma_start(rows[8:16, 1, :], g_ffn.rearrange("(i c) -> i c", c=P)).then_inc(row_in, 16)
            act.dma_start(rows[16:32, 1, :], g_ssm.rearrange("(i c) -> i c", c=P)).then_inc(row_in, 16)
            for dst, src, n in ((dtb, dt_bias, SH), (alog, a_log, SH), (dskip, d_skip, SH), (brt, b_rt, E),
                                (sink_nat, sinks, HEADS)):
                act.dma_start(dst[:, :], bass.AP(src.tensor, 0, [[0, P], [1, n]])).then_inc(vec_in, 16)
            act.dma_start(wdt[:, :, :], cols_of(w_in, COL_DT, n=SH)).then_inc(vec_in, 16)
            act.dma_start(wrt[:, :, :], w_rt.rearrange("(k p) e -> p k e", p=P)).then_inc(vec_in, 16)

            def squared(ins, val):
                ins.then_inc(sq_done, 1)
                act.wait_ge(sq_done, val)

            act.wait_ge(x_in, 32)
            act.wait_ge(zeros_set, 1)
            for c, r in ((0, META), (1, P), (2, P)):
                squared(sc.activation(uT.rearrange("p k n -> p (k n)")[0:r, 0:D], xin[0:r, c, :], ACT.Square,
                                      accum_out=ssq[0:r, c:c + 1]), c + 1)
            act.wait_ge(rows_T, 1)
            ch.link(sc.activation(cols[:, 0:120], bank[4][:, 0:120], ACT.Copy))
            sc.activation(cols[:, 120:152], bank[4][:, 128:160], ACT.Copy).then_inc(cols_saved, 1)
            act.wait_ge(cols_saved, 1)
            act.wait_ge(avec_ready, 1)
            ch.link(sc.activation(avec[0:HEADS, 0, :], bank[5][0:HEADS, 0:VL], ACT.Copy))
            sc.activation(avec[0:HEADS, 1, :], bank[6][0:HEADS, 0:VL], ACT.Copy).then_inc(avec_saved, 1)
            act.wait_ge(vec_in, 7 * 16)
            sc.activation(dts[:, 6, 0:SH], alog[:, :], ACT.Exp).then_inc(alog_exp, 1)

            def tile(p):
                act.wait_ge(tile_ready, p + 1)
                return bank[p % 4]

            def saved(ins):
                ins.then_inc(tile_saved, 1)

            for k in range(KT):
                saved(sc.activation(uT[:, k, :], tile(T_U + k)[:, 0:NT], ACT.Copy, scale=col_gmix[:, k:k + 1]))
            for j in range(2):
                b = tile(T_K + j)
                ch.link(sc.activation(kz[0:64, 2 * j, :], b[0:64, 0:NT], ACT.Copy))
                saved(sc.activation(kz[64:128, 2 * j + 1, :], b[64:128, 0:NT], ACT.Copy))
            for c, r in ((0, META), (1, P), (2, P)):
                saved(sc.activation(vTC[0:r, c, :], tile(T_V + c)[0:r, 0:256], ACT.Copy))
            for i in range(8):
                saved(sc.activation(qT[:, i, :], tile(T_Q + i)[:, 0:SEQ], ACT.Copy))
            for c, r in ((0, META), (1, P), (2, P)):
                saved(sc.activation(dts[0:r, 2, 32 * c:32 * c + 32], tile(T_DT + c)[0:r, 0:SH], ACT.Copy))
            act.wait_ge(nabs_ready, 1)
            sc.activation(dts[:, 4, :], dts[:, 3, :], ACT.Exp).then_inc(dt_exp, 1)
            act.wait_ge(cum_ready, 1)
            sc.activation(decays[:, :, :, :], bank[7][:, 0:288].rearrange("p (a c h) -> p a c h", a=3, c=3),
                          ACT.Exp).then_inc(decay_ready, 1)

            def att_exp(t):
                act.wait_ge(max_ready, t + 1)
                for half in range(2):
                    for n, (a, b) in enumerate(((0, NT), (NT, LK))):
                        ch.link(sc.activation(logit[:, t % 2, half, a:b], logit[:, t % 2, half, a:b], ACT.Exp,
                                              bias=stats[:, 1, 2 * half + n:2 * half + n + 1],
                                              accum_out=stats[:, 3, 2 * half + n:2 * half + n + 1]))
                sc.activation(stats[:, 4, :], stats[:, 2, :], ACT.Exp).then_inc(exp_ready, 1)

            def att_save(t):
                act.wait_ge(pt_ready, t + 1)
                if t >= 1:
                    act.wait_ge(pv_ready, t)
                for half in range(2):
                    ins = sc.activation(pT[:, half, 0:384], bank[4 + half][:, 0:384], ACT.Copy)
                    if half:
                        ins.then_inc(ptb_saved, 1)
                act.wait_ge(pv_ready, t + 1)
                sc.activation(yaT[:, t, :], bank[7][:, 0:SEQ], ACT.Copy).then_inc(ya_saved, 1)

            att_exp(0)
            for t in range(8):
                if t + 1 < 8:
                    att_exp(t + 1)
                att_save(t)

            def conv_evict(i):
                b = tile(T_X + i)
                if i >= 2:
                    act.wait_ge(conv_ready, i - 1)
                saved(sc.activation(xpre[:, i % 2, 3:3 + NT], b[:, 0:NT], ACT.Copy))

            def conv_sig(i):
                act.wait_ge(conv_ready, i + 1)
                if i >= 2:
                    act.wait_ge(xs_ready, i - 1)
                sc.activation(sg[:, i % 2, :], cv[:, i % 2, :], ACT.Sigmoid).then_inc(csig_ready, 1)

            def conv_tr(i):
                if 4 <= i < 8:
                    return
                n = i if i < 4 else i - 4
                act.wait_ge(tr_ready, n + 1)
                b = bank[4 + n % 2]
                if i < 4:
                    ch.link(sc.activation(bTC[0:META, 0, i * P:(i + 1) * P], b[0:META, 0:P], ACT.Copy))
                    sc.activation(bTC[:, 1, i * P:(i + 1) * P], b[:, P:2 * P], ACT.Copy).then_inc(tr_saved, 1)
                else:
                    j = i - 8
                    if j % 4 == 0 and j:
                        act.wait_ge(xdec0_ready, j // 4)
                    ch.link(sc.activation(xm[0:META, (j % 4) * P:(j % 4 + 1) * P], b[0:META, 0:P], ACT.Copy))
                    sc.activation(xTC[:, :, j * P:(j + 1) * P],
                                  b[:, P:3 * P].rearrange("p (c n) -> p c n", c=2), ACT.Copy).then_inc(tr_saved, 1)

            def st0_save(g):
                act.wait_ge(st0_ready, g + 1)
                sc.activation(hst[:, g, :], bank[6][:, :], ACT.Copy).then_inc(st0_saved, 1)

            for i in range(24 + 5):
                if i < 24:
                    conv_evict(i)
                if 0 <= i - 1 < 24:
                    conv_sig(i - 1)
                if 0 <= i - 3 < 24:
                    conv_tr(i - 3)
                if i - 5 >= 11 and (i - 5 - 8) % 4 == 3:
                    st0_save((i - 5 - 8) // 4)

            for n in range(4):
                for c in range(2):
                    q = 2 * n + c
                    b = tile(T_Z + q)
                    if q >= 2:
                        act.wait_ge(z_done, q - 1)
                    ch.link(sc.activation(zy[:, c, 512 * n:512 * n + 512], b[:, :], ACT.Sigmoid))
                    saved(sc.activation(ztmp[:, q % 2, :], b[:, :], ACT.Copy))

            def ssd_exp(it):
                act.wait_ge(seg_ready, it + 1)
                if it >= 2:
                    act.wait_ge(y_ready, it - 1)
                for j in range(2):
                    ins = sc.activation(em[:, it % 2, 4 * j:4 * j + 4, :],
                                        bank[j][:, :].rearrange("p (h l) -> p h l", h=4), ACT.Exp)
                    if j:
                        ins.then_inc(e_ready, 1)

            ssd_exp(0)
            for it in range(8):
                if it + 1 < 8:
                    ssd_exp(it + 1)
                act.wait_ge(y_done, it + 1)
                c, g = divmod(it, 4)
                squared(sc.activation(sq_scratch, zy[:, c, 512 * g:512 * g + 512], ACT.Square,
                                      accum_out=ssq[:, it:it + 1]), 3 + it + 1)

            for i in range(16):
                saved(sc.activation(yT[:, i, :], tile(T_Y + i)[:, 0:SEQ], ACT.Copy, scale=col_gssm[:, i:i + 1]))

            for d in range(8):
                act.wait_ge(gate_ready, d + 1)
                if d >= 2:
                    act.wait_ge(m_done, d - 1)
                sc.activation(gsig[:, d % 2, :], bank[2 * (d % 4)][:, :], ACT.Sigmoid).then_inc(gsig_ready, 1)

            for c in range(2):
                act.wait_ge(h_done, 2 * c + 2)
                squared(sc.activation(ures[:, c, :], acc[:, c, :], ACT.Square, accum_out=ssq[:, c:c + 1]), 11 + c + 1)
            for k in range(KT):
                act.wait_ge(tile_ready, T_END + k + 1)
                sc.activation(u2T[:, k, :], bank[k % 4][:, 0:SEQ], ACT.Copy,
                              scale=col_gffn[:, k:k + 1]).then_inc(tile_saved, 1)
            act.wait_ge(topexp_in, 1)
            for c in range(2):
                ins = sc.activation(tope[:, c, 0:4], topv[:, c, 0:4], ACT.Exp, bias=negm[:, c, :],
                                    accum_out=wsum[:, c, :])
                if c:
                    ins.then_inc(topexp_ready, 1)
                else:
                    ch.link(ins)
            act.wait_ge(wT_ready, 1)
            sc.activation(wT[0:E, :], bank[5][0:E, 0:SEQ], ACT.Copy).then_inc(wT_saved, 1)

            def expert(t):
                act.wait_ge(s2_ready, t + 1)
                sc.activation(s2, bank[5][:, 0:SEQ], ACT.Copy).then_inc(s2_saved, 1)
                for half in range(2):
                    act.wait_ge(glu_ready, t * 2 + half + 1)
                    sc.activation(sig[:, half, :], glu[:, half, :], ACT.Sigmoid, scale=ALPHA).then_inc(esig_ready, 1)
                for half in range(2):
                    act.wait_ge(hT_ready, t * 2 + half + 1)
                    sc.activation(hT[:, half, :, :], bank[5][:, 0:256].rearrange("p (b n) -> p b n", b=2),
                                  ACT.Copy).then_inc(hT_saved, 1)
                act.wait_ge(slot_used, t * 12 + 12)
                for n in range(2):
                    sc.activation(ysb[:, n, :], bank[2 + n][:, :], ACT.Copy).then_inc(ye_saved, 1)

            with act.Fori(0, E) as t:
                expert(t)
            act.wait_ge(flag_ready, 1)
            more = act.value_load(ofl[0:1, 0:1].bitcast(I32), min_val=0, max_val=1)
            with act.If(more):
                with act.Fori(E, PASSES * E) as t:
                    expert(t)
            act.wait_ge(acc_final, 1)
            for c in range(2):
                squared(sc.activation(ysb.rearrange("p a b -> p (a b)"), acc[:, c, :], ACT.Square,
                                      accum_out=ssq[:, c:c + 1]), 13 + c + 1)

        @block.vector
        def _(dve):
            v = nc.vector
            ch = Chain(dve, dve_chain)

            def done(ins, s, val):
                ins.then_inc(s, 1)
                dve.wait_ge(s, val)

            ch.link(v.memset(half_neg[:, :], -0.5))
            ch.link(v.memset(ssq[:, :], 1.0))
            ch.link(v.memset(dts[:, :, :], 0.0))
            ch.link(v.memset(tab[NB:NB + 1, :, :], 1.0))
            ch.link(v.memset(kz[:, :, :], 0.0))
            ch.link(v.memset(vTC[:, :, :], 0.0))
            done(v.memset(pT[:, :, :], 0.0), zeros_set, 1)
            dve.wait_ge(rel_in, 32)
            done(v.tensor_copy(tab[0:NB + 1, 1, :].rearrange("p (j r h) -> p j r h", j=2, r=4),
                               tab[0:NB + 1, 0, :].rearrange("p (j h r) -> p j r h", j=2, h=2)), tab_ready, 1)

            dve.wait_ge(sq_done, 3)
            done(v.tensor_scalar(ssq[:, 0:3], ssq[:, 0:3], 1.0 / D, EPS, ALU.mult, ALU.add), ssq_ready, 1)
            dve.wait_ge(rstd_ready, 1)
            for c, r in ((0, META), (1, P), (2, P)):
                done(v.tensor_scalar(xin[0:r, c, :], xin[0:r, c, :], rstd[0:r, c:c + 1], None, ALU.mult), un_ready, c + 1)
            dve.wait_ge(vec_in, 7 * 16)
            ch.link(v.tensor_copy(sink_p[:, :].rearrange("p (j r h) -> p j r h", j=2, r=4),
                                  sink_nat[:, :].rearrange("p (j h r) -> p j r h", j=2, h=2)))

            raw, nabs, ex, tt, acc1 = (dts[:, i, :] for i in (2, 3, 4, 5, 1))
            c3 = (lambda v_: v_.rearrange("p (c h) -> p c h", c=3))
            bc = (lambda v_: v_.unsqueeze(1).to_broadcast([P, 3, SH]))
            dve.wait_ge(tile_saved, T_X)
            ch.link(v.tensor_tensor(c3(raw), c3(raw), bc(dtb[:, :]), ALU.add))
            ch.link(v.tensor_scalar(tt, raw, -1.0, None, ALU.mult))
            done(v.tensor_tensor(nabs, raw, tt, ALU.min), nabs_ready, 1)
            ch.link(v.tensor_scalar(raw, raw, 0.0, None, ALU.max))
            dve.wait_ge(dt_exp, 1)
            ch.link(v.tensor_scalar(tt, ex, 2.0, None, ALU.add))
            ch.link(v.reciprocal(tt, tt))
            ch.link(v.tensor_tensor(ex, ex, tt, ALU.mult))
            ch.link(v.tensor_tensor(tt, ex, ex, ALU.mult))
            ch.link(v.memset(nabs, 1.0 / 17))
            for k in (15, 13, 11, 9, 7, 5, 3, 1):
                ch.link(v.tensor_tensor(nabs, nabs, tt, ALU.mult))
                ch.link(v.tensor_scalar(nabs, nabs, 1.0 / k, None, ALU.add))
            ch.link(v.tensor_tensor(nabs, nabs, ex, ALU.mult))
            ch.link(v.memset(dt, 0.0))
            for c, r in ((0, META), (1, P), (2, P)):
                s = slice(32 * c, 32 * c + 32)
                ch.link(v.scalar_tensor_tensor(dt[0:r, s], nabs[0:r, s], 2.0, raw[0:r, s], ALU.mult, ALU.add))
            dve.wait_ge(alog_exp, 1)
            done(v.scalar_tensor_tensor(c3(aa), c3(dt), -1.0, bc(dts[:, 6, 0:SH]), ALU.mult, ALU.mult), a_ready, 1)

            dve.wait_ge(toep_in, 64)

            def att_max(t):
                dve.wait_ge(qk_ready, t + 1)
                if t >= 2:
                    dve.wait_ge(pt_ready, t - 1)
                for half in range(2):
                    ins = v.scalar_tensor_tensor(logit[:, t % 2, half, :], bank[2 * (t % 2) + half][:, 0:LK],
                                                 HD ** -0.5, toep[:, 2 * t + half, :], ALU.mult, ALU.add)
                    done(ins, logit_done, 2 * t + half + 1)
                if t >= 1:
                    dve.wait_ge(exp_ready, t)
                mx = stats[:, 0, :].rearrange("p (h n) -> p h n", n=2)
                ch.link(v.tensor_reduce(mx[:, :, 0], logit[:, t % 2, :, 0:NT], AX, ALU.max))
                ch.link(v.tensor_reduce(mx[:, :, 1], logit[:, t % 2, :, NT:LK], AX, ALU.max))
                sk = sink_p[:, 2 * t:2 * t + 2].unsqueeze(2).to_broadcast([P, 2, 2])
                ch.link(v.tensor_tensor(mx, mx, sk, ALU.max))
                ch.link(v.tensor_tensor(stats[:, 2, :].rearrange("p (h n) -> p h n", n=2), sk, mx, ALU.subtract))
                done(v.tensor_scalar(stats[:, 1, :], stats[:, 0, :], -1.0, None, ALU.mult), max_ready, t + 1)

            def att_norm(t):
                dve.wait_ge(exp_ready, t + 1)
                ch.link(v.tensor_tensor(stats[:, 5, :], stats[:, 3, :], stats[:, 4, :], ALU.add))
                ch.link(v.reciprocal(stats[:, 5, :], stats[:, 5, :]))
                for half in range(2):
                    for n, (a, b) in enumerate(((0, NT), (NT, LK))):
                        ins = v.tensor_scalar(logit[:, t % 2, half, a:b], logit[:, t % 2, half, a:b],
                                              stats[:, 5, 2 * half + n:2 * half + n + 1], None, ALU.mult)
                        if half and n:
                            done(ins, p_ready, t + 1)
                        else:
                            ch.link(ins)

            def att_meta(t):
                dve.wait_ge(pt_ready, t + 1)
                if t >= 1:
                    dve.wait_ge(pv_ready, t)
                done(v.tensor_copy(pT[0:META, :, 384:640], bank[6][0:META, :].rearrange("p (h n) -> p h n", h=2)),
                     ptm_saved, t + 1)

            for t in range(8):
                att_max(t)
                att_norm(t)
                if t >= 1:
                    att_meta(t - 1)
            att_meta(7)

            dve.wait_ge(ya_saved, 8)
            ch.link(v.memset(xpre[:, :, 0:3], 0.0))
            ch.link(v.memset(xdec0, 0.0))
            done(v.memset(bTC[:, 0, :], 0.0), zeros_set, 2)

            def conv(i):
                ct = conv_tiles[i]
                w = (lambda k: col_cw[:, k * 24 + ct:k * 24 + ct + 1])
                dve.wait_ge(tile_saved, T_X + i + 1)
                if i >= 2:
                    dve.wait_ge(csig_ready, i - 1)
                xp, o = xpre[:, i % 2, :], cv[:, i % 2, :]
                ch.link(v.tensor_scalar(o, xp[:, 0:NT], w(0), col_cb[:, ct:ct + 1], ALU.mult, ALU.add))
                for k in (1, 2):
                    ch.link(v.scalar_tensor_tensor(o, xp[:, k:k + NT], w(k), o, ALU.mult, ALU.add))
                done(v.scalar_tensor_tensor(o, xp[:, 3:3 + NT], w(3), o, ALU.mult, ALU.add), conv_ready, i + 1)

            def silu(i):
                dve.wait_ge(csig_ready, i + 1)
                if i < 4:
                    o = bT[:, i, :]
                elif i < 8:
                    o = cT[:, i - 4, :]
                else:
                    o = xs[:, i % 3, :]
                    if i >= 11:
                        dve.wait_ge(tr_ready, i - 3 - 4 + 1)
                done(v.tensor_tensor(o, cv[:, i % 2, :], sg[:, i % 2, :], ALU.mult), xs_ready, i + 1)

            def xdecay0(g):
                dve.wait_ge(tr_saved, 4 + 4 * g + 4)
                if g:
                    dve.wait_ge(st0_ready, g)
                m = (lambda v_: v_.rearrange("p (h d) -> p h d", h=HPG))
                sc_ = (lambda v_: v_.unsqueeze(2).to_broadcast([META, HPG, HD]))
                ch.link(v.tensor_tensor(m(xdec0[0:META]), m(xm[0:META]), sc_(dt[0:META, 8 * g:8 * g + 8]), ALU.mult))
                done(v.tensor_tensor(m(xdec0[0:META]), m(xdec0[0:META]),
                                     sc_(decays[0:META, 1, 0, 8 * g:8 * g + 8]), ALU.mult), xdec0_ready, g + 1)

            dve.wait_ge(decay_ready, 1)
            for i in range(24 + 5):
                if i < 24:
                    conv(i)
                if 0 <= i - 1 < 24:
                    silu(i - 1)
                if i - 4 >= 11 and (i - 4 - 8) % 4 == 3:
                    xdecay0((i - 4 - 8) // 4)

            for q in range(8):
                n, c = divmod(q, 2)
                dve.wait_ge(tile_saved, T_Z + q + 1)
                zz = zy[:, c, 512 * n:512 * n + 512]
                done(v.tensor_tensor(zz, zz, ztmp[:, q % 2, :], ALU.mult), z_done, q + 1)

            def ssd_au(it):
                c, g = divmod(it, 4)
                if it >= 2:
                    dve.wait_ge(seg_ready, it - 1)
                done(v.tensor_tensor(au[:, it % 2, :, :],
                                     aa[:, 32 * (c + 1) + 8 * g:32 * (c + 1) + 8 * g + 8].unsqueeze(2).to_broadcast([P, HPG, BLK]),
                                     tri_le.unsqueeze(1).to_broadcast([P, HPG, BLK]), ALU.mult), au_ready, it + 1)

            def heads(v_, h0=0):
                return v_.unsqueeze(2).to_broadcast([P, HPG, HD])

            def ssd_pre(it):
                c, g = divmod(it, 4)
                dve.wait_ge(e_ready, it + 1)
                if it >= 2:
                    dve.wait_ge(y_ready, it - 1)
                ch.link(v.tensor_tensor(cbm[:, it % 2, :], bank[4 + it % 2][:, 0:BLK], tri_le, ALU.mult))
                ch.link(v.tensor_tensor(em[:, it % 2, :, :], em[:, it % 2, :, :],
                                        cbm[:, it % 2, :].unsqueeze(1).to_broadcast([P, HPG, BLK]), ALU.mult))
                xg = xTC[:, c, 512 * g:512 * g + 512].rearrange("p (h d) -> p h d", h=HPG)
                s = slice(32 * (c + 1) + 8 * g, 32 * (c + 1) + 8 * g + 8)
                ins = v.tensor_tensor(xdt[:, it % 2, :, :], xg, heads(dt[:, s]), ALU.mult)
                if c == 0:
                    ch.link(ins)
                    if it >= 1:
                        dve.wait_ge(y_ready, it)
                    ins = v.tensor_tensor(xdec, xdt[:, it % 2, :, :], heads(decays[:, 1, 1, 8 * g:8 * g + 8]), ALU.mult)
                done(ins, m_ready, it + 1)

            def ssd_post(it):
                c, g = divmod(it, 4)
                dve.wait_ge(y_ready, it + 1)
                ys = ysum
                ch.link(v.tensor_tensor(ys, bank[6][:, :].rearrange("p (h d) -> p h d", h=HPG),
                                        heads(decays[:, 0, c + 1, 8 * g:8 * g + 8]), ALU.mult))
                yv = ys.rearrange("p (q i) d -> p q i d", i=2)
                for i in range(2):
                    for j in range(2):
                        src = bank[2 + j][:, :].rearrange("p (q i o d) -> p q i o d", q=2, i=2, o=2)[:, :, i, i, :]
                        ch.link(v.tensor_tensor(yv[:, 2 * j:2 * j + 2, i, :], yv[:, 2 * j:2 * j + 2, i, :], src, ALU.add))
                xg = xTC[:, c, 512 * g:512 * g + 512].rearrange("p (h d) -> p h d", h=HPG)
                ch.link(v.tensor_tensor(xg, xg, heads(dskip[:, 8 * g:8 * g + 8]), ALU.mult))
                ch.link(v.tensor_tensor(ys, ys, xg, ALU.add))
                zz = zy[:, c, 512 * g:512 * g + 512].rearrange("p (h d) -> p h d", h=HPG)
                if c == 0:
                    hg = hst[:, g, :].rearrange("p (h d) -> p h d", h=HPG)
                    ch.link(v.tensor_tensor(hg, hg, heads(decays[:, 2, 1, 8 * g:8 * g + 8]), ALU.mult))
                    ch.link(v.tensor_tensor(hg, hg, bank[7][:, :].rearrange("p (h d) -> p h d", h=HPG), ALU.add))
                done(v.tensor_tensor(zz, zz, ys, ALU.mult), y_done, it + 1)

            ssd_au(0)
            ssd_au(1)
            ssd_pre(0)
            for it in range(8):
                if it + 2 < 8:
                    ssd_au(it + 2)
                if it + 1 < 8:
                    ssd_pre(it + 1)
                ssd_post(it)
            dve.wait_ge(sq_done, 11)
            done(v.tensor_scalar(ssq[:, :], ssq[:, :], float(G) / DI, EPS, ALU.mult, ALU.add), ssq_ready, 2)
            dve.wait_ge(rstd_ready, 2)
            for it in range(8):
                c, g = divmod(it, 4)
                zz = zy[:, c, 512 * g:512 * g + 512]
                done(v.tensor_scalar(zz, zz, rstd[:, it:it + 1], None, ALU.mult), yn_ready, it + 1)

            for d in range(8):
                dve.wait_ge(gsig_ready, d + 1)
                dve.wait_ge(branch_ready, d + 1)
                ch.link(v.tensor_tensor(gmul[:, d % 2, :], gsig[:, d % 2, :], bank[2 * (d % 4) + 1][:, :], ALU.mult))
                done(v.tensor_tensor(mT[:, d, :], gmul[:, d % 2, 0:256], gmul[:, d % 2, 256:512], ALU.add), m_done, d + 1)
                if d == 1:
                    dve.wait_ge(b1_in, 16)
                    ch.link(v.tensor_copy(b1all[0:E, :], b1raw[0:E, :]))
                    ch.link(v.tensor_tensor(b1raw[0:E, :], b1raw[0:E, :], b1all[0:E, :], ALU.subtract))
                    ch.link(v.tensor_copy(b1mid[0:E, :], b1raw[0:E, :]))
                    ch.link(v.tensor_tensor(b1raw[0:E, :], b1raw[0:E, :], b1mid[0:E, :], ALU.subtract))
                    done(v.tensor_copy(b1lo[0:E, :], b1raw[0:E, :]), b1_ready, 1)

            dve.wait_ge(xres_in, 16)
            dve.wait_ge(h_ready, 1)
            for c in range(2):
                for n in range(2):
                    done(v.tensor_tensor(acc[:, c, 512 * n:512 * n + 512], bank[2 * c + n][:, :],
                                         xres[:, c, 512 * n:512 * n + 512], ALU.add), h_done, 2 * c + n + 1)
            dve.wait_ge(sq_done, 13)
            done(v.tensor_scalar(ssq[:, 0:2], ssq[:, 0:2], 1.0 / D, EPS, ALU.mult, ALU.add), ssq_ready, 3)
            dve.wait_ge(rstd_ready, 3)
            for c in range(2):
                done(v.tensor_scalar(un[:, c, :], acc[:, c, :], rstd[:, c:c + 1], None, ALU.mult), un_ready, 4 + c)
            ch.link(v.tensor_copy(upart[:, 0, :, :], un))
            ch.link(v.tensor_tensor(ures, un, upart[:, 0, :, :], ALU.subtract))
            ch.link(v.tensor_copy(upart[:, 1, :, :], ures))
            ch.link(v.tensor_tensor(ures, ures, upart[:, 1, :, :], ALU.subtract))
            ch.link(v.tensor_copy(upart[:, 2, :, :], ures))

            ch.link(v.tensor_tensor(tri_lt_b, tri_le, ident, ALU.subtract))
            ch.link(v.tensor_copy(ones_b, ones))
            ch.link(v.memset(pos, -1.0))
            ch.link(v.memset(wtok, 0.0))
            ch.link(v.memset(ident3, 0.0))
            for i in range(3):
                ch.link(v.tensor_copy(ident3[E * i:E * i + E, 0:E], ident[E * i:E * i + E, E * i:E * i + E]))
            dve.wait_ge(lg_ready, 1)
            lg, oh = rt[:, 0:2, 0:E], rt[:, 2:4, 0:E]
            ch.link(v.tensor_tensor(lg, bank[4][:, 0:64].rearrange("p (c e) -> p c e", c=2),
                                    brt[:, :].unsqueeze(1).to_broadcast([P, 2, E]), ALU.add))
            for c in range(2):
                ch.link(v.max(topv[:, c, :], lg[:, c, :]))
                ch.link(v.max_index(topi[:, c, :], topv[:, c, :], lg[:, c, :]))
                ch.link(v.tensor_copy(topf[:, c, :], topi[:, c, :]))
            done(v.tensor_scalar(negm, topv[:, :, 0:1], -1.0, None, ALU.mult), topexp_in, 1)
            dve.wait_ge(topexp_ready, 1)
            ch.link(v.reciprocal(wsum, wsum))
            mk = rt[:, 4:6, 0:E]
            ch.link(v.memset(mk, 0.0))
            for c in range(2):
                ch.link(v.tensor_scalar(tope[:, c, 0:4], tope[:, c, 0:4], wsum[:, c, :], None, ALU.mult))
                for k in range(4):
                    ch.link(v.tensor_scalar(oh[:, c, :], iota2[:, 0:E], topf[:, c, k:k + 1], None, ALU.is_equal))
                    ch.link(v.tensor_tensor(mk[:, c, :], mk[:, c, :], oh[:, c, :], ALU.add))
                    ch.link(v.scalar_tensor_tensor(wtok[:, c, 0:E], oh[:, c, :], tope[:, c, k:k + 1], wtok[:, c, 0:E],
                                                   ALU.mult, ALU.add))
            done(v.tensor_copy(maskb, mk), mask_ready, 1)
            dve.wait_ge(rank_ready, 1)
            ps = pos[:, :, 0:E]
            ch.link(v.scalar_tensor_tensor(ps, bank[6][:, 0:64].rearrange("p (c e) -> p c e", c=2), 1.0, mk,
                                           ALU.add, ALU.mult))
            ch.link(v.tensor_scalar(ps, ps, -1.0, None, ALU.add))
            ch.link(v.tensor_reduce(ofl[:, 1:2], bank[6][:, 64:96], AX, ALU.max))
            done(v.tensor_scalar(ofl[:, 0:1].bitcast(I32), ofl[:, 1:2], float(CAP), None, ALU.is_gt), flag_ready, 1)
            dve.wait_ge(b2_ready, 1)
            for c in range(2):
                for n in range(2):
                    ch.link(v.tensor_tensor(acc[:, c, 512 * n:512 * n + 512], acc[:, c, 512 * n:512 * n + 512],
                                            bank[2 * c + n][:, :], ALU.add))
            ch.link(v.memset(s2, 0.0))
            done(v.memset(ysb, 0.0), route_done, 1)

            def routing(col, val):
                for c in range(2):
                    ch.link(v.tensor_scalar(gsel[:, c, :], iota2[:, 0:CAP], pos[:, c, bass.ds(col, 1)], None, ALU.is_equal))
                    ch.link(v.tensor_scalar(gwt[:, c, :], iota2, pos[:, c, bass.ds(col, 1)], wtok[:, c, bass.ds(col, 1)],
                                            ALU.is_equal, ALU.mult))
                done(v.tensor_copy(bsel[0:3 * E, :], ident3[0:3 * E, bass.ds(col, 1)].to_broadcast([3 * E, CAP])),
                     g_ready, val)

            def scatter_add(s):
                for i in range(4):
                    c, n = divmod(i, 2)
                    dve.wait_ge(sc_ready, s * 4 + (i + 1))
                    a = acc[:, c, 512 * n:512 * n + 512]
                    done(v.tensor_tensor(a, a, bank[6 + n][:, :], ALU.add), sc_added, s * 4 + (i + 1))

            def expert(t, e, b, extra):
                dve.wait_ge(gat_ready, t + 1)
                done(v.tensor_tensor(usel, bank[4][:, :].rearrange("p (k s) -> p k s", k=KT),
                                     col_gffn.unsqueeze(2).to_broadcast([P, KT, CAP]), ALU.mult), usel_ready, t + 1)
                scatter_add(t + extra)
                dve.wait_ge(s2_ready, t + 1)
                routing(e + 1, t + b + 2)
                for half in range(2):
                    dve.wait_ge(slot_used, t * 12 + (4 * half + 4))
                    hv = bank[half][:, :].rearrange("p (f two) -> p f two", two=2)
                    done(v.tensor_scalar(glu[:, half, :], hv[:, :, 0], LIMIT, None, ALU.min), glu_ready, t * 2 + half + 1)
                    ch.link(v.tensor_scalar(lin[:, half, :], hv[:, :, 1], -LIMIT, LIMIT, ALU.max, ALU.min))
                    ch.link(v.scalar_tensor_tensor(lin[:, half, :], lin[:, half, :], 1.0, glu[:, half, :], ALU.add, ALU.mult))
                    dve.wait_ge(esig_ready, t * 2 + half + 1)
                    done(v.tensor_tensor(hsw[:, half, :], lin[:, half, :], sig[:, half, :], ALU.mult), hs_ready, t * 2 + half + 1)

            PER = 4 + 4
            routing(0, 1)
            base = ch.n
            with dve.Fori(0, E) as t:
                ch.base, ch.n = t * PER + base, 0
                expert(t, t, 0, 0)
                assert ch.n == PER
            ch.base, ch.n = 0, base + E * PER
            scatter_add(E)
            more = dve.value_load(ofl[0:1, 0:1].bitcast(I32), min_val=0, max_val=1)
            with dve.If(more):
                after = ch.n
                EXTRA = 1 + 4
                ch.link(v.memset(s2, 0.0))
                with dve.Fori(1, PASSES) as b:
                    ch.base, ch.n = b * (EXTRA + E * PER) + (after + 1 - (EXTRA + E * PER)), 0
                    ch.link(v.tensor_scalar(pos, pos, -float(CAP), None, ALU.add))
                    routing(0, b * (E + 1) + 1)
                    assert ch.n == EXTRA
                    v.memset(ofl[:, 3:4], 0.0)
                    with dve.Fori(0, E) as e:
                        ch.base = b * (EXTRA + E * PER) + (e * PER + (after + 1 - E * PER))
                        ch.n = 0
                        expert(b * E + e, e, b, 1)
                dve.wait_ge(sc_ready, 4 * PASSES * E + 4)
                scatter_add(PASSES * E + 1)
            tail = Chain(dve, tail_chain)
            done(v.memset(ofl[:, 2:3], 0.0), acc_final, 1)
            dve.wait_ge(sq_done, 15)
            done(v.tensor_scalar(ssq[:, 0:2], ssq[:, 0:2], 1.0 / D, EPS, ALU.mult, ALU.add), ssq_ready, 4)
            dve.wait_ge(gfin_in, 16)
            dve.wait_ge(rstd_ready, 4)
            for c in range(2):
                done(v.scalar_tensor_tensor(un[:, c, :], acc[:, c, :], rstd[:, c:c + 1], gfin, ALU.mult, ALU.mult),
                     fin_ready, c + 1)

        @block.tensor
        def _(pe):
            tn = nc.tensor

            def mm(o, lhsT, rhs, first, last):
                return tn.matmul(o, lhsT, rhs, start=first, stop=last, skip_group_check=True)

            pe.wait_ge(const_in, 16)
            pe.wait_ge(row_in, 5 * 16)
            tn.transpose(bank[4][:, 0:120], rows[0:120, 0, :], ident[0:120, 0:120])
            tn.transpose(bank[4][:, 128:160], rows[0:32, 1, :], ident[0:32, 0:32]).then_inc(rows_T, 1)
            pe.wait_ge(tab_ready, 1)
            mm(bank[5][0:HEADS, 0:VL], tab[0:NB + 1, 1, :], ohs[0:NB + 1, 0, :], True, True)
            mm(bank[6][0:HEADS, 0:VL], tab[0:NB + 1, 1, :], ohs[0:NB + 1, 1, :], True, True).then_inc(avec_ready, 1)

            def tile(p):
                if p >= 4:
                    pe.wait_ge(tile_saved, p - 3)
                return bank[p % 4]

            def ready(ins):
                ins.then_inc(tile_ready, 1)

            spans = ((0, META), (META, META + BLK), (META + BLK, NT))
            pe.wait_ge(un_ready, 3)
            for k in range(KT):
                b = tile(T_U + k)
                for c, (t0, t1) in enumerate(spans):
                    ins = tn.transpose(b[:, t0:t1], xin[0:t1 - t0, c, k * P:(k + 1) * P], ident[0:t1 - t0, 0:t1 - t0])
                ready(ins)

            def project(p, n, w, cols_n):
                b = tile(p)
                arrived(pe, n)
                for k in range(KT):
                    ins = mm(b[:, 0:cols_n], w(k), uT[:, k, NT - cols_n:NT], k == 0, k == KT - 1)
                ready(ins)

            pe.wait_ge(tile_saved, T_U + 8)
            for j in range(2):
                wk = slot_view(ck % SLOTS, KT, 256)
                project(T_K + j, ck, lambda k, j=j, wk=wk: wk[:, k, P * j:P * j + P], NT)
            wv = slot_view(cvv % SLOTS, KT, 256)
            for c, (t0, t1) in enumerate(spans):
                b = tile(T_V + c)
                arrived(pe, cvv)
                for k in range(KT):
                    ins = mm(b[0:t1 - t0, 0:256], uT[:, k, t0:t1], wv[:, k, :], k == 0, k == KT - 1)
                ready(ins)
            for i in range(8):
                n = cq[i // 2]
                wq = slot_view(n % SLOTS, KT, 2, 128)
                r = i % 2
                project(T_Q + i, n, lambda k, wq=wq, r=r: wq[:, k, r, :], SEQ)
            pe.wait_ge(vec_in, 7 * 16)
            for c, (t0, t1) in enumerate(spans):
                b = tile(T_DT + c)
                for k in range(KT):
                    ins = mm(b[0:t1 - t0, 0:SH], uT[:, k, t0:t1], wdt[:, k, :], k == 0, k == KT - 1)
                ready(ins)

            pe.wait_ge(avec_saved, 1)
            pe.wait_ge(tile_saved, T_X)

            def att_qk(t):
                if t >= 2:
                    pe.wait_ge(logit_done, 2 * (t - 1))
                for half in range(2):
                    b, kk = bank[2 * (t % 2) + half], kz[:, 2 * (t // 4) + half, :]
                    mm(b[:, 0:NT], qT[:, t, BLK:SEQ], kk[:, 0:NT], True, True)
                    ins = mm(b[:, NT:LK], qT[:, t, 0:BLK], kk[:, 0:META + BLK], True, True)
                ins.then_inc(qk_ready, 1)

            def att_transpose(t):
                pe.wait_ge(p_ready, t + 1)
                if t >= 1:
                    pe.wait_ge(ptb_saved, t)
                    pe.wait_ge(ptm_saved, t)
                for half in range(2):
                    pr = logit[:, t % 2, half, :]
                    for i, k0 in enumerate((NT + META, META, META + BLK)):
                        tn.transpose(bank[4 + half][:, i * P:(i + 1) * P], pr[:, k0:k0 + P], ident)
                    for i, k0 in enumerate((NT, 0)):
                        ins = tn.transpose(bank[6][0:META, 256 * half + P * i:256 * half + P * i + P],
                                           pr[:, k0:k0 + META], ident)
                ins.then_inc(pt_ready, 1)

            def att_pv(t):
                pe.wait_ge(ptb_saved, t + 1)
                pe.wait_ge(ptm_saved, t + 1)
                if t >= 1:
                    pe.wait_ge(ya_saved, t)
                for half in range(2):
                    h = 2 * (t // 4) + half
                    o, vv = bank[7][64 * half:64 * half + 64, :], vTC[:, :, HD * h:HD * h + HD]
                    mm(o[:, 0:SEQ], vv[:, 0, :], pT[:, half, 384:640], True, False)
                    mm(o[:, 0:SEQ], vv[:, 1, :], pT[:, half, 0:256], False, False)
                    ins = mm(o[:, BLK:SEQ], vv[:, 2, :], pT[:, half, 256:384], False, True)
                ins.then_inc(pv_ready, 1)

            att_qk(0)
            att_qk(1)
            pe.wait_ge(a_ready, 1)
            for i, m in enumerate((tri_le, tri_gt, ones)):
                ins = mm(bank[7][:, 96 * i:96 * i + 96], m, aa, True, True)
            ins.then_inc(cum_ready, 1)
            pe.wait_ge(decay_ready, 1)
            for t in range(8):
                att_transpose(t)
                if t + 2 < 8:
                    att_qk(t + 2)
                att_pv(t)

            pe.wait_ge(ya_saved, 8)
            pe.wait_ge(zeros_set, 2)

            def conv_transposes(i):
                if 4 <= i < 8:
                    return
                n = i if i < 4 else i - 4
                pe.wait_ge(xs_ready, i + 1)
                if n >= 2:
                    pe.wait_ge(tr_saved, n - 1)
                src = bT[:, i, :] if i < 4 else xs[:, i % 3, :]
                b = bank[4 + n % 2]
                tn.transpose(b[0:META, 0:P], src[:, 0:META], ident)
                ins = tn.transpose(b[:, P:2 * P], src[:, META:META + BLK], ident)
                if i >= 8:
                    ins = tn.transpose(b[:, 2 * P:3 * P], src[:, META + BLK:NT], ident)
                ins.then_inc(tr_ready, 1)

            def state0(g):
                pe.wait_ge(xdec0_ready, g + 1)
                if g:
                    pe.wait_ge(st0_saved, g)
                mm(bank[6][:, :], bTC[:, 0, P * g:P * g + P], xdec0, True, True).then_inc(st0_ready, 1)

            for i in range(24 + 5):
                if i < 24:
                    n = cx[i // 2]
                    wx = slot_view(n % SLOTS, KT, 256)
                    project(T_X + i, n, lambda k, wx=wx, i=i: wx[:, k, P * (i % 2):P * (i % 2) + P], NT)
                if 0 <= i - 2 < 24:
                    conv_transposes(i - 2)
                if i - 5 >= 11 and (i - 5 - 8) % 4 == 3:
                    state0((i - 5 - 8) // 4)

            for n in range(4):
                bs = [tile(T_Z + 2 * n + c) for c in range(2)]
                for h in range(2):
                    wz = slot_view(cz[n][h] % SLOTS, 4, 512)
                    arrived(pe, cz[n][h])
                    for c in range(2):
                        t0 = META + BLK * c
                        for k in range(4):
                            kk = 4 * h + k
                            ins = mm(bs[c][:, :], uT[:, kk, t0:t0 + BLK], wz[:, k, :], kk == 0, kk == KT - 1)
                        if h:
                            ready(ins)

            pe.wait_ge(tile_saved, T_Y)
            pe.wait_ge(tr_saved, 20)
            pe.wait_ge(st0_saved, 4)

            def ssd_seg(it):
                c, g = divmod(it, 4)
                t0 = META + BLK * c
                pe.wait_ge(au_ready, it + 1)
                if it >= 1:
                    pe.wait_ge(e_ready, it)
                if it >= 2:
                    pe.wait_ge(m_ready, it - 1)
                mm(bank[4 + it % 2][:, 0:BLK], bT[:, g, t0:t0 + BLK], cT[:, g, t0:t0 + BLK], True, True)
                for j in range(2):
                    ins = mm(bank[j][:, :], tri_gt, au[:, it % 2, 4 * j:4 * j + 4, :], True, True)
                ins.then_inc(seg_ready, 1)

            def ssd_y(it):
                c, g = divmod(it, 4)
                t0 = META + BLK * c
                pe.wait_ge(m_ready, it + 1)
                if it >= 1:
                    pe.wait_ge(y_done, it)
                mm(bank[6][:, :], cT[:, g, t0:t0 + BLK], hst[:, g, :], True, True)
                for h in range(HPG):
                    q = h // 2
                    ins = mm(bank[2 + h // 4][:, P * (h % 4):P * (h % 4) + P], em[:, it % 2, h, :],
                             xdt[:, it % 2, 2 * q:2 * q + 2, :], True, True)
                if c == 0:
                    ins = mm(bank[7][:, :], bTC[:, 1, P * g:P * g + P], xdec, True, True)
                ins.then_inc(y_ready, 1)

            ssd_seg(0)
            for it in range(8):
                if it + 1 < 8:
                    ssd_seg(it + 1)
                ssd_y(it)

            pe.wait_ge(e_ready, 8)
            pe.wait_ge(yn_ready, 8)
            for i in range(16):
                b = tile(T_Y + i)
                for c in range(2):
                    ins = tn.transpose(b[:, P * c:P * c + P], zy[:, c, P * i:P * i + P], ident)
                ready(ins)

            pe.wait_ge(tile_saved, T_END)
            for dp in range(4):
                g0, g1, ca, s0, s1 = cbr[dp]
                ds_ = (2 * dp, 2 * dp + 1)
                for gi, n in enumerate((g0, g1)):
                    arrived(pe, n)
                    wg = slot_view(n % SLOTS, KT, 256)
                    for d in ds_:
                        if gi == 0 and d >= 4:
                            pe.wait_ge(m_done, d - 3)
                        for k in range(KT):
                            ins = mm(bank[2 * (d % 4)][:, 256 * gi:256 * gi + 256], wg[:, k, P * (d % 2):P * (d % 2) + P],
                                     uT[:, k, META:NT], k == 0, k == KT - 1)
                        if gi:
                            ins.then_inc(gate_ready, 1)
                for bi, n in enumerate((ca, s0, s1)):
                    arrived(pe, n)
                    wb = slot_view(n % SLOTS, KT, 256)
                    for d in ds_:
                        for k in range(KT):
                            rhs = yaT[:, k, :] if bi == 0 else yT[:, 8 * (bi - 1) + k, :]
                            c0 = 0 if bi == 0 else 256
                            ins = mm(bank[2 * (d % 4) + 1][:, c0:c0 + 256], wb[:, k, P * (d % 2):P * (d % 2) + P], rhs,
                                     k == 0 and bi < 2, k == KT - 1 and bi != 1)
                        if bi == 2:
                            ins.then_inc(branch_ready, 1)

            pe.wait_ge(m_done, 8)
            for i in range(4):
                arrived(pe, co[i])
                wo = slot_view(co[i] % SLOTS, 2, 1024)
                for c in range(2):
                    for k in range(2):
                        for n in range(2):
                            ins = mm(bank[2 * c + n][:, :], mT[:, 2 * i + k, BLK * c:BLK * c + BLK],
                                     wo[:, k, 512 * n:512 * n + 512], i == 0 and k == 0, i == 3 and k == 1)
            ins.then_inc(h_ready, 1)

            pe.wait_ge(un_ready, 5)
            for k in range(KT):
                if k >= 4:
                    pe.wait_ge(tile_saved, T_END + k - 3)
                for c in range(2):
                    ins = tn.transpose(bank[k % 4][:, P * c:P * c + P], un[:, c, P * k:P * k + P], ident)
                ready(ins)
            pe.wait_ge(tile_saved, T_END + KT)
            for c in range(2):
                for k in range(KT):
                    ins = mm(bank[4][:, E * c:E * c + E], u2T[:, k, P * c:P * c + P], wrt[:, k, :], k == 0, k == KT - 1)
            ins.then_inc(lg_ready, 1)
            pe.wait_ge(mask_ready, 1)
            mm(bank[6][:, 0:E], tri_lt_b, maskb[:, 0, :], True, True)
            mm(bank[6][:, E:2 * E], ones_b, maskb[:, 0, :], True, False)
            mm(bank[6][:, E:2 * E], tri_lt_b, maskb[:, 1, :], False, True)
            mm(bank[6][:, 2 * E:3 * E], ones_b, maskb[:, 0, :], True, False)
            mm(bank[6][:, 2 * E:3 * E], ones_b, maskb[:, 1, :], False, True).then_inc(rank_ready, 1)
            for c in range(2):
                ins = tn.transpose(bank[5][0:E, P * c:P * c + P], wtok[:, c, 0:E], ident)
            ins.then_inc(wT_ready, 1)
            pe.wait_ge(wT_saved, 1)
            pe.wait_ge(b2_in, 16)
            for c in range(2):
                for n in range(2):
                    ins = mm(bank[2 * c + n][:, :], wT[0:E, P * c:P * c + P], b2sb[0:E, 512 * n:512 * n + 512], True, True)
            ins.then_inc(b2_ready, 1)

            def scatter(s):
                for i in range(4):
                    c, n = divmod(i, 2)
                    if i < 2:
                        pe.wait_ge(sc_added, s * 4)
                    else:
                        pe.wait_ge(sc_added, s * 4 + (i - 1))
                    mm(bank[6 + n][:, :], s2[:, P * c:P * c + P], ysb[:, n, :], True, True).then_inc(sc_ready, 1)

            def expert(t, b, extra):
                pe.wait_ge(g_ready, t + b + 1)
                for k in range(KT):
                    for part in range(3):
                        for c in range(2):
                            ins = mm(bank[4][:, CAP * k:CAP * k + CAP], upart[:, part, c, P * k:P * k + P],
                                     gsel[:, c, :], part == 0 and c == 0, part == 2 and c == 1)
                ins.then_inc(gat_ready, 1)
                for half in range(2):
                    for c in range(2):
                        c0 = 1024 * half + 512 * c
                        mm(bank[half][64 * c:64 * c + 64, :], bsel[0:3 * E, :], b1all[0:3 * E, c0:c0 + 512], True, False)
                pe.wait_ge(ye_saved, t * 2)
                scatter(t + extra)
                for c in range(2):
                    ins = tn.transpose(bank[5][:, P * c:P * c + P], gwt[:, c, :], ident)
                ins.then_inc(s2_ready, 1)
                pe.wait_ge(usel_ready, t + 1)
                for half in range(2):
                    for s_ in range(4):
                        i = 4 * half + s_
                        expert_arrived(pe, i, t)
                        w = slot_view(slot_of(i), 2, 1024)
                        for kk in range(2):
                            for c in range(2):
                                k = 2 * s_ + kk
                                ins = mm(bank[half][64 * c:64 * c + 64, :], usel[:, k, :],
                                         w[:, kk, 512 * c:512 * c + 512], False, k == KT - 1)
                        ins.then_inc(slot_used, 1)
                pe.wait_ge(s2_saved, t + 1)
                for half in range(2):
                    pe.wait_ge(hs_ready, t * 2 + half + 1)
                    if half:
                        pe.wait_ge(hT_saved, t * 2 + 1)
                    for q in range(2):
                        ins = tn.transpose(bank[5][:, P * q:P * q + P], hsw[:, half, P * q:P * q + P], ident)
                    ins.then_inc(hT_ready, 1)
                    pe.wait_ge(hT_saved, t * 2 + half + 1)
                    for q in range(2):
                        i = 8 + 2 * half + q
                        expert_arrived(pe, i, t)
                        w = slot_view(slot_of(i), 2, 1024)
                        for n in range(2):
                            for c in range(2):
                                ins = mm(bank[2 + n][64 * c:64 * c + 64, :], hT[:, half, q, 64 * c:64 * c + 64],
                                         w[:, c, 512 * n:512 * n + 512], half == 0 and q == 0, half == 1 and q == 1)
                        ins.then_inc(slot_used, 1)

            pe.wait_ge(route_done, 1)
            with pe.Fori(0, E) as t:
                expert(t, 0, 0)
            pe.wait_ge(ye_saved, 2 * E)
            scatter(E)
            more = pe.value_load(ofl[0:1, 0:1].bitcast(I32), min_val=0, max_val=1)
            with pe.If(more):
                with pe.Fori(1, PASSES) as b:
                    with pe.Fori(0, E) as e:
                        expert(b * E + e, b, 1)
                pe.wait_ge(ye_saved, 2 * PASSES * E)
                scatter(PASSES * E + 1)


def kernel(**inputs):
    import concourse.bacc as bacc
    from concourse.bass_utils import run_bass_kernel_spmd

    flat = {
        "x": inputs["x"].reshape(SEQ, D), "meta": inputs["meta_tokens"], "rel": inputs["rel_bias"],
        "g_mix": inputs["norm_mix_g"].reshape(D), "w_in": inputs["w_in"][0], "sinks": inputs["attn_sinks"].reshape(-1),
        "conv_w": inputs["conv_w"][0], "conv_b": inputs["conv_b"].reshape(-1), "dt_bias": inputs["dt_bias"].reshape(-1),
        "a_log": inputs["a_log"].reshape(-1), "d_skip": inputs["d_skip"].reshape(-1),
        "g_ssm": inputs["ssm_norm_g"].reshape(-1), "w_att": inputs["w_attn_br"][0], "w_ssm": inputs["w_ssm_br"][0],
        "w_out": inputs["w_out"][0], "g_ffn": inputs["norm_ffn_g"].reshape(-1), "w_rt": inputs["w_router"][0],
        "b_rt": inputs["b_router"].reshape(-1), "w1": inputs["w_exp_in"][0], "b1": inputs["b_exp_in"][0],
        "w2": inputs["w_exp_out"][0], "b2": inputs["b_exp_out"][0], "g_fin": inputs["norm_final_g"],
    }
    i = np.arange(P)
    squares = np.stack([i[:, None] == i[None, :], i[:, None] <= i[None, :], i[:, None] > i[None, :],
                        np.ones((P, P)), np.broadcast_to(i % CAP, (P, P))], axis=1).astype(np.float32)
    flat["c_sq"] = squares
    flat["c_oh"] = distance_one_hots()
    nc = bacc.Bacc("TRN2", target_bir_lowering=False, num_devices=1)
    arrays, args = {}, {}
    for name, a in flat.items():
        a = np.ascontiguousarray(a)
        arrays["in_" + name] = a
        args[name] = nc.dram_tensor("in_" + name, a.shape, mybir.dt.from_np(a.dtype), kind="ExternalInput").ap()
    args["out"] = nc.dram_tensor("out_0", (SEQ, D), F32, kind="ExternalOutput").ap()
    hybrid_layer(nc, **args)
    r = run_bass_kernel_spmd(nc, [arrays], core_ids=[0])
    return r.results[0]["out_0"].reshape(1, SEQ, D)
```

```python
import math
from contextlib import ExitStack

import numpy as np

import concourse.bass as bass
from concourse import mybir

F32 = mybir.dt.float32
BF16 = mybir.dt.bfloat16
U32 = mybir.dt.uint32
I32 = mybir.dt.int32
ALU = mybir.AluOpType
ACT = mybir.ActivationFunctionType
AX = mybir.AxisListType.X

P = 128
D = 1024
KT = D // P
META = 16
SEQ = 256
NT = META + SEQ
BLK = 128
HEADS, KV, HD = 16, 4, 64
NB, MAXD, WINDOW = 32, 128, 128
DI = 2048
SH = 32
G = 4
HPG = SH // G
NS = 128
CW = 4
E = 32
FF = 1024
CAP = 64
PASSES = SEQ // CAP
EPS = 1e-5
ALPHA, LIMIT = 1.702, 7.0
COL_Q, COL_K, COL_V, COL_Z = 0, 1024, 1280, 1536
COL_X = COL_Z + DI
COL_B = COL_X + DI
COL_C = COL_B + G * NS
COL_DT = COL_C + G * NS
COL_G = COL_DT + SH
SLOTS = 12
SLOT = 2048
FSLOTS = 8
NEG = -1e30
VL = 400
LK = NT + META + BLK


def distance_one_hots():
    x = np.arange(VL)
    dist = NT - 1 - x
    n = np.maximum(dist, 0)
    exact = NB // 2
    nf = np.maximum(n, 1).astype(np.float32)
    large = exact + (np.log(nf / np.float32(exact)) / np.float32(math.log(MAXD / exact))
                     * np.float32(NB - exact)).astype(np.int32)
    bucket = np.where(n < exact, n, np.minimum(large, NB - 1))
    oh = np.zeros((NB + 1, 2, VL), np.float32)
    oh[bucket, :, x] = 1.0
    oh[NB, 1, :] = np.where((dist >= 0) & (dist < WINDOW), 0.0, NEG)
    return oh


class Chain:

    def __init__(self, eng, sem, base=0):
        self.eng, self.sem, self.base, self.n = eng, sem, base, 0

    def link(self, ins):
        self.n += 1
        ins.then_inc(self.sem, 1)
        self.eng.wait_ge(self.sem, self.base + self.n)


def hybrid_layer(nc, x, meta, rel, g_mix, w_in, sinks, conv_w, conv_b, dt_bias, a_log, d_skip, g_ssm,
                 w_att, w_ssm, w_out, g_ffn, w_rt, b_rt, w1, b1, w2, b2, g_fin, c_sq, c_oh, out):
    ctx = ExitStack()
    with ctx:
        def sb(name, shape, dt=F32):
            return ctx.enter_context(nc.sbuf_tensor(name, shape, dt))

        def sem(name):
            return ctx.enter_context(nc.semaphore(name))

        ring = sb("ring", [P, SLOTS, SLOT])
        squares = sb("squares", [P, 5, P])
        ident, tri_le, tri_gt, ones, iota2 = (squares[:, i, :] for i in range(5))
        wdt = sb("wdt", [P, KT, SH])
        wrt = sb("wrt", [P, KT, E])
        rows = sb("rows", [P, 2, P])
        cols = sb("cols", [P, 152])
        col_cw, col_cb = cols[:, 0:96], cols[:, 96:120]
        col_gmix, col_gffn, col_gssm = cols[:, 120:128], cols[:, 128:136], cols[:, 136:152]
        dtb, alog, dskip, brt = (sb(n, [P, 32]) for n in ("dtb", "alog", "dskip", "brt"))
        sink_nat, sink_p = sb("sink_nat", [P, HEADS]), sb("sink_p", [P, HEADS])
        half_neg = sb("half_neg", [P, 8])
        ssq, rstd = sb("ssq", [P, 8]), sb("rstd", [P, 8])
        dts = sb("dts", [P, 7, 96])
        dt, aa = dts[:, 0, :], dts[:, 1, :]
        decays = sb("decays", [P, 3, 3, SH])
        stats = sb("stats", [P, 6, 4])
        tab = sb("tab", [NB + 1, 2, HEADS])
        arena = sb("arena", [P, 25024])

        def at(off, *shape, dt=F32):
            n = int(np.prod(shape))
            words = n if dt != BF16 else n // 2
            v = arena[:, off:off + words]
            if dt != F32:
                v = v.bitcast(dt)
            if len(shape) == 1:
                return v
            names = "abcd"[:len(shape)]
            return v.rearrange(f"p ({' '.join(names)}) -> p {' '.join(names)}",
                               **{names[i]: shape[i] for i in range(len(shape))})

        uT = at(0, KT, NT)
        yaT = at(2176, KT, SEQ)
        bT, cT = at(4224, G, NT), at(5312, G, NT)
        xTC = at(6400, 2, DI)
        bTC = at(10496, 2, G * NS)
        R = 11520
        qT = at(R, KT, SEQ)
        kz = at(R + 2048, KV, NT)
        vTC = at(R + 3136, 3, KV * HD)
        toep = at(R + 3904, HEADS, LK)
        xin = at(R + 3904, 3, D)
        dtT = at(6400, NT)
        logit = at(R + 10560, 2, 2, LK)
        ohs = at(R + 10560, 2, VL)
        avec = at(R + 11360, 2, VL)
        pT = at(R + 12224, 2, 640)
        zy = at(R, 2, DI)
        hst = at(R + 4096, G, HPG * HD)
        S0 = R + 6144
        xpre, cv, sg = at(S0, 2, 276), at(S0 + 552, 2, NT), at(S0 + 1096, 2, NT)
        xs = at(S0 + 1640, 3, NT)
        xm, xdec0 = at(S0 + 2456, 512), at(S0 + 2968, 512)
        ztmp = ring[:, FSLOTS, 0:1024].rearrange("p (a b) -> p a b", a=2)
        au = at(S0, 2, HPG, BLK)
        em = at(S0 + 2048, 2, HPG, BLK)
        cbm = at(S0 + 4096, 2, BLK)
        xdt = at(S0 + 4352, 2, HPG, HD)
        xdec = at(S0 + 5376, HPG, HD)
        ysum = at(S0 + 5888, HPG, HD)
        sq_scratch = at(R + 12544, 512)
        yT = at(S0, 16, SEQ)
        mT = at(6400, KT, SEQ)
        gsig = ring[:, SLOTS - 2:SLOTS, :].rearrange("p s (a b) -> p (s a) b", b=512)
        gmul = at(9472, 2, 512)
        acc = at(0, 2, D)
        xres = at(4224, 2, D)
        un = at(8448, 2, D)
        u2T = at(2176, KT, SEQ)
        upart = at(R + 10240, 3, 2, D, dt=BF16)
        ures = xres
        b1raw = at(R, 2 * FF)
        b1res = at(R + 5120, 1024)
        b1all = at(R + 2048, 2 * FF, dt=BF16)
        b1mid, b1lo = at(R + 3072, 2 * FF, dt=BF16), at(R + 4096, 2 * FF, dt=BF16)
        b2sb = at(R, D)
        X0 = R + 5120
        s2 = at(X0, SEQ)
        usel = at(X0 + 256, KT, CAP)
        glu, sig, lin, hsw = (at(X0 + 768 + 512 * i, 2, 256) for i in range(4))
        hT = at(X0 + 2816, 2, 2, P)
        wT = at(X0 + 3328, SEQ)
        rt = at(X0 + 3584, 16, 64)
        ysb = at(6400, 2, 512)
        gfin = at(7424, D)
        gwt = at(10496, 2, P)
        gsel = at(10752, 2, CAP, dt=BF16)
        bsel = at(10816, CAP, dt=BF16)
        pos = at(10880, 2, 40)
        wtok = at(10960, 2, 40)
        ident3 = at(11040, 40)
        ofl = at(11080, 8)
        maskb = at(11088, 2, E, dt=BF16)
        tri_lt_b, ones_b = at(11120, P, dt=BF16), at(11184, P, dt=BF16)
        topv, negm, wsum = at(11248, 2, 8), at(11264, 2, 1), at(11268, 2, 1)
        topi = at(11272, 2, 8).bitcast(U32)
        topf, tope = at(11288, 2, 8), at(11304, 2, 8)

        bank = [ctx.enter_context(nc.psum_tensor(f"bank{i}", [P, 512], F32)) for i in range(8)]
        toep_rows = nc.dram_tensor("toep_rows", (P, HEADS, 2, VL), F32, kind="Internal").ap()

        slot_loaded = [sem(f"slot_loaded{i}") for i in range(SLOTS)]
        slot_used = sem("slot_used")
        x_in, const_in, vec_in, row_in, rel_in = (sem(n) for n in ("x_in", "const_in", "vec_in", "row_in", "rel_in"))
        toep_out, toep_in, xres_in, b1_in, b1_spread, b2_in, gfin_in, out_done = (sem(n) for n in (
            "toep_out", "toep_in", "xres_in", "b1_in", "b1_spread", "b2_in", "gfin_in", "out_done"))
        dve_chain, act_chain = sem("dve_chain"), sem("act_chain")
        zeros_set, sq_done, ssq_ready, rstd_ready, un_ready, acc_final, tail_chain = (sem(n) for n in (
            "zeros_set", "sq_done", "ssq_ready", "rstd_ready", "un_ready", "acc_final", "tail_chain"))
        tile_ready, tile_saved = sem("tile_ready"), sem("tile_saved")
        rows_T, cols_saved, tab_ready, avec_ready, avec_saved = (sem(n) for n in (
            "rows_T", "cols_saved", "tab_ready", "avec_ready", "avec_saved"))
        a_ready, cum_ready, decay_ready, alog_exp, nabs_ready, dt_exp = (sem(n) for n in (
            "a_ready", "cum_ready", "decay_ready", "alog_exp", "nabs_ready", "dt_exp"))
        qk_ready, logit_done, max_ready, exp_ready, p_ready, pt_ready, ptm_saved, ptb_saved, pv_ready, ya_saved = (
            sem(n) for n in ("qk_ready", "logit_done", "max_ready", "exp_ready", "p_ready", "pt_ready",
                             "ptm_saved", "ptb_saved", "pv_ready", "ya_saved"))
        conv_ready, csig_ready, xs_ready, tr_ready, tr_saved, xdec0_ready, st0_ready, st0_saved, z_ready, z_saved = (
            sem(n) for n in ("conv_ready", "csig_ready", "xs_ready", "tr_ready", "tr_saved", "xdec0_ready",
                             "st0_ready", "st0_saved", "z_ready", "z_saved"))
        au_ready, seg_ready, e_ready, m_ready, y_ready, y_done, yn_ready = (sem(n) for n in (
            "au_ready", "seg_ready", "e_ready", "m_ready", "y_ready", "y_done", "yn_ready"))
        gate_ready, gate_saved, branch_ready, gsig_ready, m_done, h_ready, h_done = (sem(n) for n in (
            "gate_ready", "gate_saved", "branch_ready", "gsig_ready", "m_done", "h_ready", "h_done"))
        lg_ready, b2_cleared, topexp_in, topexp_ready, mask_ready, rank_ready, wtok_ready, wT_ready, wT_saved, b2_ready, route_done = (
            sem(n) for n in ("lg_ready", "b2_cleared", "topexp_in", "topexp_ready", "mask_ready", "rank_ready", "wtok_ready", "wT_ready",
                             "wT_saved", "b2_ready", "route_done"))
        b1_ready, flag_ready = sem("b1_ready"), sem("flag_ready")
        g_ready, gat_ready, s2_ready, s2_saved, usel_ready, glu_ready, esig_ready, hs_ready, hT_ready, hT_saved = (
            sem(n) for n in ("g_ready", "gat_ready", "s2_ready", "s2_saved", "usel_ready", "glu_ready",
                             "esig_ready", "hs_ready", "hT_ready", "hT_saved"))
        ye_saved, sc_ready, sc_added, fin_ready = (sem(n) for n in ("ye_saved", "sc_ready", "sc_added", "fin_ready"))

        def cols_of(w, c0, kt=KT, k0=0, n=256):
            return w[k0 * P:(k0 + kt) * P, c0:c0 + n].rearrange("(k p) c -> p k c", p=P)

        def slot_view(s, *shape):
            names = "abc"[:len(shape)]
            return ring[:, s, 0:int(np.prod(shape))].rearrange(
                f"p ({' '.join(names)}) -> p {' '.join(names)}", **{names[i]: shape[i] for i in range(len(shape))})

        chunks = []

        def add(*parts):
            chunks.append(parts)
            return len(chunks) - 1

        K8 = (lambda s: slot_view(s, KT, 256))
        ck = add((K8, cols_of(w_in, COL_K)))
        cvv = add((K8, cols_of(w_in, COL_V)))
        cq = []
        for j in range(2):
            for r in range(0, 4, 2):
                parts = []
                for half in range(2):
                    c0 = COL_Q + (8 * j + 4 * half + r) * HD
                    for i in range(2):
                        parts.append((lambda s, half=half, i=i: slot_view(s, KT, 2, 128)[:, :, i, HD * half:HD * half + HD],
                                      cols_of(w_in, c0 + HD * i, n=HD)))
                cq.append(add(*parts))
        cg = [[add((K8, cols_of(w_in, COL_G + D * gi + 256 * dp))) for gi in range(2)] for dp in range(4)]
        conv_tiles = [16 + i for i in range(8)] + list(range(16))
        cx = [add((K8, cols_of(w_in, COL_X + conv_tiles[2 * i] * P))) for i in range(12)]
        cz = [[add((lambda s: slot_view(s, 4, 512), cols_of(w_in, COL_Z + 512 * n, kt=4, k0=4 * h, n=512)))
               for h in range(2)] for n in range(4)]
        w_att_v = w_att.rearrange("(j h r d) c -> h j d r c", j=2, h=2, r=4)

        def att_branch_chunk(dp):
            parts = []
            for half in range(2):
                for j in range(2):
                    parts.append((lambda s, half=half, j=j: slot_view(s, KT, 256)[64 * half:64 * half + 64, 4 * j:4 * j + 4, :],
                                  w_att_v[half, j, :, :, 256 * dp:256 * dp + 256]))
            return add(*parts)

        ca = [att_branch_chunk(dp) for dp in range(2)]
        cs = []
        for dp in range(4):
            if dp >= 2:
                ca.append(att_branch_chunk(dp))
            cs.append([add((K8, cols_of(w_ssm, 256 * dp, k0=k0))) for k0 in (0, 8)])
        co = [add((lambda s: slot_view(s, 2, 1024), cols_of(w_out, 0, kt=2, k0=2 * i, n=1024))) for i in range(4)]
        FRONT = len(chunks)
        loaded_at, seen = [], [0] * SLOTS
        for n, parts in enumerate(chunks):
            seen[n % FSLOTS] += 16 * len(parts)
            loaded_at.append(seen[n % FSLOTS])

        def arrived(eng, n):
            eng.wait_ge(slot_loaded[n % FSLOTS], loaded_at[n])

        T_U, T_K, T_V = 0, 8, 10
        T_DT, T_DTT = 13, 15
        T_Q = [14] + list(range(16, 23))
        T_X = 23
        T_Y = T_X + 24
        T_END = T_Y + 16

        released = [None] * FRONT
        released[ck], released[cvv] = (tile_ready, T_K + 2), (tile_ready, T_V + 3)
        for i, n in enumerate(cq):
            released[n] = (tile_ready, T_Q[2 * i + 1] + 1)
        for i, n in enumerate(cx):
            released[n] = (tile_ready, T_X + 2 * i + 2)
        for i, pair in enumerate(cz):
            for n in pair:
                released[n] = (z_ready, 2 * i + 2)
        for dp in range(4):
            for n in cg[dp]:
                released[n] = (gate_ready, 2 * dp + 2)
            for n in (ca[dp], *cs[dp]):
                released[n] = (branch_ready, 2 * dp + 2)
        for n in co:
            released[n] = (h_ready, 2)

        def slot_of(i):
            return (FSLOTS + i) % SLOTS

        def b2_bank(c, n):
            return bank[(0, 1, 4, 5)[2 * c + n]]

        def z_bank(it):
            return bank[5 if it else 7]

        GATE_FIRST = 4
        gate_before = [t % 2 for t in range(8)]
        gates_by = [(GATE_FIRST + sum(gate_before[:t + 1]) + t + 1) // 2 for t in range(8)]
        assert gates_by[-1] == 8

        def expert_arrived(eng, i, t):
            eng.wait_ge(slot_loaded[slot_of(i)], t * 16 + (seen[slot_of(i)] + 16))

        w1_v = w1.rearrange("e (s k p) (h c) -> e h s p k c", p=P, k=2, h=2)
        w2_v = w2.rearrange("e (h c b p) n -> e h b p c n", p=P, h=2, c=2)

        def expert_sources(e):
            one = bass.ds(e, 1)
            src = [w1_v[one, h, s].rearrange("e p k c -> p (e k) c") for h in range(2) for s in range(4)]
            src += [w2_v[one, h, b].rearrange("e p c n -> p (e c) n") for h in range(2) for b in range(2)]
            return src

        block = ctx.enter_context(nc.Block())

        @block.sync
        def _(sp):
            sp.dma_start(xin[:, 1:3, :], x.rearrange("(c p) d -> p c d", p=P)).then_inc(x_in, 16)
            sp.dma_start(xin[0:META, 0, :], meta).then_inc(x_in, 16)
            for n, parts in enumerate(chunks):
                if n >= FSLOTS:
                    sp.wait_ge(*released[n - FSLOTS])
                for dst, src in parts:
                    sp.dma_start(dst(n % FSLOTS), src).then_inc(slot_loaded[n % FSLOTS], 16)

            def expert(t, e):
                for i, src in enumerate(expert_sources(e)):
                    if isinstance(t, int):
                        if i < SLOTS - FSLOTS:
                            sp.wait_ge(m_done, 8)
                        else:
                            last = max(n for n in range(FRONT) if n % FSLOTS == slot_of(i))
                            sp.wait_ge(*released[last])
                    else:
                        sp.wait_ge(slot_used, t * 12 + (i + 1 - SLOTS))
                    sp.dma_start(slot_view(slot_of(i), 2, 1024), src).then_inc(slot_loaded[slot_of(i)], 16)

            expert(0, 0)
            with sp.Fori(1, E) as e:
                expert(e, e)
            sp.wait_ge(flag_ready, 1)
            more = sp.value_load(ofl[0:1, 0:1].bitcast(I32), min_val=0, max_val=1)
            with sp.If(more):
                with sp.Fori(1, PASSES) as b:
                    with sp.Fori(0, E) as e:
                        expert(b * E + e, e)
            for c in range(2):
                sp.wait_ge(fin_ready, c + 1)
                sp.dma_start(out[c * P:(c + 1) * P, :], un[:, c, :]).then_inc(out_done, 16)
            sp.wait_ge(out_done, 32)

        @block.gpsimd
        def _(pool):
            pool.dma_start(ohs[0:NB + 1, :, :], c_oh).then_inc(rel_in, 16)
            pool.dma_start(tab[0:NB, 0, :], rel).then_inc(rel_in, 16)
            norms = ((0, 3), (0, 8), (0, 1), (1, 2), (0, 2))

            def rsqrt(n):
                pool.wait_ge(ssq_ready, n + 1)
                a, b = norms[n]
                pool.tensor_tensor(rstd[:, a:b], ssq[:, a:b], half_neg[:, a:b],
                                   ALU.pow).then_inc(rstd_ready, 1)

            rsqrt(0)
            pool.wait_ge(avec_saved, 1)
            pool.dma_start(toep_rows.rearrange("q h a v -> h q (a v)"),
                           avec[0:HEADS, :, :].rearrange("p a v -> p (a v)").unsqueeze(1).to_broadcast([HEADS, P, 2 * VL])
                           ).then_inc(toep_out, 16)
            pool.wait_ge(toep_out, 16)
            pool.wait_ge(tile_ready, T_U + 8)
            RP = HEADS * 2 * VL

            def toeplitz(x0, half, n):
                return bass.AP(toep_rows.tensor, half * VL + x0, [[RP - 1, P], [2 * VL, HEADS], [1, n]])

            with nc.allow_non_contiguous_dma(reason="short runs of the bias"):
                pool.dma_start(toep[:, :, 0:META], toeplitz(127, 0, META)).then_inc(toep_in, 16)
                pool.dma_start(toep[:, :, META:NT], toeplitz(127 + META, 1, SEQ)).then_inc(toep_in, 16)
                pool.dma_start(toep[:, :, NT:NT + META], toeplitz(255, 0, META)).then_inc(toep_in, 16)
                pool.dma_start(toep[:, :, NT + META:LK], toeplitz(255 + META, 1, BLK)).then_inc(toep_in, 16)
            for n in range(1, 5):
                rsqrt(n)
                if n == 1:
                    pool.wait_ge(y_done, 8)
                    pool.dma_start(xres, x.rearrange("(c p) d -> p c d", p=P)).then_inc(xres_in, 16)
                    pool.wait_ge(tile_ready, T_END)
                    pool.dma_start(b1raw[0:E, :], b1).then_inc(b1_in, 16)
                    pool.wait_ge(b1_ready, 1)
                    pool.dma_start(b1all[E:2 * E, :], b1mid[0:E, :]).then_inc(b1_spread, 16)
                    pool.dma_start(b1all[2 * E:3 * E, :], b1lo[0:E, :]).then_inc(b1_spread, 16)
                    pool.memset(b2sb, 0.0).then_inc(b2_cleared, 1)
                    pool.wait_ge(branch_ready, 8)
                    pool.memset(wT, 0.0).then_inc(b2_cleared, 1)
                    pool.wait_ge(b2_cleared, 2)
                    pool.dma_start(b2sb[0:E, :], b2).then_inc(b2_in, 16)
                if n == 3:
                    pool.wait_ge(route_done, 1)
                    pool.dma_start(gfin, bass.AP(g_fin.tensor, 0, [[0, P], [1, D]])).then_inc(gfin_in, 16)

        @block.scalar
        def _(act):
            sc = nc.scalar
            ch = Chain(act, act_chain)
            act.dma_start(squares[:, :, :], c_sq).then_inc(const_in, 16)
            act.dma_start(rows[0:96, 0, :], conv_w.rearrange("w (i c) -> (w i) c", c=P)).then_inc(row_in, 16)
            act.dma_start(rows[96:120, 0, :], conv_b.rearrange("(i c) -> i c", c=P)).then_inc(row_in, 16)
            act.dma_start(rows[0:8, 1, :], g_mix.rearrange("(i c) -> i c", c=P)).then_inc(row_in, 16)
            act.dma_start(rows[8:16, 1, :], g_ffn.rearrange("(i c) -> i c", c=P)).then_inc(row_in, 16)
            act.dma_start(rows[16:32, 1, :], g_ssm.rearrange("(i c) -> i c", c=P)).then_inc(row_in, 16)
            for dst, src, n in ((dtb, dt_bias, SH), (alog, a_log, SH), (dskip, d_skip, SH), (brt, b_rt, E),
                                (sink_nat, sinks, HEADS)):
                act.dma_start(dst[:, :], bass.AP(src.tensor, 0, [[0, P], [1, n]])).then_inc(vec_in, 16)
            act.dma_start(wdt[:, :, :], cols_of(w_in, COL_DT, n=SH)).then_inc(vec_in, 16)
            act.dma_start(wrt[:, :, :], w_rt.rearrange("(k p) e -> p k e", p=P)).then_inc(vec_in, 16)

            def squared(ins, val):
                ins.then_inc(sq_done, 1)
                act.wait_ge(sq_done, val)

            act.wait_ge(x_in, 32)
            act.wait_ge(zeros_set, 1)
            for c, r in ((0, META), (1, P), (2, P)):
                squared(sc.activation(uT.rearrange("p k n -> p (k n)")[0:r, 0:D], xin[0:r, c, :], ACT.Square,
                                      accum_out=ssq[0:r, c:c + 1]), c + 1)
            act.wait_ge(rows_T, 1)
            ch.link(sc.activation(cols[:, 0:120], bank[4][:, 0:120], ACT.Copy))
            sc.activation(cols[:, 120:152], bank[4][:, 128:160], ACT.Copy).then_inc(cols_saved, 1)
            act.wait_ge(cols_saved, 1)
            act.wait_ge(avec_ready, 1)
            ch.link(sc.activation(avec[0:HEADS, 0, :], bank[5][0:HEADS, 0:VL], ACT.Copy))
            sc.activation(avec[0:HEADS, 1, :], bank[6][0:HEADS, 0:VL], ACT.Copy).then_inc(avec_saved, 1)
            def tile(p):
                act.wait_ge(tile_ready, p + 1)
                return bank[p % 4]

            def saved(ins):
                ins.then_inc(tile_saved, 1)

            for k in range(KT):
                saved(sc.activation(uT[:, k, :], tile(T_U + k)[:, 0:NT], ACT.Copy, scale=col_gmix[:, k:k + 1]))
            for j in range(2):
                b = tile(T_K + j)
                ch.link(sc.activation(kz[0:64, 2 * j, :], b[0:64, 0:NT], ACT.Copy))
                saved(sc.activation(kz[64:128, 2 * j + 1, :], b[64:128, 0:NT], ACT.Copy))
            for c, r in ((0, META), (1, P), (2, P)):
                saved(sc.activation(vTC[0:r, c, :], tile(T_V + c)[0:r, 0:256], ACT.Copy))
            saved(sc.activation(dtT[0:SH, :], tile(T_DT)[0:SH, 0:NT], ACT.Copy))
            for i in range(8):
                saved(sc.activation(qT[:, i, :], tile(T_Q[i])[:, 0:SEQ], ACT.Copy))
                if i == 0:
                    b = tile(T_DTT)
                    ch.link(sc.activation(dts[0:META, 2, 0:SH], b[0:META, 0:SH], ACT.Copy))
                    saved(sc.activation(dts[:, 2, SH:3 * SH], b[:, SH:3 * SH], ACT.Copy))
            act.wait_ge(vec_in, 7 * 16)
            sc.activation(dts[:, 6, 0:SH], alog[:, :], ACT.Exp).then_inc(alog_exp, 1)
            act.wait_ge(nabs_ready, 1)
            sc.activation(dts[:, 4, :], dts[:, 3, :], ACT.Exp).then_inc(dt_exp, 1)
            act.wait_ge(cum_ready, 1)
            sc.activation(decays[:, :, :, :], bank[7][:, 0:288].rearrange("p (a c h) -> p a c h", a=3, c=3),
                          ACT.Exp).then_inc(decay_ready, 1)

            def att_exp(t):
                act.wait_ge(max_ready, t + 1)
                for half in range(2):
                    for n, (a, b) in enumerate(((0, NT), (NT, LK))):
                        ch.link(sc.activation(logit[:, t % 2, half, a:b], logit[:, t % 2, half, a:b], ACT.Exp,
                                              bias=stats[:, 1, 2 * half + n:2 * half + n + 1],
                                              accum_out=stats[:, 3, 2 * half + n:2 * half + n + 1]))
                sc.activation(stats[:, 4, :], stats[:, 2, :], ACT.Exp).then_inc(exp_ready, 1)

            def att_save(t):
                act.wait_ge(pt_ready, t + 1)
                if t >= 1:
                    act.wait_ge(pv_ready, t)
                for half in range(2):
                    ins = sc.activation(pT[:, half, 0:384], bank[4 + half][:, 0:384], ACT.Copy)
                    if half:
                        ins.then_inc(ptb_saved, 1)
                act.wait_ge(pv_ready, t + 1)
                sc.activation(yaT[:, t, :], bank[7][:, 0:SEQ], ACT.Copy).then_inc(ya_saved, 1)

            def gate_save(d):
                act.wait_ge(gate_ready, d + 1)
                sc.activation(gsig[:, d, :], bank[2 + d % 2][:, :], ACT.Copy).then_inc(gate_saved, 1)

            gate_save(0)
            att_exp(0)
            gate_save(1)
            for t in range(8):
                if t + 1 < 8:
                    att_exp(t + 1)
                att_save(t)
                for d in range(gates_by[t - 1] if t else 2, gates_by[t]):
                    gate_save(d)

            def conv_evict(i):
                b = tile(T_X + i)
                if i >= 2:
                    act.wait_ge(conv_ready, i - 1)
                saved(sc.activation(xpre[:, i % 2, 3:3 + NT], b[:, 0:NT], ACT.Copy))

            def conv_sig(i):
                act.wait_ge(conv_ready, i + 1)
                if i >= 2:
                    act.wait_ge(xs_ready, i - 1)
                sc.activation(sg[:, i % 2, :], cv[:, i % 2, :], ACT.Sigmoid).then_inc(csig_ready, 1)

            def conv_tr(i):
                if 4 <= i < 8:
                    return
                n = i if i < 4 else i - 4
                act.wait_ge(tr_ready, n + 1)
                b = bank[4 + n % 2]
                if i < 4:
                    ch.link(sc.activation(bTC[0:META, 0, i * P:(i + 1) * P], b[0:META, 0:P], ACT.Copy))
                    sc.activation(bTC[:, 1, i * P:(i + 1) * P], b[:, P:2 * P], ACT.Copy).then_inc(tr_saved, 1)
                else:
                    j = i - 8
                    if j % 4 == 0 and j:
                        act.wait_ge(xdec0_ready, j // 4)
                    ch.link(sc.activation(xm[0:META, (j % 4) * P:(j % 4 + 1) * P], b[0:META, 0:P], ACT.Copy))
                    sc.activation(xTC[:, :, j * P:(j + 1) * P],
                                  b[:, P:3 * P].rearrange("p (c n) -> p c n", c=2), ACT.Copy).then_inc(tr_saved, 1)

            def st0_save(g):
                act.wait_ge(st0_ready, g + 1)
                sc.activation(hst[:, g, :], bank[6][:, :], ACT.Copy).then_inc(st0_saved, 1)

            def z_evict(it):
                g, c = divmod(it, 2)
                act.wait_ge(z_ready, it + 1)
                if it >= 2:
                    act.wait_ge(y_done, it - 1)
                ch.link(sc.activation(zy[:, c, 512 * g:512 * g + 512], z_bank(it)[:, :], ACT.Sigmoid))
                sc.activation(ztmp[:, it % 2, :], z_bank(it)[:, :], ACT.Copy).then_inc(z_saved, 1)

            act.wait_ge(gate_saved, 8)
            for i in range(24 + 5):
                if i < 24:
                    conv_evict(i)
                if 8 <= i < 16:
                    sc.activation(gsig[:, i - 8, :], gsig[:, i - 8, :], ACT.Sigmoid).then_inc(gsig_ready, 1)
                if i == 24:
                    z_evict(0)
                if 0 <= i - 1 < 24:
                    conv_sig(i - 1)
                if 0 <= i - 3 < 24:
                    conv_tr(i - 3)
                if i - 5 >= 11 and (i - 5 - 8) % 4 == 3:
                    st0_save((i - 5 - 8) // 4)

            def ssd_exp(it):
                act.wait_ge(seg_ready, it + 1)
                if it >= 2:
                    act.wait_ge(y_ready, it - 1)
                for j in range(2):
                    ins = sc.activation(em[:, it % 2, 4 * j:4 * j + 4, :],
                                        bank[j][:, :].rearrange("p (h l) -> p h l", h=4), ACT.Exp)
                    if j:
                        ins.then_inc(e_ready, 1)

            ssd_exp(0)
            for it in range(8):
                if it + 1 < 8:
                    ssd_exp(it + 1)
                    z_evict(it + 1)
                act.wait_ge(y_done, it + 1)
                g, c = divmod(it, 2)
                squared(sc.activation(sq_scratch, zy[:, c, 512 * g:512 * g + 512], ACT.Square,
                                      accum_out=ssq[:, it:it + 1]), 3 + it + 1)

            for i in range(16):
                act.wait_ge(tile_ready, T_Y + i + 1)
                saved(sc.activation(yT[:, i, :], bank[4 + i % 4][:, 0:SEQ], ACT.Copy, scale=col_gssm[:, i:i + 1]))

            for c in range(2):
                act.wait_ge(h_done, 2 * c + 2)
                squared(sc.activation(ures[:, c, :], acc[:, c, :], ACT.Square, accum_out=ssq[:, c:c + 1]), 11 + c + 1)
            for k in range(KT):
                act.wait_ge(tile_ready, T_END + k + 1)
                sc.activation(u2T[:, k, :], bank[4 + k % 4][:, 0:SEQ], ACT.Copy,
                              scale=col_gffn[:, k:k + 1]).then_inc(tile_saved, 1)
            act.wait_ge(topexp_in, 1)
            for c in range(2):
                ins = sc.activation(tope[:, c, 0:4], topv[:, c, 0:4], ACT.Exp, bias=negm[:, c, :],
                                    accum_out=wsum[:, c, :])
                if c:
                    ins.then_inc(topexp_ready, 1)
                else:
                    ch.link(ins)
            act.wait_ge(b2_cleared, 2)
            act.wait_ge(wT_ready, 1)
            sc.activation(wT[0:E, :], bank[5][0:E, 0:SEQ], ACT.Copy).then_inc(wT_saved, 1)

            for n in range(2):
                sc.activation(ysb[:, n, :], squares[:, 0:4, :], ACT.Copy, scale=0.0).then_inc(ye_saved, 1)

            def expert(t):
                act.wait_ge(s2_ready, t + 1)
                sc.activation(s2, bank[5][:, 0:SEQ], ACT.Copy).then_inc(s2_saved, 1)
                for half in range(2):
                    act.wait_ge(glu_ready, t * 2 + half + 1)
                    sc.activation(sig[:, half, :], glu[:, half, :], ACT.Sigmoid, scale=ALPHA).then_inc(esig_ready, 1)
                for half in range(2):
                    act.wait_ge(hT_ready, t * 2 + half + 1)
                    sc.activation(hT[:, half, :, :], bank[5][:, 0:256].rearrange("p (b n) -> p b n", b=2),
                                  ACT.Copy).then_inc(hT_saved, 1)
                act.wait_ge(slot_used, t * 12 + 12)
                for n in range(2):
                    sc.activation(ysb[:, n, :], bank[2 + n][:, :], ACT.Copy).then_inc(ye_saved, 1)

            with act.Fori(0, E) as t:
                expert(t)
            act.wait_ge(flag_ready, 1)
            more = act.value_load(ofl[0:1, 0:1].bitcast(I32), min_val=0, max_val=1)
            with act.If(more):
                with act.Fori(E, PASSES * E) as t:
                    expert(t)
            act.wait_ge(acc_final, 1)
            for c in range(2):
                squared(sc.activation(ysb.rearrange("p a b -> p (a b)"), acc[:, c, :], ACT.Square,
                                      accum_out=ssq[:, c:c + 1]), 13 + c + 1)

        @block.vector
        def _(dve):
            v = nc.vector
            ch = Chain(dve, dve_chain)

            def done(ins, s, val):
                ins.then_inc(s, 1)
                dve.wait_ge(s, val)

            ch.link(v.memset(half_neg[:, :], -0.5))
            ch.link(v.memset(ssq[:, :], 1.0))
            ch.link(v.memset(dts[:, :, :], 0.0))
            ch.link(v.memset(tab[NB:NB + 1, :, :], 1.0))
            ch.link(v.memset(kz[:, :, :], 0.0))
            ch.link(v.memset(vTC[:, :, :], 0.0))
            done(v.memset(pT[:, :, :], 0.0), zeros_set, 1)
            dve.wait_ge(rel_in, 32)
            done(v.tensor_copy(tab[0:NB + 1, 1, :].rearrange("p (j r h) -> p j r h", j=2, r=4),
                               tab[0:NB + 1, 0, :].rearrange("p (j h r) -> p j r h", j=2, h=2)), tab_ready, 1)

            dve.wait_ge(sq_done, 3)
            done(v.tensor_scalar(ssq[:, 0:3], ssq[:, 0:3], 1.0 / D, EPS, ALU.mult, ALU.add), ssq_ready, 1)
            dve.wait_ge(rstd_ready, 1)
            for c, r in ((0, META), (1, P), (2, P)):
                done(v.tensor_scalar(xin[0:r, c, :], xin[0:r, c, :], rstd[0:r, c:c + 1], None, ALU.mult), un_ready, c + 1)
            dve.wait_ge(vec_in, 7 * 16)
            ch.link(v.tensor_copy(sink_p[:, :].rearrange("p (j r h) -> p j r h", j=2, r=4),
                                  sink_nat[:, :].rearrange("p (j h r) -> p j r h", j=2, h=2)))

            raw, nabs, ex, tt, acc1 = (dts[:, i, :] for i in (2, 3, 4, 5, 1))
            c3 = (lambda v_: v_.rearrange("p (c h) -> p c h", c=3))
            bc = (lambda v_: v_.unsqueeze(1).to_broadcast([P, 3, SH]))
            dve.wait_ge(tile_saved, T_DTT + 1)
            ch.link(v.tensor_tensor(c3(raw), c3(raw), bc(dtb[:, :]), ALU.add))
            ch.link(v.tensor_scalar(tt, raw, -1.0, None, ALU.mult))
            done(v.tensor_tensor(nabs, raw, tt, ALU.min), nabs_ready, 1)
            ch.link(v.tensor_scalar(raw, raw, 0.0, None, ALU.max))
            dve.wait_ge(dt_exp, 1)
            ch.link(v.tensor_scalar(tt, ex, 2.0, None, ALU.add))
            ch.link(v.reciprocal(tt, tt))
            ch.link(v.tensor_tensor(ex, ex, tt, ALU.mult))
            ch.link(v.tensor_tensor(tt, ex, ex, ALU.mult))
            ch.link(v.memset(nabs, 1.0 / 17))
            for k in (15, 13, 11, 9, 7, 5, 3, 1):
                ch.link(v.tensor_tensor(nabs, nabs, tt, ALU.mult))
                ch.link(v.tensor_scalar(nabs, nabs, 1.0 / k, None, ALU.add))
            ch.link(v.tensor_tensor(nabs, nabs, ex, ALU.mult))
            ch.link(v.memset(dt, 0.0))
            for c, r in ((0, META), (1, P), (2, P)):
                s = slice(32 * c, 32 * c + 32)
                ch.link(v.scalar_tensor_tensor(dt[0:r, s], nabs[0:r, s], 2.0, raw[0:r, s], ALU.mult, ALU.add))
            dve.wait_ge(alog_exp, 1)
            done(v.scalar_tensor_tensor(c3(aa), c3(dt), -1.0, bc(dts[:, 6, 0:SH]), ALU.mult, ALU.mult), a_ready, 1)

            dve.wait_ge(toep_in, 64)

            def att_max(t):
                dve.wait_ge(qk_ready, t + 1)
                if t >= 2:
                    dve.wait_ge(pt_ready, t - 1)
                for half in range(2):
                    ins = v.scalar_tensor_tensor(logit[:, t % 2, half, :], bank[half][:, 0:LK],
                                                 HD ** -0.5, toep[:, 2 * t + half, :], ALU.mult, ALU.add)
                    done(ins, logit_done, 2 * t + half + 1)
                if t >= 1:
                    dve.wait_ge(exp_ready, t)
                mx = stats[:, 0, :].rearrange("p (h n) -> p h n", n=2)
                ch.link(v.tensor_reduce(mx[:, :, 0], logit[:, t % 2, :, 0:NT], AX, ALU.max))
                ch.link(v.tensor_reduce(mx[:, :, 1], logit[:, t % 2, :, NT:LK], AX, ALU.max))
                sk = sink_p[:, 2 * t:2 * t + 2].unsqueeze(2).to_broadcast([P, 2, 2])
                ch.link(v.tensor_tensor(mx, mx, sk, ALU.max))
                ch.link(v.tensor_tensor(stats[:, 2, :].rearrange("p (h n) -> p h n", n=2), sk, mx, ALU.subtract))
                done(v.tensor_scalar(stats[:, 1, :], stats[:, 0, :], -1.0, None, ALU.mult), max_ready, t + 1)

            def att_norm(t):
                dve.wait_ge(exp_ready, t + 1)
                ch.link(v.tensor_tensor(stats[:, 5, :], stats[:, 3, :], stats[:, 4, :], ALU.add))
                ch.link(v.reciprocal(stats[:, 5, :], stats[:, 5, :]))
                for half in range(2):
                    for n, (a, b) in enumerate(((0, NT), (NT, LK))):
                        ins = v.tensor_scalar(logit[:, t % 2, half, a:b], logit[:, t % 2, half, a:b],
                                              stats[:, 5, 2 * half + n:2 * half + n + 1], None, ALU.mult)
                        if half and n:
                            done(ins, p_ready, t + 1)
                        else:
                            ch.link(ins)

            def att_meta(t):
                dve.wait_ge(pt_ready, t + 1)
                if t >= 1:
                    dve.wait_ge(pv_ready, t)
                done(v.tensor_copy(pT[0:META, :, 384:640], bank[6][0:META, :].rearrange("p (h n) -> p h n", h=2)),
                     ptm_saved, t + 1)

            for t in range(8):
                att_max(t)
                att_norm(t)
                if t >= 1:
                    att_meta(t - 1)
            att_meta(7)

            dve.wait_ge(ya_saved, 8)
            ch.link(v.memset(xpre[:, :, 0:3], 0.0))
            ch.link(v.memset(xdec0, 0.0))
            done(v.memset(bTC[:, 0, :], 0.0), zeros_set, 2)

            def conv(i):
                ct = conv_tiles[i]
                w = (lambda k: col_cw[:, k * 24 + ct:k * 24 + ct + 1])
                dve.wait_ge(tile_saved, T_X + i + 1)
                if i >= 2:
                    dve.wait_ge(csig_ready, i - 1)
                xp, o = xpre[:, i % 2, :], cv[:, i % 2, :]
                ch.link(v.tensor_scalar(o, xp[:, 0:NT], w(0), col_cb[:, ct:ct + 1], ALU.mult, ALU.add))
                for k in (1, 2):
                    ch.link(v.scalar_tensor_tensor(o, xp[:, k:k + NT], w(k), o, ALU.mult, ALU.add))
                done(v.scalar_tensor_tensor(o, xp[:, 3:3 + NT], w(3), o, ALU.mult, ALU.add), conv_ready, i + 1)

            def silu(i):
                dve.wait_ge(csig_ready, i + 1)
                if i < 4:
                    o = bT[:, i, :]
                elif i < 8:
                    o = cT[:, i - 4, :]
                else:
                    o = xs[:, i % 3, :]
                    if i >= 11:
                        dve.wait_ge(tr_ready, i - 3 - 4 + 1)
                done(v.tensor_tensor(o, cv[:, i % 2, :], sg[:, i % 2, :], ALU.mult), xs_ready, i + 1)

            def xdecay0(g):
                dve.wait_ge(tr_saved, 4 + 4 * g + 4)
                if g:
                    dve.wait_ge(st0_ready, g)
                m = (lambda v_: v_.rearrange("p (h d) -> p h d", h=HPG))
                sc_ = (lambda v_: v_.unsqueeze(2).to_broadcast([META, HPG, HD]))
                ch.link(v.tensor_tensor(m(xdec0[0:META]), m(xm[0:META]), sc_(dt[0:META, 8 * g:8 * g + 8]), ALU.mult))
                done(v.tensor_tensor(m(xdec0[0:META]), m(xdec0[0:META]),
                                     sc_(decays[0:META, 1, 0, 8 * g:8 * g + 8]), ALU.mult), xdec0_ready, g + 1)

            dve.wait_ge(decay_ready, 1)
            for i in range(24 + 5):
                if i < 24:
                    conv(i)
                if 0 <= i - 1 < 24:
                    silu(i - 1)
                if i - 4 >= 11 and (i - 4 - 8) % 4 == 3:
                    xdecay0((i - 4 - 8) // 4)

            def ssd_au(it):
                g, c = divmod(it, 2)
                if it >= 2:
                    dve.wait_ge(seg_ready, it - 1)
                done(v.tensor_tensor(au[:, it % 2, :, :],
                                     aa[:, 32 * (c + 1) + 8 * g:32 * (c + 1) + 8 * g + 8].unsqueeze(2).to_broadcast([P, HPG, BLK]),
                                     tri_le.unsqueeze(1).to_broadcast([P, HPG, BLK]), ALU.mult), au_ready, it + 1)

            def heads(v_, h0=0):
                return v_.unsqueeze(2).to_broadcast([P, HPG, HD])

            def ssd_pre(it):
                g, c = divmod(it, 2)
                dve.wait_ge(e_ready, it + 1)
                if it >= 2:
                    dve.wait_ge(y_ready, it - 1)
                ch.link(v.tensor_tensor(cbm[:, it % 2, :], bank[4][:, 0:BLK], tri_le, ALU.mult))
                ch.link(v.tensor_tensor(em[:, it % 2, :, :], em[:, it % 2, :, :],
                                        cbm[:, it % 2, :].unsqueeze(1).to_broadcast([P, HPG, BLK]), ALU.mult))
                xg = xTC[:, c, 512 * g:512 * g + 512].rearrange("p (h d) -> p h d", h=HPG)
                s = slice(32 * (c + 1) + 8 * g, 32 * (c + 1) + 8 * g + 8)
                ins = v.tensor_tensor(xdt[:, it % 2, :, :], xg, heads(dt[:, s]), ALU.mult)
                if c == 0:
                    ch.link(ins)
                    ins = v.tensor_tensor(xdec, xdt[:, it % 2, :, :], heads(decays[:, 1, 1, 8 * g:8 * g + 8]), ALU.mult)
                done(ins, m_ready, it + 1)

            def ssd_post(it):
                g, c = divmod(it, 2)
                dve.wait_ge(y_ready, it + 1)
                ys = ysum
                ch.link(v.tensor_tensor(ys, bank[6][:, :].rearrange("p (h d) -> p h d", h=HPG),
                                        heads(decays[:, 0, c + 1, 8 * g:8 * g + 8]), ALU.mult))
                yv = ys.rearrange("p (q i) d -> p q i d", i=2)
                for i in range(2):
                    for j in range(2):
                        src = bank[2 + j][:, :].rearrange("p (q i o d) -> p q i o d", q=2, i=2, o=2)[:, :, i, i, :]
                        ch.link(v.tensor_tensor(yv[:, 2 * j:2 * j + 2, i, :], yv[:, 2 * j:2 * j + 2, i, :], src, ALU.add))
                xg = xTC[:, c, 512 * g:512 * g + 512].rearrange("p (h d) -> p h d", h=HPG)
                ch.link(v.tensor_tensor(xg, xg, heads(dskip[:, 8 * g:8 * g + 8]), ALU.mult))
                ch.link(v.tensor_tensor(ys, ys, xg, ALU.add))
                zz = zy[:, c, 512 * g:512 * g + 512].rearrange("p (h d) -> p h d", h=HPG)
                if c == 0:
                    hg = hst[:, g, :].rearrange("p (h d) -> p h d", h=HPG)
                    ch.link(v.tensor_tensor(hg, hg, heads(decays[:, 2, 1, 8 * g:8 * g + 8]), ALU.mult))
                    ch.link(v.tensor_tensor(hg, hg, bank[7][:, :].rearrange("p (h d) -> p h d", h=HPG), ALU.add))
                dve.wait_ge(z_saved, it + 1)
                ch.link(v.tensor_tensor(ys, ys, ztmp[:, it % 2, :].rearrange("p (h d) -> p h d", h=HPG), ALU.mult))
                done(v.tensor_tensor(zz, zz, ys, ALU.mult), y_done, it + 1)

            ssd_au(0)
            ssd_au(1)
            ssd_pre(0)
            for it in range(8):
                if it + 2 < 8:
                    ssd_au(it + 2)
                ssd_post(it)
                if it + 1 < 8:
                    ssd_pre(it + 1)
            dve.wait_ge(sq_done, 11)
            done(v.tensor_scalar(ssq[:, :], ssq[:, :], float(G) / DI, EPS, ALU.mult, ALU.add), ssq_ready, 2)
            dve.wait_ge(rstd_ready, 2)
            for it in range(8):
                g, c = divmod(it, 2)
                zz = zy[:, c, 512 * g:512 * g + 512]
                done(v.tensor_scalar(zz, zz, rstd[:, it:it + 1], None, ALU.mult), yn_ready, it + 1)

            dve.wait_ge(gsig_ready, 8)
            for d in range(8):
                dve.wait_ge(branch_ready, d + 1)
                ch.link(v.tensor_tensor(gmul[:, d % 2, :], gsig[:, d, :], bank[d % 4][:, :], ALU.mult))
                done(v.tensor_tensor(mT[:, d, :], gmul[:, d % 2, 0:256], gmul[:, d % 2, 256:512], ALU.add), m_done, d + 1)
                if d == 1:
                    dve.wait_ge(b1_in, 16)
                    ch.link(v.tensor_copy(b1all[0:E, :], b1raw[0:E, :]))
                    ch.link(v.tensor_tensor(b1raw[0:E, :], b1raw[0:E, :], b1all[0:E, :], ALU.subtract))
                    ch.link(v.tensor_copy(b1mid[0:E, :], b1raw[0:E, :]))
                    ch.link(v.tensor_tensor(b1raw[0:E, :], b1raw[0:E, :], b1mid[0:E, :], ALU.subtract))
                    done(v.tensor_copy(b1lo[0:E, :], b1raw[0:E, :]), b1_ready, 1)

            dve.wait_ge(xres_in, 16)
            for c in range(2):
                dve.wait_ge(h_ready, c + 1)
                for n in range(2):
                    done(v.tensor_tensor(acc[:, c, 512 * n:512 * n + 512], bank[2 * c + n][:, :],
                                         xres[:, c, 512 * n:512 * n + 512], ALU.add), h_done, 2 * c + n + 1)
                dve.wait_ge(sq_done, 12 + c)
                done(v.tensor_scalar(ssq[:, c:c + 1], ssq[:, c:c + 1], 1.0 / D, EPS, ALU.mult, ALU.add), ssq_ready, 3 + c)
                dve.wait_ge(rstd_ready, 3 + c)
                done(v.tensor_scalar(un[:, c, :], acc[:, c, :], rstd[:, c:c + 1], None, ALU.mult), un_ready, 4 + c)
                ch.link(v.tensor_copy(upart[:, 0, c, :], un[:, c, :]))
                ch.link(v.tensor_tensor(ures[:, c, :], un[:, c, :], upart[:, 0, c, :], ALU.subtract))
                ch.link(v.tensor_copy(upart[:, 1, c, :], ures[:, c, :]))
                ch.link(v.tensor_tensor(ures[:, c, :], ures[:, c, :], upart[:, 1, c, :], ALU.subtract))
                ch.link(v.tensor_copy(upart[:, 2, c, :], ures[:, c, :]))

            ch.link(v.tensor_tensor(tri_lt_b, tri_le, ident, ALU.subtract))
            ch.link(v.tensor_copy(ones_b, ones))
            ch.link(v.memset(pos, -1.0))
            ch.link(v.memset(wtok, 0.0))
            ch.link(v.memset(ident3, 0.0))
            for i in range(3):
                ch.link(v.tensor_copy(ident3[E * i:E * i + E, 0:E], ident[E * i:E * i + E, E * i:E * i + E]))
            dve.wait_ge(lg_ready, 1)
            lg, mk = rt[:, 0:2, 0:E], rt[:, 4:6, 0:E]
            oh, woh = (rt[:, r0:r0 + 4, :].rearrange("p r q -> p (r q)").rearrange("p (c k e) -> p c k e", c=2, k=4)
                       for r0 in (8, 12))
            ch.link(v.tensor_tensor(lg, bank[4][:, 0:64].rearrange("p (c e) -> p c e", c=2),
                                    brt[:, :].unsqueeze(1).to_broadcast([P, 2, E]), ALU.add))
            for c in range(2):
                ch.link(v.max(topv[:, c, :], lg[:, c, :]))
                ch.link(v.max_index(topi[:, c, :], topv[:, c, :], lg[:, c, :]))
                ch.link(v.tensor_copy(topf[:, c, :], topi[:, c, :]))
            done(v.tensor_scalar(negm, topv[:, :, 0:1], -1.0, None, ALU.mult), topexp_in, 1)
            for c in range(2):
                ch.link(v.tensor_tensor(oh[:, c, :, :], iota2[:, 0:E].unsqueeze(1).to_broadcast([P, 4, E]),
                                        topf[:, c, 0:4].unsqueeze(2).to_broadcast([P, 4, E]), ALU.is_equal))
                ch.link(v.tensor_reduce(mk[:, c, :], oh[:, c, :, :].rearrange("p k e -> p e k"), AX, ALU.add))
            done(v.tensor_copy(maskb, mk), mask_ready, 1)
            dve.wait_ge(topexp_ready, 1)
            ch.link(v.reciprocal(wsum, wsum))
            ch.link(v.tensor_tensor(tope[:, :, 0:4], tope[:, :, 0:4], wsum.to_broadcast([P, 2, 4]), ALU.mult))
            for c in range(2):
                ch.link(v.tensor_tensor(woh[:, c, :, :], oh[:, c, :, :],
                                        tope[:, c, 0:4].unsqueeze(2).to_broadcast([P, 4, E]), ALU.mult))
                done(v.tensor_reduce(wtok[:, c, 0:E], woh[:, c, :, :].rearrange("p k e -> p e k"), AX, ALU.add),
                     wtok_ready, c + 1)
            dve.wait_ge(rank_ready, 1)
            ps = pos[:, :, 0:E]
            ch.link(v.scalar_tensor_tensor(ps, bank[6][:, 0:64].rearrange("p (c e) -> p c e", c=2), 1.0, mk,
                                           ALU.add, ALU.mult))
            ch.link(v.tensor_scalar(ps, ps, -1.0, None, ALU.add))
            ch.link(v.tensor_reduce(ofl[:, 1:2], bank[6][:, 64:96], AX, ALU.max))
            done(v.tensor_scalar(ofl[:, 0:1].bitcast(I32), ofl[:, 1:2], float(CAP), None, ALU.is_gt), flag_ready, 1)
            done(v.memset(s2, 0.0), sc_added, 1)
            done(v.memset(ofl[:, 2:3], 0.0), route_done, 1)

            def routing(col, val):
                for c in range(2):
                    ch.link(v.tensor_scalar(gsel[:, c, :], iota2[:, 0:CAP], pos[:, c, bass.ds(col, 1)], None, ALU.is_equal))
                    ch.link(v.tensor_scalar(gwt[:, c, :], iota2, pos[:, c, bass.ds(col, 1)], wtok[:, c, bass.ds(col, 1)],
                                            ALU.is_equal, ALU.mult))
                done(v.tensor_copy(bsel[0:3 * E, :], ident3[0:3 * E, bass.ds(col, 1)].to_broadcast([3 * E, CAP])),
                     g_ready, val)

            def scatter_add(s):
                for i in range(4):
                    c, n = divmod(i, 2)
                    dve.wait_ge(sc_ready, s * 4 + (i + 1))
                    a = acc[:, c, 512 * n:512 * n + 512]
                    done(v.tensor_tensor(a, a, bank[6 + n][:, :], ALU.add), sc_added, s * 4 + (i + 2))

            def expert(t, e, b, extra):
                dve.wait_ge(gat_ready, t + 1)
                done(v.tensor_tensor(usel, bank[4][:, :].rearrange("p (k s) -> p k s", k=KT),
                                     col_gffn.unsqueeze(2).to_broadcast([P, KT, CAP]), ALU.mult), usel_ready, t + 1)
                scatter_add(t + extra)
                dve.wait_ge(s2_ready, t + 1)
                routing(e + 1, t + b + 2)
                for half in range(2):
                    dve.wait_ge(slot_used, t * 12 + (4 * half + 4))
                    hv = bank[half][:, :].rearrange("p (f two) -> p f two", two=2)
                    done(v.tensor_scalar(glu[:, half, :], hv[:, :, 0], LIMIT, None, ALU.min), glu_ready, t * 2 + half + 1)
                    ch.link(v.tensor_scalar(lin[:, half, :], hv[:, :, 1], -LIMIT, LIMIT, ALU.max, ALU.min))
                    ch.link(v.scalar_tensor_tensor(lin[:, half, :], lin[:, half, :], 1.0, glu[:, half, :], ALU.add, ALU.mult))
                    dve.wait_ge(esig_ready, t * 2 + half + 1)
                    done(v.tensor_tensor(hsw[:, half, :], lin[:, half, :], sig[:, half, :], ALU.mult), hs_ready, t * 2 + half + 1)

            PER = 4 + 4
            routing(0, 1)
            base = ch.n
            with dve.Fori(0, E) as t:
                ch.base, ch.n = t * PER + base, 0
                expert(t, t, 0, 0)
                assert ch.n == PER
            ch.base, ch.n = 0, base + E * PER
            dve.wait_ge(b2_ready, 1)
            for c in range(2):
                for n in range(2):
                    ch.link(v.tensor_tensor(acc[:, c, 512 * n:512 * n + 512], acc[:, c, 512 * n:512 * n + 512],
                                            b2_bank(c, n)[:, :], ALU.add))
            scatter_add(E)
            more = dve.value_load(ofl[0:1, 0:1].bitcast(I32), min_val=0, max_val=1)
            with dve.If(more):
                after = ch.n
                EXTRA = 1 + 4
                ch.link(v.memset(s2, 0.0))
                with dve.Fori(1, PASSES) as b:
                    ch.base, ch.n = b * (EXTRA + E * PER) + (after + 1 - (EXTRA + E * PER)), 0
                    ch.link(v.tensor_scalar(pos, pos, -float(CAP), None, ALU.add))
                    routing(0, b * (E + 1) + 1)
                    assert ch.n == EXTRA
                    v.memset(ofl[:, 3:4], 0.0)
                    with dve.Fori(0, E) as e:
                        ch.base = b * (EXTRA + E * PER) + (e * PER + (after + 1 - E * PER))
                        ch.n = 0
                        expert(b * E + e, e, b, 1)
                dve.wait_ge(sc_ready, 4 * PASSES * E + 4)
                scatter_add(PASSES * E + 1)
            tail = Chain(dve, tail_chain)
            done(v.memset(ofl[:, 2:3], 0.0), acc_final, 1)
            dve.wait_ge(sq_done, 15)
            done(v.tensor_scalar(ssq[:, 0:2], ssq[:, 0:2], 1.0 / D, EPS, ALU.mult, ALU.add), ssq_ready, 5)
            dve.wait_ge(gfin_in, 16)
            dve.wait_ge(rstd_ready, 5)
            for c in range(2):
                done(v.scalar_tensor_tensor(un[:, c, :], acc[:, c, :], rstd[:, c:c + 1], gfin, ALU.mult, ALU.mult),
                     fin_ready, c + 1)

        @block.tensor
        def _(pe):
            tn = nc.tensor

            def mm(o, lhsT, rhs, first, last):
                return tn.matmul(o, lhsT, rhs, start=first, stop=last, skip_group_check=True)

            pe.wait_ge(const_in, 16)
            pe.wait_ge(row_in, 5 * 16)
            tn.transpose(bank[4][:, 0:120], rows[0:120, 0, :], ident[0:120, 0:120])
            tn.transpose(bank[4][:, 128:160], rows[0:32, 1, :], ident[0:32, 0:32]).then_inc(rows_T, 1)
            pe.wait_ge(tab_ready, 1)
            mm(bank[5][0:HEADS, 0:VL], tab[0:NB + 1, 1, :], ohs[0:NB + 1, 0, :], True, True)
            mm(bank[6][0:HEADS, 0:VL], tab[0:NB + 1, 1, :], ohs[0:NB + 1, 1, :], True, True).then_inc(avec_ready, 1)

            def tile(p):
                if p >= 4:
                    pe.wait_ge(tile_saved, p - 3)
                return bank[p % 4]

            def ready(ins):
                ins.then_inc(tile_ready, 1)

            spans = ((0, META), (META, META + BLK), (META + BLK, NT))
            pe.wait_ge(un_ready, 3)
            for k in range(KT):
                b = tile(T_U + k)
                for c, (t0, t1) in enumerate(spans):
                    ins = tn.transpose(b[:, t0:t1], xin[0:t1 - t0, c, k * P:(k + 1) * P], ident[0:t1 - t0, 0:t1 - t0])
                ready(ins)

            def project(p, n, w, cols_n):
                b = tile(p)
                arrived(pe, n)
                for k in range(KT):
                    ins = mm(b[:, 0:cols_n], w(k), uT[:, k, NT - cols_n:NT], k == 0, k == KT - 1)
                ready(ins)

            pe.wait_ge(tile_saved, T_U + 8)
            for j in range(2):
                wk = slot_view(ck % FSLOTS, KT, 256)
                project(T_K + j, ck, lambda k, j=j, wk=wk: wk[:, k, P * j:P * j + P], NT)
            wv = slot_view(cvv % FSLOTS, KT, 256)
            for c, (t0, t1) in enumerate(spans):
                b = tile(T_V + c)
                arrived(pe, cvv)
                for k in range(KT):
                    ins = mm(b[0:t1 - t0, 0:256], uT[:, k, t0:t1], wv[:, k, :], k == 0, k == KT - 1)
                ready(ins)
            b = tile(T_DT)
            pe.wait_ge(vec_in, 7 * 16)
            for k in range(KT):
                ins = mm(b[0:SH, 0:NT], wdt[:, k, :], uT[:, k, :], k == 0, k == KT - 1)
            ready(ins)
            for i in range(8):
                n = cq[i // 2]
                wq = slot_view(n % FSLOTS, KT, 2, 128)
                r = i % 2
                project(T_Q[i], n, lambda k, wq=wq, r=r: wq[:, k, r, :], SEQ)
                if i == 0:
                    b = tile(T_DTT)
                    pe.wait_ge(tile_saved, T_DT + 1)
                    for c, (t0, t1) in enumerate(spans):
                        ins = tn.transpose(b[0:t1 - t0, SH * c:SH * c + SH], dtT[0:SH, t0:t1], ident[0:SH, 0:SH])
                    ready(ins)

            pe.wait_ge(avec_saved, 1)
            pe.wait_ge(tile_saved, T_X)

            def att_qk(t):
                if t >= 1:
                    pe.wait_ge(logit_done, 2 * t)
                for half in range(2):
                    b, kk = bank[half], kz[:, 2 * (t // 4) + half, :]
                    mm(b[:, 0:NT], qT[:, t, BLK:SEQ], kk[:, 0:NT], True, True)
                    ins = mm(b[:, NT:LK], qT[:, t, 0:BLK], kk[:, 0:META + BLK], True, True)
                ins.then_inc(qk_ready, 1)

            def att_transpose(t):
                pe.wait_ge(p_ready, t + 1)
                if t >= 1:
                    pe.wait_ge(ptb_saved, t)
                    pe.wait_ge(ptm_saved, t)
                for half in range(2):
                    pr = logit[:, t % 2, half, :]
                    for i, k0 in enumerate((NT + META, META, META + BLK)):
                        tn.transpose(bank[4 + half][:, i * P:(i + 1) * P], pr[:, k0:k0 + P], ident)
                    for i, k0 in enumerate((NT, 0)):
                        ins = tn.transpose(bank[6][0:META, 256 * half + P * i:256 * half + P * i + P],
                                           pr[:, k0:k0 + META], ident)
                ins.then_inc(pt_ready, 1)

            def att_pv(t):
                pe.wait_ge(ptb_saved, t + 1)
                pe.wait_ge(ptm_saved, t + 1)
                if t >= 1:
                    pe.wait_ge(ya_saved, t)
                for half in range(2):
                    h = 2 * (t // 4) + half
                    o, vv = bank[7][64 * half:64 * half + 64, :], vTC[:, :, HD * h:HD * h + HD]
                    mm(o[:, 0:SEQ], vv[:, 0, :], pT[:, half, 384:640], True, False)
                    mm(o[:, 0:SEQ], vv[:, 1, :], pT[:, half, 0:256], False, False)
                    ins = mm(o[:, BLK:SEQ], vv[:, 2, :], pT[:, half, 256:384], False, True)
                ins.then_inc(pv_ready, 1)

            def gate_half(h):
                d, gi = divmod(h, 2)
                n = cg[d // 2][gi]
                if gi == 0 and d >= 2:
                    pe.wait_ge(gate_saved, d - 1)
                arrived(pe, n)
                wg = slot_view(n % FSLOTS, KT, 256)
                for k in range(KT):
                    ins = mm(bank[2 + d % 2][:, 256 * gi:256 * gi + 256], wg[:, k, P * (d % 2):P * (d % 2) + P],
                             uT[:, k, META:NT], k == 0, k == KT - 1)
                if gi:
                    ins.then_inc(gate_ready, 1)

            att_qk(0)
            half_units = iter(range(16))
            for _ in range(GATE_FIRST):
                gate_half(next(half_units))
            pe.wait_ge(a_ready, 1)
            for i, m in enumerate((tri_le, tri_gt, ones)):
                ins = mm(bank[7][:, 96 * i:96 * i + 96], m, aa, True, True)
            ins.then_inc(cum_ready, 1)
            pe.wait_ge(decay_ready, 1)
            for t in range(8):
                if t + 1 < 8:
                    att_qk(t + 1)
                for _ in range(gate_before[t]):
                    gate_half(next(half_units))
                att_transpose(t)
                gate_half(next(half_units))
                att_pv(t)

            pe.wait_ge(ya_saved, 8)
            pe.wait_ge(gate_saved, 8)
            pe.wait_ge(zeros_set, 2)

            def conv_transposes(i):
                if 4 <= i < 8:
                    return
                n = i if i < 4 else i - 4
                pe.wait_ge(xs_ready, i + 1)
                if n >= 2:
                    pe.wait_ge(tr_saved, n - 1)
                src = bT[:, i, :] if i < 4 else xs[:, i % 3, :]
                b = bank[4 + n % 2]
                tn.transpose(b[0:META, 0:P], src[:, 0:META], ident)
                ins = tn.transpose(b[:, P:2 * P], src[:, META:META + BLK], ident)
                if i >= 8:
                    ins = tn.transpose(b[:, 2 * P:3 * P], src[:, META + BLK:NT], ident)
                ins.then_inc(tr_ready, 1)

            def state0(g):
                pe.wait_ge(xdec0_ready, g + 1)
                if g:
                    pe.wait_ge(st0_saved, g)
                mm(bank[6][:, :], bTC[:, 0, P * g:P * g + P], xdec0, True, True).then_inc(st0_ready, 1)

            def z_tile(it):
                g, c = divmod(it, 2)
                t0 = META + BLK * c
                if it >= 1:
                    pe.wait_ge(z_saved, it)
                for h in range(2):
                    wz = slot_view(cz[g][h] % FSLOTS, 4, 512)
                    arrived(pe, cz[g][h])
                    for k in range(4):
                        kk = 4 * h + k
                        ins = mm(z_bank(it)[:, :], uT[:, kk, t0:t0 + BLK], wz[:, k, :], kk == 0, kk == KT - 1)
                ins.then_inc(z_ready, 1)

            for i in range(24 + 5):
                if i == 24:
                    z_tile(0)
                if i < 24:
                    n = cx[i // 2]
                    wx = slot_view(n % FSLOTS, KT, 256)
                    project(T_X + i, n, lambda k, wx=wx, i=i: wx[:, k, P * (i % 2):P * (i % 2) + P], NT)
                if 0 <= i - 2 < 24:
                    conv_transposes(i - 2)
                if i - 5 >= 11 and (i - 5 - 8) % 4 == 3:
                    state0((i - 5 - 8) // 4)

            pe.wait_ge(tile_saved, T_Y)
            pe.wait_ge(tr_saved, 20)
            pe.wait_ge(st0_saved, 4)
            pe.wait_ge(z_saved, 1)

            def ssd_seg(it):
                g, c = divmod(it, 2)
                t0 = META + BLK * c
                pe.wait_ge(au_ready, it + 1)
                if it >= 1:
                    pe.wait_ge(e_ready, it)
                    pe.wait_ge(m_ready, it)
                mm(bank[4][:, 0:BLK], bT[:, g, t0:t0 + BLK], cT[:, g, t0:t0 + BLK], True, True)
                for j in range(2):
                    ins = mm(bank[j][:, :], tri_gt, au[:, it % 2, 4 * j:4 * j + 4, :], True, True)
                ins.then_inc(seg_ready, 1)

            def ssd_y(it):
                g, c = divmod(it, 2)
                t0 = META + BLK * c
                pe.wait_ge(m_ready, it + 1)
                if it >= 1:
                    pe.wait_ge(y_done, it)
                mm(bank[6][:, :], cT[:, g, t0:t0 + BLK], hst[:, g, :], True, True)
                for h in range(HPG):
                    q = h // 2
                    ins = mm(bank[2 + h // 4][:, P * (h % 4):P * (h % 4) + P], em[:, it % 2, h, :],
                             xdt[:, it % 2, 2 * q:2 * q + 2, :], True, True)
                if c == 0:
                    ins = mm(bank[7][:, :], bTC[:, 1, P * g:P * g + P], xdec, True, True)
                ins.then_inc(y_ready, 1)

            ssd_seg(0)
            for it in range(8):
                ssd_y(it)
                if it + 1 < 8:
                    ssd_seg(it + 1)
                    z_tile(it + 1)

            def branch(dp, bi):
                n = (ca[dp], *cs[dp])[bi]
                arrived(pe, n)
                wb = slot_view(n % FSLOTS, KT, 256)
                c0 = 0 if bi == 0 else 256
                for d in (2 * dp, 2 * dp + 1):
                    if bi == 0 and d >= 4:
                        pe.wait_ge(m_done, d - 3)
                    for k in range(KT):
                        rhs = yaT[:, k, :] if bi == 0 else yT[:, 8 * (bi - 1) + k, :]
                        ins = mm(bank[d % 4][:, c0:c0 + 256], wb[:, k, P * (d % 2):P * (d % 2) + P], rhs,
                                 k == 0 and bi < 2, k == KT - 1 and bi != 1)
                    if bi == 2:
                        ins.then_inc(branch_ready, 1)

            pe.wait_ge(e_ready, 8)
            branch(0, 0)
            pe.wait_ge(y_done, 8)
            branch(1, 0)
            pe.wait_ge(yn_ready, 8)
            for i in range(16):
                if i >= 4:
                    pe.wait_ge(tile_saved, T_Y + i - 3)
                b = bank[4 + i % 4]
                for c in range(2):
                    ins = tn.transpose(b[:, P * c:P * c + P], zy[:, c, P * i:P * i + P], ident)
                ready(ins)
            pe.wait_ge(tile_saved, T_END)
            for dp in range(4):
                for bi in range(3):
                    if bi or dp >= 2:
                        branch(dp, bi)

            pe.wait_ge(m_done, 8)
            for c in range(2):
                for i in range(4):
                    arrived(pe, co[i])
                    wo = slot_view(co[i] % FSLOTS, 2, 1024)
                    for k in range(2):
                        for n in range(2):
                            ins = mm(bank[2 * c + n][:, :], mT[:, 2 * i + k, BLK * c:BLK * c + BLK],
                                     wo[:, k, 512 * n:512 * n + 512], i == 0 and k == 0, i == 3 and k == 1)
                ins.then_inc(h_ready, 1)

            pe.wait_ge(un_ready, 4)
            for k in range(4):
                tn.transpose(bank[4 + k][:, 0:P], un[:, 0, P * k:P * k + P], ident)
            pe.wait_ge(un_ready, 5)
            for k in range(KT):
                if k >= 4:
                    pe.wait_ge(tile_saved, T_END + k - 3)
                for c in range(2):
                    if k >= 4 or c:
                        ins = tn.transpose(bank[4 + k % 4][:, P * c:P * c + P], un[:, c, P * k:P * k + P], ident)
                ready(ins)
            pe.wait_ge(tile_saved, T_END + KT)
            for c in range(2):
                for k in range(KT):
                    ins = mm(bank[4][:, E * c:E * c + E], u2T[:, k, P * c:P * c + P], wrt[:, k, :], k == 0, k == KT - 1)
            ins.then_inc(lg_ready, 1)
            pe.wait_ge(mask_ready, 1)
            mm(bank[6][:, 0:E], tri_lt_b, maskb[:, 0, :], True, True)
            mm(bank[6][:, E:2 * E], ones_b, maskb[:, 0, :], True, False)
            mm(bank[6][:, E:2 * E], tri_lt_b, maskb[:, 1, :], False, True)
            mm(bank[6][:, 2 * E:3 * E], ones_b, maskb[:, 0, :], True, False)
            mm(bank[6][:, 2 * E:3 * E], ones_b, maskb[:, 1, :], False, True).then_inc(rank_ready, 1)
            pe.wait_ge(wtok_ready, 2)
            for c in range(2):
                ins = tn.transpose(bank[5][0:E, P * c:P * c + P], wtok[:, c, 0:E], ident)
            ins.then_inc(wT_ready, 1)

            def scatter(s):
                for i in range(4):
                    c, n = divmod(i, 2)
                    if i < 2:
                        pe.wait_ge(sc_added, s * 4 + 1)
                    else:
                        pe.wait_ge(sc_added, s * 4 + i)
                    mm(bank[6 + n][:, :], s2[:, P * c:P * c + P], ysb[:, n, :], True, True).then_inc(sc_ready, 1)

            def expert(t, b, extra):
                pe.wait_ge(g_ready, t + b + 1)
                for k in range(KT):
                    for part in range(3):
                        for c in range(2):
                            ins = mm(bank[4][:, CAP * k:CAP * k + CAP], upart[:, part, c, P * k:P * k + P],
                                     gsel[:, c, :], part == 0 and c == 0, part == 2 and c == 1)
                ins.then_inc(gat_ready, 1)
                for half in range(2):
                    for c in range(2):
                        c0 = 1024 * half + 512 * c
                        mm(bank[half][64 * c:64 * c + 64, :], bsel[0:3 * E, :], b1all[0:3 * E, c0:c0 + 512], True, False)
                pe.wait_ge(ye_saved, t * 2 + 2)
                scatter(t + extra)
                for c in range(2):
                    ins = tn.transpose(bank[5][:, P * c:P * c + P], gwt[:, c, :], ident)
                ins.then_inc(s2_ready, 1)
                pe.wait_ge(usel_ready, t + 1)
                for half in range(2):
                    for s_ in range(4):
                        i = 4 * half + s_
                        expert_arrived(pe, i, t)
                        w = slot_view(slot_of(i), 2, 1024)
                        for kk in range(2):
                            for c in range(2):
                                k = 2 * s_ + kk
                                ins = mm(bank[half][64 * c:64 * c + 64, :], usel[:, k, :],
                                         w[:, kk, 512 * c:512 * c + 512], False, k == KT - 1)
                        ins.then_inc(slot_used, 1)
                pe.wait_ge(s2_saved, t + 1)
                for half in range(2):
                    pe.wait_ge(hs_ready, t * 2 + half + 1)
                    if half:
                        pe.wait_ge(hT_saved, t * 2 + 1)
                    for q in range(2):
                        ins = tn.transpose(bank[5][:, P * q:P * q + P], hsw[:, half, P * q:P * q + P], ident)
                    ins.then_inc(hT_ready, 1)
                    pe.wait_ge(hT_saved, t * 2 + half + 1)
                    for q in range(2):
                        i = 8 + 2 * half + q
                        expert_arrived(pe, i, t)
                        w = slot_view(slot_of(i), 2, 1024)
                        for n in range(2):
                            for c in range(2):
                                ins = mm(bank[2 + n][64 * c:64 * c + 64, :], hT[:, half, q, 64 * c:64 * c + 64],
                                         w[:, c, 512 * n:512 * n + 512], half == 0 and q == 0, half == 1 and q == 1)
                        ins.then_inc(slot_used, 1)

            pe.wait_ge(route_done, 1)
            pe.wait_ge(wT_saved, 1)
            pe.wait_ge(b1_spread, 32)
            with pe.Fori(0, E) as t:
                expert(t, 0, 0)
            pe.wait_ge(b2_in, 16)
            for c in range(2):
                for n in range(2):
                    ins = mm(b2_bank(c, n)[:, :], wT[:, P * c:P * c + P], b2sb[:, 512 * n:512 * n + 512], True, True)
            ins.then_inc(b2_ready, 1)
            pe.wait_ge(ye_saved, 2 * E + 2)
            scatter(E)
            more = pe.value_load(ofl[0:1, 0:1].bitcast(I32), min_val=0, max_val=1)
            with pe.If(more):
                with pe.Fori(1, PASSES) as b:
                    with pe.Fori(0, E) as e:
                        expert(b * E + e, b, 1)
                pe.wait_ge(ye_saved, 2 * PASSES * E + 2)
                scatter(PASSES * E + 1)


def kernel(**inputs):
    import concourse.bacc as bacc
    from concourse.bass_utils import run_bass_kernel_spmd

    flat = {
        "x": inputs["x"].reshape(SEQ, D), "meta": inputs["meta_tokens"], "rel": inputs["rel_bias"],
        "g_mix": inputs["norm_mix_g"].reshape(D), "w_in": inputs["w_in"][0], "sinks": inputs["attn_sinks"].reshape(-1),
        "conv_w": inputs["conv_w"][0], "conv_b": inputs["conv_b"].reshape(-1), "dt_bias": inputs["dt_bias"].reshape(-1),
        "a_log": inputs["a_log"].reshape(-1), "d_skip": inputs["d_skip"].reshape(-1),
        "g_ssm": inputs["ssm_norm_g"].reshape(-1), "w_att": inputs["w_attn_br"][0], "w_ssm": inputs["w_ssm_br"][0],
        "w_out": inputs["w_out"][0], "g_ffn": inputs["norm_ffn_g"].reshape(-1), "w_rt": inputs["w_router"][0],
        "b_rt": inputs["b_router"].reshape(-1), "w1": inputs["w_exp_in"][0], "b1": inputs["b_exp_in"][0],
        "w2": inputs["w_exp_out"][0], "b2": inputs["b_exp_out"][0], "g_fin": inputs["norm_final_g"],
    }
    i = np.arange(P)
    squares = np.stack([i[:, None] == i[None, :], i[:, None] <= i[None, :], i[:, None] > i[None, :],
                        np.ones((P, P)), np.broadcast_to(i % CAP, (P, P))], axis=1).astype(np.float32)
    flat["c_sq"] = squares
    flat["c_oh"] = distance_one_hots()
    nc = bacc.Bacc("TRN2", target_bir_lowering=False, num_devices=1)
    arrays, args = {}, {}
    for name, a in flat.items():
        a = np.ascontiguousarray(a)
        arrays["in_" + name] = a
        args[name] = nc.dram_tensor("in_" + name, a.shape, mybir.dt.from_np(a.dtype), kind="ExternalInput").ap()
    args["out"] = nc.dram_tensor("out_0", (SEQ, D), F32, kind="ExternalOutput").ap()
    hybrid_layer(nc, **args)
    r = run_bass_kernel_spmd(nc, [arrays], core_ids=[0])
    return r.results[0]["out_0"].reshape(1, SEQ, D)
```

```python
import math
from contextlib import ExitStack

import numpy as np

import concourse.bass as bass
from concourse import mybir

F32 = mybir.dt.float32
BF16 = mybir.dt.bfloat16
U32 = mybir.dt.uint32
I32 = mybir.dt.int32
ALU = mybir.AluOpType
ACT = mybir.ActivationFunctionType
AX = mybir.AxisListType.X

P = 128
D = 1024
KT = D // P
META = 16
SEQ = 256
NT = META + SEQ
BLK = 128
HEADS, KV, HD = 16, 4, 64
NB, MAXD, WINDOW = 32, 128, 128
DI = 2048
SH = 32
G = 4
HPG = SH // G
NS = 128
CW = 4
E = 32
FF = 1024
CAP = 64
PASSES = SEQ // CAP
EPS = 1e-5
ALPHA, LIMIT = 1.702, 7.0
COL_Q, COL_K, COL_V, COL_Z = 0, 1024, 1280, 1536
COL_X = COL_Z + DI
COL_B = COL_X + DI
COL_C = COL_B + G * NS
COL_DT = COL_C + G * NS
COL_G = COL_DT + SH
SLOTS = 12
SLOT = 2048
FSLOTS = 7
NEG = -1e30
VL = 400
LK = NT + META + BLK


def distance_one_hots():
    x = np.arange(VL)
    dist = NT - 1 - x
    n = np.maximum(dist, 0)
    exact = NB // 2
    nf = np.maximum(n, 1).astype(np.float32)
    large = exact + (np.log(nf / np.float32(exact)) / np.float32(math.log(MAXD / exact))
                     * np.float32(NB - exact)).astype(np.int32)
    bucket = np.where(n < exact, n, np.minimum(large, NB - 1))
    oh = np.zeros((NB + 1, 2, VL), np.float32)
    oh[bucket, :, x] = 1.0
    oh[NB, 1, :] = np.where((dist >= 0) & (dist < WINDOW), 0.0, NEG)
    return oh


class Chain:

    def __init__(self, eng, sem, base=0):
        self.eng, self.sem, self.base, self.n = eng, sem, base, 0

    def link(self, ins):
        self.n += 1
        ins.then_inc(self.sem, 1)
        self.eng.wait_ge(self.sem, self.base + self.n)


def hybrid_layer(nc, x, meta, rel, g_mix, w_in, sinks, conv_w, conv_b, dt_bias, a_log, d_skip, g_ssm,
                 w_att, w_ssm, w_out, g_ffn, w_rt, b_rt, w1, b1, w2, b2, g_fin, c_sq, c_oh, out):
    ctx = ExitStack()
    with ctx:
        def sb(name, shape, dt=F32):
            return ctx.enter_context(nc.sbuf_tensor(name, shape, dt))

        def sem(name):
            return ctx.enter_context(nc.semaphore(name))

        ring = sb("ring", [P, SLOTS, SLOT])
        squares = sb("squares", [P, 5, P])
        ident, tri_le, tri_gt, ones, iota2 = (squares[:, i, :] for i in range(5))
        wdt = sb("wdt", [P, KT, SH])
        wrt = sb("wrt", [P, KT, E])
        rows = sb("rows", [P, 2, P])
        cols = sb("cols", [P, 152])
        col_cw, col_cb = cols[:, 0:96], cols[:, 96:120]
        col_gmix, col_gffn, col_gssm = cols[:, 120:128], cols[:, 128:136], cols[:, 136:152]
        dtb, alog, dskip, brt = (sb(n, [P, 32]) for n in ("dtb", "alog", "dskip", "brt"))
        sink_nat, sink_p = sb("sink_nat", [P, HEADS]), sb("sink_p", [P, HEADS])
        half_neg = sb("half_neg", [P, 8])
        ssq, rstd = sb("ssq", [P, 8]), sb("rstd", [P, 8])
        dts = sb("dts", [P, 7, 96])
        dt, aa = dts[:, 0, :], dts[:, 1, :]
        decays = sb("decays", [P, 3, 3, SH])
        stats = sb("stats", [P, 6, 4])
        tab = sb("tab", [NB + 1, 2, HEADS])
        arena = sb("arena", [P, 25024])

        def at(off, *shape, dt=F32):
            n = int(np.prod(shape))
            words = n if dt != BF16 else n // 2
            v = arena[:, off:off + words]
            if dt != F32:
                v = v.bitcast(dt)
            if len(shape) == 1:
                return v
            names = "abcd"[:len(shape)]
            return v.rearrange(f"p ({' '.join(names)}) -> p {' '.join(names)}",
                               **{names[i]: shape[i] for i in range(len(shape))})

        uT = at(0, KT, NT)
        yaT = at(2176, KT, SEQ)
        bT, cT = at(4224, G, NT), at(5312, G, NT)
        xTC = at(6400, 2, DI)
        bTC = at(10496, 2, G * NS)
        R = 11520
        qT = at(R, KT, SEQ)
        kz = at(R + 2048, KV, NT)
        vTC = at(R + 3136, 3, KV * HD)
        toep = at(R + 3904, HEADS, LK)
        xin = at(R + 3904, 3, D)
        dtT = at(6400, NT)
        logit = at(R + 10560, 2, 2, LK)
        ohs = at(R + 10560, 2, VL)
        avec = at(R + 11360, 2, VL)
        pT = at(R + 12224, 2, 640)
        zy = at(R, 2, DI)
        hst = at(R + 4096, G, HPG * HD)
        S0 = R + 6144
        spare = ring[:, FSLOTS:SLOTS - 2, :].rearrange("p s w -> p (s w)")

        def spare_at(off, a, b):
            return spare[:, off:off + a * b].rearrange("p (a b) -> p a b", a=a)

        xpre, cv, sg = spare_at(0, 2, 276), spare_at(552, 2, NT), spare_at(1096, 2, NT)
        xs = spare_at(1640, 3, NT)
        xm, xdec0 = spare[:, 2456:2968], spare[:, 2968:3480]
        ztmp = spare_at(2 * SLOT, 2, 512)
        au = at(S0, 2, HPG, BLK)
        em = at(S0 + 2048, 2, HPG, BLK)
        cbm = at(S0 + 4096, 2, BLK)
        xdt = at(S0 + 4352, 2, HPG, HD)
        xdec = at(S0 + 5376, HPG, HD)
        ysum = at(S0 + 5888, HPG, HD)
        sq_scratch = at(R + 12544, 512)
        yT = at(S0, 16, SEQ)
        mT = at(0, KT, SEQ)
        gsig = ring[:, SLOTS - 2:SLOTS, :].rearrange("p s (a b) -> p (s a) b", b=512)
        gmul = at(R + 12288, 2, 512)
        acc = xres = at(4224, 2, D)
        un = at(R + 3072, 2, D)
        u2T = at(2176, KT, SEQ)
        upart = at(R + 10240, 3, 2, D, dt=BF16)
        ures = at(R, 2, D)
        b1raw = at(R, 2 * FF)
        b1all = at(R + 2048, 2 * FF, dt=BF16)
        b1mid, b1lo = at(R + 3072, 2 * FF, dt=BF16), at(R + 4096, 2 * FF, dt=BF16)
        X0 = R + 5120
        s2 = at(X0, SEQ)
        usel = at(X0 + 256, KT, CAP)
        glu, sig, lin, hsw = (at(512 * i, 2, 256) for i in range(4))
        hT = at(2176, 2, 2, P)
        rt = at(2688, 16, 64)
        ysb = at(6400, 2, 512)
        gfin = at(7424, D)
        gwt = at(10496, 2, P)
        gsel = at(10752, 2, CAP, dt=BF16)
        bsel = at(10816, CAP, dt=BF16)
        pos = at(10880, 2, 40)
        wtok = at(10960, 2, 40)
        ident3 = at(11040, 40)
        ofl = at(11080, 8)
        maskb = at(11088, 2, E, dt=BF16)
        tri_lt_b, ones_b = at(11120, P, dt=BF16), at(11184, P, dt=BF16)
        topv, negm, wsum = at(11248, 2, 8), at(11264, 2, 1), at(11268, 2, 1)
        topi = at(11272, 2, 8).bitcast(U32)
        topf, tope = at(11288, 2, 8), at(11304, 2, 8)

        more_slots = [at(off, SLOT) for off in (R + 6144, R + 8192, 8448, R)]
        DOUBLED = range(len(more_slots))

        bank = [ctx.enter_context(nc.psum_tensor(f"bank{i}", [P, 512], F32)) for i in range(8)]
        toep_rows = nc.dram_tensor("toep_rows", (P, HEADS, 2, VL), F32, kind="Internal").ap()

        slot_loaded = [sem(f"slot_loaded{i}") for i in range(SLOTS)]
        slot_used = sem("slot_used")
        more_loaded = [sem(f"more_loaded{i}") for i in range(len(more_slots))]
        x_in, const_in, vec_in, row_in, rel_in = (sem(n) for n in ("x_in", "const_in", "vec_in", "row_in", "rel_in"))
        toep_out, toep_in, xres_in, b1_in, b1_spread, b2_in, gfin_in, out_done = (sem(n) for n in (
            "toep_out", "toep_in", "xres_in", "b1_in", "b1_spread", "b2_in", "gfin_in", "out_done"))
        dve_chain, act_chain = sem("dve_chain"), sem("act_chain")
        zeros_set, sq_done, ssq_ready, rstd_ready, un_ready, acc_final, tail_chain = (sem(n) for n in (
            "zeros_set", "sq_done", "ssq_ready", "rstd_ready", "un_ready", "acc_final", "tail_chain"))
        tile_ready, tile_saved = sem("tile_ready"), sem("tile_saved")
        rows_T, cols_saved, tab_ready, avec_ready, avec_saved = (sem(n) for n in (
            "rows_T", "cols_saved", "tab_ready", "avec_ready", "avec_saved"))
        a_ready, cum_ready, decay_ready, alog_exp, nabs_ready, dt_exp = (sem(n) for n in (
            "a_ready", "cum_ready", "decay_ready", "alog_exp", "nabs_ready", "dt_exp"))
        qk_ready, logit_done, max_ready, exp_ready, p_ready, pt_ready, ptm_saved, ptb_saved, pv_ready, ya_saved = (
            sem(n) for n in ("qk_ready", "logit_done", "max_ready", "exp_ready", "p_ready", "pt_ready",
                             "ptm_saved", "ptb_saved", "pv_ready", "ya_saved"))
        conv_ready, csig_ready, xs_ready, tr_ready, tr_saved, xdec0_ready, st0_ready, st0_saved, z_ready, z_saved = (
            sem(n) for n in ("conv_ready", "csig_ready", "xs_ready", "tr_ready", "tr_saved", "xdec0_ready",
                             "st0_ready", "st0_saved", "z_ready", "z_saved"))
        au_ready, seg_ready, e_ready, m_ready, y_ready, y_done, yn_ready = (sem(n) for n in (
            "au_ready", "seg_ready", "e_ready", "m_ready", "y_ready", "y_done", "yn_ready"))
        gate_ready, gate_saved, branch_used, gsig_ready, m_done, h_ready, h_done = (sem(n) for n in (
            "gate_ready", "gate_saved", "branch_used", "gsig_ready", "m_done", "h_ready", "h_done"))
        u2_ready, u2_saved, lg_ready, b2_cleared, topexp_in, topexp_ready, mask_ready, rank_ready, wtok_ready, wT_ready = (
            sem(n) for n in ("u2_ready", "u2_saved", "lg_ready", "b2_cleared", "topexp_in", "topexp_ready", "mask_ready", "rank_ready", "wtok_ready", "wT_ready",
                             ))
        b1_ready, flag_ready = sem("b1_ready"), sem("flag_ready")
        g_ready, gat_ready, s2_ready, s2_saved, usel_ready, glu_ready, esig_ready, hs_ready, hT_ready, hT_saved = (
            sem(n) for n in ("g_ready", "gat_ready", "s2_ready", "s2_saved", "usel_ready", "glu_ready",
                             "esig_ready", "hs_ready", "hT_ready", "hT_saved"))
        ye_saved, last_sc_ready, sc_ready, sc_added, fin_ready = (sem(n) for n in ("ye_saved", "last_sc_ready", "sc_ready", "sc_added", "fin_ready"))

        def cols_of(w, c0, kt=KT, k0=0, n=256):
            return w[k0 * P:(k0 + kt) * P, c0:c0 + n].rearrange("(k p) c -> p k c", p=P)

        def slot_view(s, *shape):
            names = "abc"[:len(shape)]
            return ring[:, s, 0:int(np.prod(shape))].rearrange(
                f"p ({' '.join(names)}) -> p {' '.join(names)}", **{names[i]: shape[i] for i in range(len(shape))})

        chunks = []

        def add(*parts):
            chunks.append(parts)
            return len(chunks) - 1

        K8 = (lambda s: slot_view(s, KT, 256))
        ck = add((K8, cols_of(w_in, COL_K)))
        cvv = add((K8, cols_of(w_in, COL_V)))
        cq = []
        for j in range(2):
            for r in range(0, 4, 2):
                parts = []
                for half in range(2):
                    c0 = COL_Q + (8 * j + 4 * half + r) * HD
                    for i in range(2):
                        parts.append((lambda s, half=half, i=i: slot_view(s, KT, 2, 128)[:, :, i, HD * half:HD * half + HD],
                                      cols_of(w_in, c0 + HD * i, n=HD)))
                cq.append(add(*parts))
        cg = [[add((K8, cols_of(w_in, COL_G + D * gi + 256 * dp))) for gi in range(2)] for dp in range(4)]
        conv_tiles = [16 + i for i in range(8)] + list(range(16))
        cx = [add((K8, cols_of(w_in, COL_X + conv_tiles[2 * i] * P))) for i in range(12)]
        cz = [[add((lambda s: slot_view(s, 4, 512), cols_of(w_in, COL_Z + 512 * n, kt=4, k0=4 * h, n=512)))
               for h in range(2)] for n in range(4)]
        w_att_v = w_att.rearrange("(j h r d) c -> h j d r c", j=2, h=2, r=4)

        def att_branch_chunk(dp):
            parts = []
            for half in range(2):
                for j in range(2):
                    parts.append((lambda s, half=half, j=j: slot_view(s, KT, 256)[64 * half:64 * half + 64, 4 * j:4 * j + 4, :],
                                  w_att_v[half, j, :, :, 256 * dp:256 * dp + 256]))
            return add(*parts)

        ca = [att_branch_chunk(dp) for dp in range(2)]
        cs = []
        for dp in range(4):
            if dp >= 2:
                ca.append(att_branch_chunk(dp))
            cs.append([add((K8, cols_of(w_ssm, 256 * dp, k0=k0))) for k0 in (0, 8)])
        co = [add((lambda s: slot_view(s, 2, 1024), cols_of(w_out, 0, kt=2, k0=2 * i, n=1024))) for i in range(4)]
        FRONT = len(chunks)
        loaded_at, seen = [], [0] * SLOTS
        for n, parts in enumerate(chunks):
            seen[n % FSLOTS] += 16 * len(parts)
            loaded_at.append(seen[n % FSLOTS])

        def arrived(eng, n):
            eng.wait_ge(slot_loaded[n % FSLOTS], loaded_at[n])

        T_U, T_K, T_V = 0, 8, 10
        T_DT, T_DTT = 17, 19
        T_Q = [13, 14, 15, 16, 18, 20, 21, 22]
        T_X = 23
        T_Y = T_X + 24
        T_END = T_Y + 16

        branch_order = [(0, 0), (1, 0), (0, 1), (0, 2), (1, 1), (1, 2)] + [(dp, bi) for dp in (2, 3) for bi in range(3)]

        def branch_chunk(j):
            dp, bi = branch_order[j]
            return (ca[dp], *cs[dp])[bi]

        def branch_done(dp):
            return branch_order.index((dp, 2)) + 1

        released = [None] * FRONT
        released[ck], released[cvv] = (tile_ready, T_K + 2), (tile_ready, T_V + 3)
        for i, n in enumerate(cq):
            released[n] = (tile_ready, T_Q[2 * i + 1] + 1)
        for i, n in enumerate(cx):
            released[n] = (tile_ready, T_X + 2 * i + 2)
        for i, pair in enumerate(cz):
            for n in pair:
                released[n] = (z_ready, 2 * i + 2)
        for dp in range(4):
            for n in cg[dp]:
                released[n] = (gate_ready, 2 * dp + 2)
            for bi, n in enumerate((ca[dp], *cs[dp])):
                released[n] = (branch_used, branch_order.index((dp, bi)) + 1)
        for n in co:
            released[n] = (h_ready, 2)

        def slot_of(i):
            return (FSLOTS + i) % SLOTS

        def z_bank(it):
            return bank[5 if it else 3]

        def cb_bank(it):
            return bank[4 if it else 7]

        GATE_FIRST = 5
        gate_before = [int(t in (1, 4, 6)) for t in range(8)]
        gates_by = [(GATE_FIRST + sum(gate_before[:t + 1]) + t + 1) // 2 for t in range(8)]
        assert gates_by[-1] == 8

        def expert_slot(i, odd):
            if odd and i in DOUBLED:
                return more_slots[i - DOUBLED.start].rearrange("p (a b) -> p a b", a=2), more_loaded[i - DOUBLED.start]
            return slot_view(slot_of(i), 2, 1024), slot_loaded[slot_of(i)]

        def expert_arrived(eng, i, t, pair, odd):
            _, loaded = expert_slot(i, odd)
            if i not in DOUBLED:
                eng.wait_ge(loaded, t * 16 + (seen[slot_of(i)] + 16))
            elif odd:
                eng.wait_ge(loaded, pair * 16 + 16)
            else:
                eng.wait_ge(loaded, pair * 16 + (seen[slot_of(i)] + 16))

        w1_v = w1.rearrange("e (s k p) (h c) -> e h s p k c", p=P, k=2, h=2)
        w2_v = w2.rearrange("e (h c b p) n -> e h b p c n", p=P, h=2, c=2)

        def expert_sources(e, ahead=0):
            one = bass.ds(e, 1)
            src = [w1_v[ahead:][one, h, s].rearrange("e p k c -> p (e k) c") for h in range(2) for s in range(4)]
            src += [w2_v[ahead:][one, h, b].rearrange("e p c n -> p (e c) n") for h in range(2) for b in range(2)]
            return src

        block = ctx.enter_context(nc.Block())

        @block.sync
        def _(sp):
            sp.dma_start(xin[:, 1:3, :], x.rearrange("(c p) d -> p c d", p=P)).then_inc(x_in, 16)
            sp.dma_start(xin[0:META, 0, :], meta).then_inc(x_in, 16)
            sp.wait_ge(row_in, 5 * 16)

            def fetch(i, src, odd):
                dst, loaded = expert_slot(i, odd)
                sp.dma_start(dst, src).then_inc(loaded, 16)

            sources = expert_sources(0), expert_sources(1)
            for n, parts in enumerate(chunks):
                if n == ca[0] + FSLOTS + 1:
                    sp.wait_ge(y_done, 8)
                    for i in range(SLOTS - 2 - FSLOTS):
                        fetch(i, sources[0][i], 0)
                    fetch(DOUBLED[2], sources[1][DOUBLED[2]], 1)
                if n >= FSLOTS:
                    sp.wait_ge(*released[n - FSLOTS])
                for dst, src in parts:
                    sp.dma_start(dst(n % FSLOTS), src).then_inc(slot_loaded[n % FSLOTS], 16)

            def first_experts():
                late = [n % FSLOTS for n in co]
                for i in range(SLOTS - 2 - FSLOTS, SLOTS):
                    if slot_of(i) not in late:
                        if i < SLOTS - FSLOTS:
                            sp.wait_ge(m_done, 8)
                        else:
                            sp.wait_ge(branch_used, 12)
                        fetch(i, sources[0][i], 0)
                for i in DOUBLED[:2]:
                    sp.wait_ge(m_done, 8)
                    fetch(i, sources[1][i], 1)
                for i in range(SLOTS):
                    if slot_of(i) in late:
                        sp.wait_ge(h_ready, 2)
                        fetch(i, sources[0][i], 0)
                sp.wait_ge(topexp_in, 1)
                fetch(DOUBLED[3], sources[1][DOUBLED[3]], 1)

            def doubled(sources, odd, used):
                for i in DOUBLED:
                    sp.wait_ge(slot_used, used + (i + 1))
                    fetch(i, sources[i], odd)

            def single(sources, odd, used):
                for i in range(DOUBLED.stop, SLOTS):
                    sp.wait_ge(slot_used, used + (i + 1))
                    fetch(i, sources[i], odd)

            def step(e, odd, used):
                sources, following = expert_sources(e), expert_sources(e, 1)
                doubled(following, 1 - odd, used)
                single(sources, odd, used)

            def last_two(used):
                single(expert_sources(E - 2), 0, used)
                sources = expert_sources(E - 1)
                doubled(sources, 1, used)
                single(sources, 1, used + SLOTS)

            first_experts()
            PAIR = 2 * SLOTS
            with sp.Fori(0, E // 2 - 2) as pair:
                step(pair * 2 + 1, 1, pair * PAIR)
                step(pair * 2 + 2, 0, pair * PAIR + SLOTS)
            step(E - 3, 1, (E - 4) * SLOTS)
            last_two((E - 3) * SLOTS)
            sp.wait_ge(flag_ready, 1)
            more = sp.value_load(ofl[0:1, 0:1].bitcast(I32), min_val=0, max_val=1)
            with sp.If(more):
                with sp.Fori(0, PASSES - 1) as b:
                    doubled(expert_sources(0), 0, b * (E * SLOTS) + (E - 2) * SLOTS)
                    with sp.Fori(0, E // 2 - 2) as pair:
                        step(pair * 2, 0, b * (E * SLOTS) + (pair * PAIR + (E - 1) * SLOTS))
                        step(pair * 2 + 1, 1, b * (E * SLOTS) + (pair * PAIR + E * SLOTS))
                    step(E - 4, 0, b * (E * SLOTS) + (2 * E - 5) * SLOTS)
                    step(E - 3, 1, b * (E * SLOTS) + (2 * E - 4) * SLOTS)
                    last_two(b * (E * SLOTS) + (2 * E - 3) * SLOTS)
            for c in range(2):
                sp.wait_ge(fin_ready, c + 1)
                sp.dma_start(out[c * P:(c + 1) * P, :], un[:, c, :]).then_inc(out_done, 16)
            sp.wait_ge(out_done, 32)

        @block.gpsimd
        def _(pool):
            pool.dma_start(ohs[0:NB + 1, :, :], c_oh).then_inc(rel_in, 16)
            pool.dma_start(tab[0:NB, 0, :], rel).then_inc(rel_in, 16)
            norms = ((0, 3), (0, 4), (4, 8), (0, 1), (1, 2), (0, 1), (1, 2))

            def rsqrt(n):
                pool.wait_ge(ssq_ready, n + 1)
                a, b = norms[n]
                pool.tensor_tensor(rstd[:, a:b], ssq[:, a:b], half_neg[:, a:b],
                                   ALU.pow).then_inc(rstd_ready, 1)

            rsqrt(0)
            for dst, src, n in ((dtb, dt_bias, SH), (alog, a_log, SH), (dskip, d_skip, SH), (brt, b_rt, E),
                                (sink_nat, sinks, HEADS)):
                pool.dma_start(dst[:, :], bass.AP(src.tensor, 0, [[0, P], [1, n]])).then_inc(vec_in, 16)
            pool.dma_start(wdt[:, :, :], cols_of(w_in, COL_DT, n=SH)).then_inc(vec_in, 16)
            pool.dma_start(wrt[:, :, :], w_rt.rearrange("(k p) e -> p k e", p=P)).then_inc(vec_in, 16)
            pool.wait_ge(avec_saved, 1)
            pool.dma_start(toep_rows.rearrange("q h a v -> h q (a v)"),
                           avec[0:HEADS, :, :].rearrange("p a v -> p (a v)").unsqueeze(1).to_broadcast([HEADS, P, 2 * VL])
                           ).then_inc(toep_out, 16)
            pool.wait_ge(toep_out, 16)
            pool.wait_ge(tile_ready, T_U + 8)
            RP = HEADS * 2 * VL

            def toeplitz(x0, half, n):
                return bass.AP(toep_rows.tensor, half * VL + x0, [[RP - 1, P], [2 * VL, HEADS], [1, n]])

            with nc.allow_non_contiguous_dma(reason="short runs of the bias"):
                pool.dma_start(toep[:, :, 0:META], toeplitz(127, 0, META)).then_inc(toep_in, 16)
                pool.dma_start(toep[:, :, META:NT], toeplitz(127 + META, 1, SEQ)).then_inc(toep_in, 16)
                pool.dma_start(toep[:, :, NT:NT + META], toeplitz(255, 0, META)).then_inc(toep_in, 16)
                pool.dma_start(toep[:, :, NT + META:LK], toeplitz(255 + META, 1, BLK)).then_inc(toep_in, 16)
            for n in range(1, 7):
                rsqrt(n)
                if n == 2:
                    pool.wait_ge(y_done, 8)
                    pool.dma_start(xres, x.rearrange("(c p) d -> p c d", p=P)).then_inc(xres_in, 16)
                    pool.wait_ge(tile_ready, T_END)
                    pool.dma_start(b1raw[0:E, :], b1).then_inc(b1_in, 16)
                    pool.wait_ge(b1_ready, 1)
                    pool.dma_start(b1all[E:2 * E, :], b1mid[0:E, :]).then_inc(b1_spread, 16)
                    pool.dma_start(b1all[2 * E:3 * E, :], b1lo[0:E, :]).then_inc(b1_spread, 16)
                if n == 3:
                    pool.memset(s2, 0.0).then_inc(b2_cleared, 1)
                    pool.wait_ge(h_ready, 2)
                    pool.memset(ysb, 0.0).then_inc(b2_cleared, 1)
                    pool.wait_ge(b2_cleared, 2)
                    pool.dma_start(ysb[0:E, :, :].rearrange("e a b -> e (a b)"), b2).then_inc(b2_in, 16)
                if n == 4:
                    pool.wait_ge(flag_ready, 1)
                    pool.dma_start(gfin, bass.AP(g_fin.tensor, 0, [[0, P], [1, D]])).then_inc(gfin_in, 16)

        @block.scalar
        def _(act):
            sc = nc.scalar
            ch = Chain(act, act_chain)
            act.dma_start(squares[:, :, :], c_sq).then_inc(const_in, 16)
            act.dma_start(rows[0:96, 0, :], conv_w.rearrange("w (i c) -> (w i) c", c=P)).then_inc(row_in, 16)
            act.dma_start(rows[96:120, 0, :], conv_b.rearrange("(i c) -> i c", c=P)).then_inc(row_in, 16)
            act.dma_start(rows[0:8, 1, :], g_mix.rearrange("(i c) -> i c", c=P)).then_inc(row_in, 16)
            act.dma_start(rows[8:16, 1, :], g_ffn.rearrange("(i c) -> i c", c=P)).then_inc(row_in, 16)
            act.dma_start(rows[16:32, 1, :], g_ssm.rearrange("(i c) -> i c", c=P)).then_inc(row_in, 16)

            def squared(ins, val):
                ins.then_inc(sq_done, 1)
                act.wait_ge(sq_done, val)

            act.wait_ge(x_in, 32)
            act.wait_ge(zeros_set, 1)
            for c, r in ((0, META), (1, P), (2, P)):
                squared(sc.activation(uT.rearrange("p k n -> p (k n)")[0:r, 0:D], xin[0:r, c, :], ACT.Square,
                                      accum_out=ssq[0:r, c:c + 1]), c + 1)
            act.wait_ge(rows_T, 1)
            ch.link(sc.activation(cols[:, 0:120], bank[4][:, 0:120], ACT.Copy))
            sc.activation(cols[:, 120:152], bank[4][:, 128:160], ACT.Copy).then_inc(cols_saved, 1)
            act.wait_ge(cols_saved, 1)
            act.wait_ge(avec_ready, 1)
            ch.link(sc.activation(avec[0:HEADS, 0, :], bank[5][0:HEADS, 0:VL], ACT.Copy))
            sc.activation(avec[0:HEADS, 1, :], bank[6][0:HEADS, 0:VL], ACT.Copy).then_inc(avec_saved, 1)
            def tile(p):
                act.wait_ge(tile_ready, p + 1)
                return bank[p % 4]

            def saved(ins):
                ins.then_inc(tile_saved, 1)

            for k in range(KT):
                saved(sc.activation(uT[:, k, :], tile(T_U + k)[:, 0:NT], ACT.Copy, scale=col_gmix[:, k:k + 1]))
            for j in range(2):
                b = tile(T_K + j)
                ch.link(sc.activation(kz[0:64, 2 * j, :], b[0:64, 0:NT], ACT.Copy))
                saved(sc.activation(kz[64:128, 2 * j + 1, :], b[64:128, 0:NT], ACT.Copy))
            for c, r in ((0, META), (1, P), (2, P)):
                saved(sc.activation(vTC[0:r, c, :], tile(T_V + c)[0:r, 0:256], ACT.Copy))
            for i in range(8):
                if i == 4:
                    saved(sc.activation(dtT[0:SH, :], tile(T_DT)[0:SH, 0:NT], ACT.Copy))
                saved(sc.activation(qT[:, i, :], tile(T_Q[i])[:, 0:SEQ], ACT.Copy))
                if i == 4:
                    b = tile(T_DTT)
                    ch.link(sc.activation(dts[0:META, 2, 0:SH], b[0:META, 0:SH], ACT.Copy))
                    saved(sc.activation(dts[:, 2, SH:3 * SH], b[:, SH:3 * SH], ACT.Copy))
            act.wait_ge(vec_in, 7 * 16)
            sc.activation(dts[:, 6, 0:SH], alog[:, :], ACT.Exp).then_inc(alog_exp, 1)
            act.wait_ge(nabs_ready, 1)
            sc.activation(dts[:, 4, :], dts[:, 3, :], ACT.Exp).then_inc(dt_exp, 1)
            act.wait_ge(cum_ready, 1)
            sc.activation(decays[:, :, :, :], bank[7][:, 0:288].rearrange("p (a c h) -> p a c h", a=3, c=3),
                          ACT.Exp).then_inc(decay_ready, 1)

            def att_exp(t):
                act.wait_ge(max_ready, t + 1)
                for half in range(2):
                    for n, (a, b) in enumerate(((0, NT), (NT, LK))):
                        ch.link(sc.activation(logit[:, t % 2, half, a:b], logit[:, t % 2, half, a:b], ACT.Exp,
                                              bias=stats[:, 1, 2 * half + n:2 * half + n + 1],
                                              accum_out=stats[:, 3, 2 * half + n:2 * half + n + 1]))
                sc.activation(stats[:, 4, :], stats[:, 2, :], ACT.Exp).then_inc(exp_ready, 1)

            def att_save_pt(t):
                act.wait_ge(pt_ready, t + 1)
                if t >= 1:
                    act.wait_ge(pv_ready, t)
                for half in range(2):
                    ins = sc.activation(pT[:, half, 0:384], bank[4 + half][:, 0:384], ACT.Copy)
                    if half:
                        ins.then_inc(ptb_saved, 1)

            def att_save_y(t):
                act.wait_ge(pv_ready, t + 1)
                sc.activation(yaT[:, t, :], bank[7][:, 0:SEQ], ACT.Copy).then_inc(ya_saved, 1)

            def gate_save(d):
                act.wait_ge(gate_ready, d + 1)
                sc.activation(gsig[:, d, :], bank[2 + d % 2][:, :], ACT.Copy).then_inc(gate_saved, 1)

            gate_save(0)
            att_exp(0)
            gate_save(1)
            for t in range(8):
                att_save_pt(t)
                if t + 1 < 8:
                    att_exp(t + 1)
                att_save_y(t)
                for d in range(gates_by[t - 1] if t else 2, gates_by[t]):
                    gate_save(d)

            def conv_evict(i):
                b = tile(T_X + i)
                if i >= 2:
                    act.wait_ge(conv_ready, i - 1)
                saved(sc.activation(xpre[:, i % 2, 3:3 + NT], b[:, 0:NT], ACT.Copy))

            def conv_sig(i):
                act.wait_ge(conv_ready, i + 1)
                if i >= 2:
                    act.wait_ge(xs_ready, i - 1)
                sc.activation(sg[:, i % 2, :], cv[:, i % 2, :], ACT.Sigmoid).then_inc(csig_ready, 1)

            def conv_tr(i):
                if 4 <= i < 8:
                    return
                n = i if i < 4 else i - 4
                act.wait_ge(tr_ready, n + 1)
                b = bank[4 + n % 2]
                if i < 4:
                    ch.link(sc.activation(bTC[0:META, 0, i * P:(i + 1) * P], b[0:META, 0:P], ACT.Copy))
                    sc.activation(bTC[:, 1, i * P:(i + 1) * P], b[:, P:2 * P], ACT.Copy).then_inc(tr_saved, 1)
                else:
                    j = i - 8
                    if j % 4 == 0 and j:
                        act.wait_ge(xdec0_ready, j // 4)
                    ch.link(sc.activation(xm[0:META, (j % 4) * P:(j % 4 + 1) * P], b[0:META, 0:P], ACT.Copy))
                    sc.activation(xTC[:, :, j * P:(j + 1) * P],
                                  b[:, P:3 * P].rearrange("p (c n) -> p c n", c=2), ACT.Copy).then_inc(tr_saved, 1)

            def st0_save(g):
                act.wait_ge(st0_ready, g + 1)
                sc.activation(hst[:, g, :], bank[6][:, :], ACT.Copy).then_inc(st0_saved, 1)

            def z_evict(it):
                g, c = divmod(it, 2)
                act.wait_ge(z_ready, it + 1)
                if it >= 2:
                    act.wait_ge(y_done, it - 1)
                ch.link(sc.activation(zy[:, c, 512 * g:512 * g + 512], z_bank(it)[:, :], ACT.Sigmoid))
                sc.activation(ztmp[:, it % 2, :], z_bank(it)[:, :], ACT.Copy).then_inc(z_saved, 1)

            def ssd_exp(it):
                act.wait_ge(seg_ready, it + 1)
                if it >= 2:
                    act.wait_ge(y_ready, it - 1)
                for j in range(2):
                    ins = sc.activation(em[:, it % 2, 4 * j:4 * j + 4, :],
                                        bank[j][:, :].rearrange("p (h l) -> p h l", h=4), ACT.Exp)
                    if j:
                        ins.then_inc(e_ready, 1)

            act.wait_ge(gate_saved, 8)
            for i in range(24 + 5):
                if i < 24:
                    conv_evict(i)
                if 8 <= i < 16:
                    sc.activation(gsig[:, i - 8, :], gsig[:, i - 8, :], ACT.Sigmoid).then_inc(gsig_ready, 1)
                if 0 <= i - 1 < 24:
                    conv_sig(i - 1)
                if 0 <= i - 3 < 24:
                    conv_tr(i - 3)
                if i == 26:
                    z_evict(0)
                if i == 27:
                    ssd_exp(0)
                if i - 5 >= 11 and (i - 5 - 8) % 4 == 3:
                    st0_save((i - 5 - 8) // 4)

            for it in range(8):
                if it + 1 < 8:
                    ssd_exp(it + 1)
                    z_evict(it + 1)
                act.wait_ge(y_done, it + 1)
                g, c = divmod(it, 2)
                squared(sc.activation(sq_scratch, zy[:, c, 512 * g:512 * g + 512], ACT.Square,
                                      accum_out=ssq[:, it:it + 1]), 3 + it + 1)

            for i in range(16):
                act.wait_ge(tile_ready, T_Y + i + 1)
                saved(sc.activation(yT[:, i, :], bank[4 + i % 4][:, 0:SEQ], ACT.Copy,
                                    scale=col_gssm[:, i:i + 1]))

            for c in range(2):
                act.wait_ge(h_done, 2 * c + 2)
                squared(sc.activation(ures[:, c, :], acc[:, c, :], ACT.Square, accum_out=ssq[:, c:c + 1]), 11 + c + 1)
                for k in range(KT):
                    if k % 4 == 0:
                        act.wait_ge(u2_ready, 2 * c + k // 4 + 1)
                    ins = sc.activation(u2T[:, k, P * c:P * c + P], bank[4 + 2 * c + k // 4][:, P * (k % 4):P * (k % 4) + P],
                                        ACT.Copy, scale=col_gffn[:, k:k + 1])
                    if k % 4 == 3:
                        ins.then_inc(u2_saved, 1)
            act.wait_ge(topexp_in, 1)
            for c in range(2):
                ins = sc.activation(tope[:, c, 0:4], topv[:, c, 0:4], ACT.Exp, bias=negm[:, c, :],
                                    accum_out=wsum[:, c, :])
                if c:
                    ins.then_inc(topexp_ready, 1)
                else:
                    ch.link(ins)
            act.wait_ge(b2_cleared, 2)
            act.wait_ge(wT_ready, 1)
            for c in range(2):
                sc.activation(s2[0:E, P * c:P * c + P], bank[5][0:E, P * c:P * c + P], ACT.Copy).then_inc(ye_saved, 1)

            def expert(t):
                act.wait_ge(s2_ready, t + 1)
                sc.activation(s2, bank[5][:, 0:SEQ], ACT.Copy).then_inc(s2_saved, 1)
                for half in range(2):
                    act.wait_ge(glu_ready, t * 2 + half + 1)
                    sc.activation(sig[:, half, :], glu[:, half, :], ACT.Sigmoid, scale=ALPHA).then_inc(esig_ready, 1)
                for half in range(2):
                    act.wait_ge(hT_ready, t * 2 + half + 1)
                    sc.activation(hT[:, half, :, :], bank[5][:, 0:256].rearrange("p (b n) -> p b n", b=2),
                                  ACT.Copy).then_inc(hT_saved, 1)
                act.wait_ge(slot_used, t * 12 + 12)
                for n in range(2):
                    sc.activation(ysb[:, n, :], bank[2 + n][:, :], ACT.Copy).then_inc(ye_saved, 1)

            with act.Fori(0, E) as t:
                expert(t)
            act.wait_ge(flag_ready, 1)
            more = act.value_load(ofl[0:1, 0:1].bitcast(I32), min_val=0, max_val=1)
            with act.If(more):
                with act.Fori(E, PASSES * E) as t:
                    expert(t)
            for c in range(2):
                act.wait_ge(acc_final, 2 * c + 2)
                squared(sc.activation(at(0, D), acc[:, c, :], ACT.Square,
                                      accum_out=ssq[:, c:c + 1]), 13 + c + 1)

        @block.vector
        def _(dve):
            v = nc.vector
            ch = Chain(dve, dve_chain)

            def done(ins, s, val):
                ins.then_inc(s, 1)
                dve.wait_ge(s, val)

            ch.link(v.memset(half_neg[:, :], -0.5))
            ch.link(v.memset(ssq[:, :], 1.0))
            ch.link(v.memset(dts[:, :, :], 0.0))
            ch.link(v.memset(tab[NB:NB + 1, :, :], 1.0))
            ch.link(v.memset(kz[:, :, :], 0.0))
            ch.link(v.memset(vTC[:, :, :], 0.0))
            done(v.memset(pT[:, :, :], 0.0), zeros_set, 1)
            dve.wait_ge(rel_in, 32)
            done(v.tensor_copy(tab[0:NB + 1, 1, :].rearrange("p (j r h) -> p j r h", j=2, r=4),
                               tab[0:NB + 1, 0, :].rearrange("p (j h r) -> p j r h", j=2, h=2)), tab_ready, 1)

            dve.wait_ge(sq_done, 3)
            done(v.tensor_scalar(ssq[:, 0:3], ssq[:, 0:3], 1.0 / D, EPS, ALU.mult, ALU.add), ssq_ready, 1)
            dve.wait_ge(rstd_ready, 1)
            for c, r in ((0, META), (1, P), (2, P)):
                done(v.tensor_scalar(xin[0:r, c, :], xin[0:r, c, :], rstd[0:r, c:c + 1], None, ALU.mult), un_ready, c + 1)
            dve.wait_ge(vec_in, 7 * 16)
            ch.link(v.tensor_copy(sink_p[:, :].rearrange("p (j r h) -> p j r h", j=2, r=4),
                                  sink_nat[:, :].rearrange("p (j h r) -> p j r h", j=2, h=2)))

            raw, nabs, ex, tt, acc1 = (dts[:, i, :] for i in (2, 3, 4, 5, 1))
            c3 = (lambda v_: v_.rearrange("p (c h) -> p c h", c=3))
            bc = (lambda v_: v_.unsqueeze(1).to_broadcast([P, 3, SH]))
            dve.wait_ge(tile_saved, T_DTT + 1)
            ch.link(v.tensor_tensor(c3(raw), c3(raw), bc(dtb[:, :]), ALU.add))
            ch.link(v.tensor_scalar(tt, raw, -1.0, None, ALU.mult))
            done(v.tensor_tensor(nabs, raw, tt, ALU.min), nabs_ready, 1)
            ch.link(v.tensor_scalar(raw, raw, 0.0, None, ALU.max))
            dve.wait_ge(dt_exp, 1)
            ch.link(v.tensor_scalar(tt, ex, 2.0, None, ALU.add))
            ch.link(v.reciprocal(tt, tt))
            ch.link(v.tensor_tensor(ex, ex, tt, ALU.mult))
            ch.link(v.tensor_tensor(tt, ex, ex, ALU.mult))
            ch.link(v.memset(nabs, 1.0 / 17))
            for k in (15, 13, 11, 9, 7, 5, 3, 1):
                ch.link(v.tensor_tensor(nabs, nabs, tt, ALU.mult))
                ch.link(v.tensor_scalar(nabs, nabs, 1.0 / k, None, ALU.add))
            ch.link(v.tensor_tensor(nabs, nabs, ex, ALU.mult))
            ch.link(v.memset(dt, 0.0))
            for c, r in ((0, META), (1, P), (2, P)):
                s = slice(32 * c, 32 * c + 32)
                ch.link(v.scalar_tensor_tensor(dt[0:r, s], nabs[0:r, s], 2.0, raw[0:r, s], ALU.mult, ALU.add))
            dve.wait_ge(alog_exp, 1)
            done(v.scalar_tensor_tensor(c3(aa), c3(dt), -1.0, bc(dts[:, 6, 0:SH]), ALU.mult, ALU.mult), a_ready, 1)

            dve.wait_ge(toep_in, 64)

            def att_max(t):
                dve.wait_ge(qk_ready, t + 1)
                if t >= 2:
                    dve.wait_ge(pt_ready, t - 1)
                for half in range(2):
                    ins = v.scalar_tensor_tensor(logit[:, t % 2, half, :], bank[half][:, 0:LK],
                                                 HD ** -0.5, toep[:, 2 * t + half, :], ALU.mult, ALU.add)
                    done(ins, logit_done, 2 * t + half + 1)
                if t >= 1:
                    dve.wait_ge(exp_ready, t)
                mx = stats[:, 0, :].rearrange("p (h n) -> p h n", n=2)
                ch.link(v.tensor_reduce(mx[:, :, 0], logit[:, t % 2, :, 0:NT], AX, ALU.max))
                ch.link(v.tensor_reduce(mx[:, :, 1], logit[:, t % 2, :, NT:LK], AX, ALU.max))
                sk = sink_p[:, 2 * t:2 * t + 2].unsqueeze(2).to_broadcast([P, 2, 2])
                ch.link(v.tensor_tensor(mx, mx, sk, ALU.max))
                ch.link(v.tensor_tensor(stats[:, 2, :].rearrange("p (h n) -> p h n", n=2), sk, mx, ALU.subtract))
                done(v.tensor_scalar(stats[:, 1, :], stats[:, 0, :], -1.0, None, ALU.mult), max_ready, t + 1)

            def att_norm(t):
                dve.wait_ge(exp_ready, t + 1)
                ch.link(v.tensor_tensor(stats[:, 5, :], stats[:, 3, :], stats[:, 4, :], ALU.add))
                ch.link(v.reciprocal(stats[:, 5, :], stats[:, 5, :]))
                for half in range(2):
                    for n, (a, b) in enumerate(((0, NT), (NT, LK))):
                        ins = v.tensor_scalar(logit[:, t % 2, half, a:b], logit[:, t % 2, half, a:b],
                                              stats[:, 5, 2 * half + n:2 * half + n + 1], None, ALU.mult)
                        if half and n:
                            done(ins, p_ready, t + 1)
                        else:
                            ch.link(ins)

            def att_meta(t):
                dve.wait_ge(pt_ready, t + 1)
                if t >= 1:
                    dve.wait_ge(pv_ready, t)
                done(v.tensor_copy(pT[0:META, :, 384:640], bank[6][0:META, :].rearrange("p (h n) -> p h n", h=2)),
                     ptm_saved, t + 1)

            for t in range(8):
                att_max(t)
                if t >= 1:
                    att_meta(t - 1)
                att_norm(t)
            att_meta(7)

            dve.wait_ge(ya_saved, 8)
            ch.link(v.memset(xpre[:, :, 0:3], 0.0))
            ch.link(v.memset(xdec0, 0.0))
            done(v.memset(bTC[:, 0, :], 0.0), zeros_set, 2)

            def conv(i):
                ct = conv_tiles[i]
                w = (lambda k: col_cw[:, k * 24 + ct:k * 24 + ct + 1])
                dve.wait_ge(tile_saved, T_X + i + 1)
                if i >= 2:
                    dve.wait_ge(csig_ready, i - 1)
                xp, o = xpre[:, i % 2, :], cv[:, i % 2, :]
                ch.link(v.tensor_scalar(o, xp[:, 0:NT], w(0), col_cb[:, ct:ct + 1], ALU.mult, ALU.add))
                for k in (1, 2):
                    ch.link(v.scalar_tensor_tensor(o, xp[:, k:k + NT], w(k), o, ALU.mult, ALU.add))
                done(v.scalar_tensor_tensor(o, xp[:, 3:3 + NT], w(3), o, ALU.mult, ALU.add), conv_ready, i + 1)

            def silu(i):
                dve.wait_ge(csig_ready, i + 1)
                if i < 4:
                    o = bT[:, i, :]
                elif i < 8:
                    o = cT[:, i - 4, :]
                else:
                    o = xs[:, i % 3, :]
                    if i >= 11:
                        dve.wait_ge(tr_ready, i - 3 - 4 + 1)
                done(v.tensor_tensor(o, cv[:, i % 2, :], sg[:, i % 2, :], ALU.mult), xs_ready, i + 1)

            def xdecay0(g):
                dve.wait_ge(tr_saved, 4 + 4 * g + 4)
                if g:
                    dve.wait_ge(st0_ready, g)
                m = (lambda v_: v_.rearrange("p (h d) -> p h d", h=HPG))
                sc_ = (lambda v_: v_.unsqueeze(2).to_broadcast([META, HPG, HD]))
                ch.link(v.tensor_tensor(m(xdec0[0:META]), m(xm[0:META]), sc_(dt[0:META, 8 * g:8 * g + 8]), ALU.mult))
                done(v.tensor_tensor(m(xdec0[0:META]), m(xdec0[0:META]),
                                     sc_(decays[0:META, 1, 0, 8 * g:8 * g + 8]), ALU.mult), xdec0_ready, g + 1)

            def ssd_au(it):
                g, c = divmod(it, 2)
                if it >= 2:
                    dve.wait_ge(seg_ready, it - 1)
                done(v.tensor_tensor(au[:, it % 2, :, :],
                                     aa[:, 32 * (c + 1) + 8 * g:32 * (c + 1) + 8 * g + 8].unsqueeze(2).to_broadcast([P, HPG, BLK]),
                                     tri_le.unsqueeze(1).to_broadcast([P, HPG, BLK]), ALU.mult), au_ready, it + 1)

            dve.wait_ge(decay_ready, 1)
            for i in range(24 + 5):
                if i < 24:
                    conv(i)
                if 0 <= i - 1 < 24:
                    silu(i - 1)
                if i - 4 >= 11 and (i - 4 - 8) % 4 == 3:
                    xdecay0((i - 4 - 8) // 4)
                if i in (20, 21):
                    ssd_au(i - 20)

            def heads(v_, h0=0):
                return v_.unsqueeze(2).to_broadcast([P, HPG, HD])

            def ssd_pre(it):
                g, c = divmod(it, 2)
                if it >= 2:
                    dve.wait_ge(y_ready, it - 1)
                xg = xTC[:, c, 512 * g:512 * g + 512].rearrange("p (h d) -> p h d", h=HPG)
                s = slice(32 * (c + 1) + 8 * g, 32 * (c + 1) + 8 * g + 8)
                ch.link(v.tensor_tensor(xdt[:, it % 2, :, :], xg, heads(dt[:, s]), ALU.mult))
                if c == 0:
                    ch.link(v.tensor_tensor(xdec, xdt[:, it % 2, :, :], heads(decays[:, 1, 1, 8 * g:8 * g + 8]), ALU.mult))
                dve.wait_ge(e_ready, it + 1)
                ch.link(v.tensor_tensor(cbm[:, it % 2, :], cb_bank(it)[:, 0:BLK], tri_le, ALU.mult))
                done(v.tensor_tensor(em[:, it % 2, :, :], em[:, it % 2, :, :],
                                     cbm[:, it % 2, :].unsqueeze(1).to_broadcast([P, HPG, BLK]), ALU.mult), m_ready, it + 1)

            def group_scale(half):
                dve.wait_ge(sq_done, 3 + 4 * (half + 1))
                m = ssq[:, 4 * half:4 * half + 4]
                done(v.tensor_scalar(m, m, float(G) / DI, EPS, ALU.mult, ALU.add), ssq_ready, 2 + half)

            def group_norm(half):
                dve.wait_ge(rstd_ready, 2 + half)
                for it in range(4 * half, 4 * half + 4):
                    g, c = divmod(it, 2)
                    zz = zy[:, c, 512 * g:512 * g + 512]
                    done(v.tensor_scalar(zz, zz, rstd[:, it:it + 1], None, ALU.mult), yn_ready, it + 1)

            def ssd_post(it):
                g, c = divmod(it, 2)
                dve.wait_ge(y_ready, it + 1)
                ys = ysum
                ch.link(v.tensor_tensor(ys, bank[6][:, :].rearrange("p (h d) -> p h d", h=HPG),
                                        heads(decays[:, 0, c + 1, 8 * g:8 * g + 8]), ALU.mult))
                yv = ys.rearrange("p (q i) d -> p q i d", i=2)
                for i in range(2):
                    for j in range(2):
                        src = bank[2 + j][:, :].rearrange("p (q i o d) -> p q i o d", q=2, i=2, o=2)[:, :, i, i, :]
                        ch.link(v.tensor_tensor(yv[:, 2 * j:2 * j + 2, i, :], yv[:, 2 * j:2 * j + 2, i, :], src, ALU.add))
                xg = xTC[:, c, 512 * g:512 * g + 512].rearrange("p (h d) -> p h d", h=HPG)
                ch.link(v.tensor_tensor(xg, xg, heads(dskip[:, 8 * g:8 * g + 8]), ALU.mult))
                ch.link(v.tensor_tensor(ys, ys, xg, ALU.add))
                zz = zy[:, c, 512 * g:512 * g + 512].rearrange("p (h d) -> p h d", h=HPG)
                if c == 0:
                    hg = hst[:, g, :].rearrange("p (h d) -> p h d", h=HPG)
                    ch.link(v.tensor_tensor(hg, hg, heads(decays[:, 2, 1, 8 * g:8 * g + 8]), ALU.mult))
                    ch.link(v.tensor_tensor(hg, hg, bank[7][:, :].rearrange("p (h d) -> p h d", h=HPG), ALU.add))
                dve.wait_ge(z_saved, it + 1)
                ch.link(v.tensor_tensor(ys, ys, ztmp[:, it % 2, :].rearrange("p (h d) -> p h d", h=HPG), ALU.mult))
                done(v.tensor_tensor(zz, zz, ys, ALU.mult), y_done, it + 1)

            ssd_pre(0)
            for it in range(8):
                if it + 2 < 8:
                    ssd_au(it + 2)
                ssd_post(it)
                if it + 1 < 8:
                    ssd_pre(it + 1)
                if it == 4:
                    group_scale(0)
                if it == 5:
                    group_norm(0)
            group_scale(1)
            group_norm(1)

            dve.wait_ge(gsig_ready, 8)
            for d in range(8):
                if d == 6:
                    dve.wait_ge(b1_in, 16)
                    ch.link(v.tensor_copy(b1all[0:E, :], b1raw[0:E, :]))
                    ch.link(v.tensor_tensor(b1raw[0:E, :], b1raw[0:E, :], b1all[0:E, :], ALU.subtract))
                    ch.link(v.tensor_copy(b1mid[0:E, :], b1raw[0:E, :]))
                    ch.link(v.tensor_tensor(b1raw[0:E, :], b1raw[0:E, :], b1mid[0:E, :], ALU.subtract))
                    done(v.tensor_copy(b1lo[0:E, :], b1raw[0:E, :]), b1_ready, 1)
                dve.wait_ge(branch_used, branch_done(d // 2))
                ch.link(v.tensor_tensor(gmul[:, d % 2, :], gsig[:, d, :], bank[d % 4][:, :], ALU.mult))
                done(v.tensor_tensor(mT[:, d, :], gmul[:, d % 2, 0:256], gmul[:, d % 2, 256:512], ALU.add), m_done, d + 1)

            dve.wait_ge(xres_in, 16)
            for c in range(2):
                dve.wait_ge(h_ready, c + 1)
                for n in range(2):
                    done(v.tensor_tensor(acc[:, c, 512 * n:512 * n + 512], bank[2 * c + n][:, :],
                                         xres[:, c, 512 * n:512 * n + 512], ALU.add), h_done, 2 * c + n + 1)
                dve.wait_ge(sq_done, 12 + c)
                done(v.tensor_scalar(ssq[:, c:c + 1], ssq[:, c:c + 1], 1.0 / D, EPS, ALU.mult, ALU.add), ssq_ready, 4 + c)
                dve.wait_ge(rstd_ready, 4 + c)
                dve.wait_ge(b1_spread, 32)
                done(v.tensor_scalar(un[:, c, :], acc[:, c, :], rstd[:, c:c + 1], None, ALU.mult), un_ready, 4 + c)
                ch.link(v.tensor_copy(upart[:, 0, c, :], un[:, c, :]))
                ch.link(v.tensor_tensor(ures[:, c, :], un[:, c, :], upart[:, 0, c, :], ALU.subtract))
                ch.link(v.tensor_copy(upart[:, 1, c, :], ures[:, c, :]))
                ch.link(v.tensor_tensor(ures[:, c, :], ures[:, c, :], upart[:, 1, c, :], ALU.subtract))
                ch.link(v.tensor_copy(upart[:, 2, c, :], ures[:, c, :]))

            ch.link(v.tensor_tensor(tri_lt_b, tri_le, ident, ALU.subtract))
            ch.link(v.tensor_copy(ones_b, ones))
            ch.link(v.memset(pos, -1.0))
            ch.link(v.memset(wtok, 0.0))
            ch.link(v.memset(ident3, 0.0))
            for i in range(3):
                ch.link(v.tensor_copy(ident3[E * i:E * i + E, 0:E], ident[E * i:E * i + E, E * i:E * i + E]))
            dve.wait_ge(lg_ready, 1)
            lg, mk = rt[:, 0:2, 0:E], rt[:, 4:6, 0:E]
            oh, woh = (rt[:, r0:r0 + 4, :].rearrange("p r q -> p (r q)").rearrange("p (c k e) -> p c k e", c=2, k=4)
                       for r0 in (8, 12))
            ch.link(v.tensor_tensor(lg, bank[4][:, 0:64].rearrange("p (c e) -> p c e", c=2),
                                    brt[:, :].unsqueeze(1).to_broadcast([P, 2, E]), ALU.add))
            for c in range(2):
                ch.link(v.max(topv[:, c, :], lg[:, c, :]))
                ch.link(v.max_index(topi[:, c, :], topv[:, c, :], lg[:, c, :]))
                ch.link(v.tensor_copy(topf[:, c, :], topi[:, c, :]))
            done(v.tensor_scalar(negm, topv[:, :, 0:1], -1.0, None, ALU.mult), topexp_in, 1)
            for c in range(2):
                ch.link(v.tensor_tensor(oh[:, c, :, :], iota2[:, 0:E].unsqueeze(1).to_broadcast([P, 4, E]),
                                        topf[:, c, 0:4].unsqueeze(2).to_broadcast([P, 4, E]), ALU.is_equal))
                ch.link(v.tensor_reduce(mk[:, c, :], oh[:, c, :, :].rearrange("p k e -> p e k"), AX, ALU.add))
            done(v.tensor_copy(maskb, mk), mask_ready, 1)
            dve.wait_ge(topexp_ready, 1)
            ch.link(v.reciprocal(wsum, wsum))
            ch.link(v.tensor_tensor(tope[:, :, 0:4], tope[:, :, 0:4], wsum.to_broadcast([P, 2, 4]), ALU.mult))
            for c in range(2):
                ch.link(v.tensor_tensor(woh[:, c, :, :], oh[:, c, :, :],
                                        tope[:, c, 0:4].unsqueeze(2).to_broadcast([P, 4, E]), ALU.mult))
                done(v.tensor_reduce(wtok[:, c, 0:E], woh[:, c, :, :].rearrange("p k e -> p e k"), AX, ALU.add),
                     wtok_ready, c + 1)
            dve.wait_ge(rank_ready, 1)
            ps = pos[:, :, 0:E]
            ch.link(v.scalar_tensor_tensor(ps, bank[6][:, 0:64].rearrange("p (c e) -> p c e", c=2), 1.0, mk,
                                           ALU.add, ALU.mult))
            ch.link(v.tensor_scalar(ps, ps, -1.0, None, ALU.add))
            def routing(col, val):
                for c in range(2):
                    ch.link(v.tensor_scalar(gsel[:, c, :], iota2[:, 0:CAP], pos[:, c, bass.ds(col, 1)], None, ALU.is_equal))
                    ch.link(v.tensor_scalar(gwt[:, c, :], iota2, pos[:, c, bass.ds(col, 1)], wtok[:, c, bass.ds(col, 1)],
                                            ALU.is_equal, ALU.mult))
                done(v.tensor_copy(bsel[0:3 * E, :], ident3[0:3 * E, bass.ds(col, 1)].to_broadcast([3 * E, CAP])),
                     g_ready, val)

            def scatter_add(s):
                for i in range(4):
                    c, n = divmod(i, 2)
                    dve.wait_ge(sc_ready, s * 4 + (i + 1))
                    a = acc[:, c, 512 * n:512 * n + 512]
                    done(v.tensor_tensor(a, a, bank[6 + n][:, :], ALU.add), sc_added, s * 4 + (i + 2))

            def expert(t, e, b):
                dve.wait_ge(gat_ready, t + 1)
                done(v.tensor_tensor(usel, bank[4][:, :].rearrange("p (k s) -> p k s", k=KT),
                                     col_gffn.unsqueeze(2).to_broadcast([P, KT, CAP]), ALU.mult), usel_ready, t + 1)
                scatter_add(t)
                dve.wait_ge(s2_ready, t + 1)
                routing(e + 1, t + b + 2)
                for half in range(2):
                    dve.wait_ge(slot_used, t * 12 + (4 * half + 4))
                    hv = bank[half][:, :].rearrange("p (f two) -> p f two", two=2)
                    done(v.tensor_scalar(glu[:, half, :], hv[:, :, 0], LIMIT, None, ALU.min), glu_ready, t * 2 + half + 1)
                    ch.link(v.tensor_scalar(lin[:, half, :], hv[:, :, 1], -LIMIT, LIMIT, ALU.max, ALU.min))
                    ch.link(v.scalar_tensor_tensor(lin[:, half, :], lin[:, half, :], 1.0, glu[:, half, :], ALU.add, ALU.mult))
                    dve.wait_ge(esig_ready, t * 2 + half + 1)
                    done(v.tensor_tensor(hsw[:, half, :], lin[:, half, :], sig[:, half, :], ALU.mult), hs_ready, t * 2 + half + 1)

            PER = 4 + 4
            routing(0, 1)
            done(v.tensor_reduce(ofl[:, 1:2], bank[6][:, 64:96], AX, ALU.max), sc_added, 1)
            done(v.tensor_scalar(ofl[:, 0:1].bitcast(I32), ofl[:, 1:2], float(CAP), None, ALU.is_gt), flag_ready, 1)
            base = ch.n
            with dve.Fori(0, E) as t:
                ch.base, ch.n = t * PER + base, 0
                expert(t, t, 0)
                assert ch.n == PER
            ch.base, ch.n = 0, base + E * PER
            more = dve.value_load(ofl[0:1, 0:1].bitcast(I32), min_val=0, max_val=1)
            with dve.If(more):
                after = ch.n
                EXTRA = 1 + 4
                with dve.Fori(0, PASSES - 1) as b:
                    ch.base, ch.n = b * (EXTRA + E * PER) + after, 0
                    ch.link(v.tensor_scalar(pos, pos, -float(CAP), None, ALU.add))
                    routing(0, b * (E + 1) + (E + 2))
                    assert ch.n == EXTRA
                    v.memset(ofl[:, 3:4], 0.0)
                    with dve.Fori(0, E) as e:
                        ch.base = b * (EXTRA + E * PER) + (e * PER + (after + EXTRA))
                        ch.n = 0
                        expert(b * E + e + E, e, b + 1)
            tail = Chain(dve, tail_chain)
            tail.link(v.memset(ofl[:, 2:3], 0.0))
            for i in range(4):
                c, n = divmod(i, 2)
                dve.wait_ge(last_sc_ready, i + 1)
                a = acc[:, c, 512 * n:512 * n + 512]
                done(v.tensor_tensor(a, a, bank[6 + n][:, :], ALU.add), acc_final, i + 1)
            dve.wait_ge(gfin_in, 16)
            for c in range(2):
                dve.wait_ge(sq_done, 14 + c)
                done(v.tensor_scalar(ssq[:, c:c + 1], ssq[:, c:c + 1], 1.0 / D, EPS, ALU.mult, ALU.add), ssq_ready, 6 + c)
                dve.wait_ge(rstd_ready, 6 + c)
                done(v.scalar_tensor_tensor(un[:, c, :], acc[:, c, :], rstd[:, c:c + 1], gfin, ALU.mult, ALU.mult),
                     fin_ready, c + 1)

        @block.tensor
        def _(pe):
            tn = nc.tensor

            def mm(o, lhsT, rhs, first, last):
                return tn.matmul(o, lhsT, rhs, start=first, stop=last, skip_group_check=True)

            pe.wait_ge(const_in, 16)
            pe.wait_ge(row_in, 5 * 16)
            tn.transpose(bank[4][:, 0:120], rows[0:120, 0, :], ident[0:120, 0:120])
            tn.transpose(bank[4][:, 128:160], rows[0:32, 1, :], ident[0:32, 0:32]).then_inc(rows_T, 1)
            pe.wait_ge(tab_ready, 1)
            mm(bank[5][0:HEADS, 0:VL], tab[0:NB + 1, 1, :], ohs[0:NB + 1, 0, :], True, True)
            mm(bank[6][0:HEADS, 0:VL], tab[0:NB + 1, 1, :], ohs[0:NB + 1, 1, :], True, True).then_inc(avec_ready, 1)

            def tile(p):
                if p >= 4:
                    pe.wait_ge(tile_saved, p - 3)
                return bank[p % 4]

            def ready(ins):
                ins.then_inc(tile_ready, 1)

            spans = ((0, META), (META, META + BLK), (META + BLK, NT))
            pe.wait_ge(un_ready, 3)
            for k in range(KT):
                b = tile(T_U + k)
                for c, (t0, t1) in enumerate(spans):
                    ins = tn.transpose(b[:, t0:t1], xin[0:t1 - t0, c, k * P:(k + 1) * P], ident[0:t1 - t0, 0:t1 - t0])
                ready(ins)

            def project(p, n, w, cols_n):
                b = tile(p)
                arrived(pe, n)
                for k in range(KT):
                    ins = mm(b[:, 0:cols_n], w(k), uT[:, k, NT - cols_n:NT], k == 0, k == KT - 1)
                ready(ins)

            pe.wait_ge(tile_saved, T_U + 8)
            for j in range(2):
                wk = slot_view(ck % FSLOTS, KT, 256)
                project(T_K + j, ck, lambda k, j=j, wk=wk: wk[:, k, P * j:P * j + P], NT)
            wv = slot_view(cvv % FSLOTS, KT, 256)
            for c, (t0, t1) in enumerate(spans):
                b = tile(T_V + c)
                arrived(pe, cvv)
                for k in range(KT):
                    ins = mm(b[0:t1 - t0, 0:256], uT[:, k, t0:t1], wv[:, k, :], k == 0, k == KT - 1)
                ready(ins)
            for i in range(8):
                if i == 4:
                    b = tile(T_DT)
                    pe.wait_ge(vec_in, 7 * 16)
                    for k in range(KT):
                        ins = mm(b[0:SH, 0:NT], wdt[:, k, :], uT[:, k, :], k == 0, k == KT - 1)
                    ready(ins)
                n = cq[i // 2]
                wq = slot_view(n % FSLOTS, KT, 2, 128)
                r = i % 2
                project(T_Q[i], n, lambda k, wq=wq, r=r: wq[:, k, r, :], SEQ)
                if i == 4:
                    b = tile(T_DTT)
                    pe.wait_ge(tile_saved, T_DT + 1)
                    for c, (t0, t1) in enumerate(spans):
                        ins = tn.transpose(b[0:t1 - t0, SH * c:SH * c + SH], dtT[0:SH, t0:t1], ident[0:SH, 0:SH])
                    ready(ins)

            pe.wait_ge(avec_saved, 1)
            pe.wait_ge(tile_saved, T_X)

            def att_qk(t):
                if t >= 1:
                    pe.wait_ge(logit_done, 2 * t)
                for half in range(2):
                    b, kk = bank[half], kz[:, 2 * (t // 4) + half, :]
                    mm(b[:, 0:NT], qT[:, t, BLK:SEQ], kk[:, 0:NT], True, True)
                    ins = mm(b[:, NT:LK], qT[:, t, 0:BLK], kk[:, 0:META + BLK], True, True)
                ins.then_inc(qk_ready, 1)

            def att_transpose(t):
                pe.wait_ge(p_ready, t + 1)
                if t >= 1:
                    pe.wait_ge(ptb_saved, t)
                    pe.wait_ge(ptm_saved, t)
                for half in range(2):
                    pr = logit[:, t % 2, half, :]
                    for i, k0 in enumerate((NT + META, META, META + BLK)):
                        tn.transpose(bank[4 + half][:, i * P:(i + 1) * P], pr[:, k0:k0 + P], ident)
                    for i, k0 in enumerate((NT, 0)):
                        ins = tn.transpose(bank[6][0:META, 256 * half + P * i:256 * half + P * i + P],
                                           pr[:, k0:k0 + META], ident)
                ins.then_inc(pt_ready, 1)

            def att_pv(t):
                pe.wait_ge(ptb_saved, t + 1)
                pe.wait_ge(ptm_saved, t + 1)
                if t >= 1:
                    pe.wait_ge(ya_saved, t)
                for half in range(2):
                    h = 2 * (t // 4) + half
                    o, vv = bank[7][64 * half:64 * half + 64, :], vTC[:, :, HD * h:HD * h + HD]
                    mm(o[:, 0:SEQ], vv[:, 0, :], pT[:, half, 384:640], True, False)
                    mm(o[:, 0:SEQ], vv[:, 1, :], pT[:, half, 0:256], False, False)
                    ins = mm(o[:, BLK:SEQ], vv[:, 2, :], pT[:, half, 256:384], False, True)
                ins.then_inc(pv_ready, 1)

            def gate_half(h):
                d, gi = divmod(h, 2)
                n = cg[d // 2][gi]
                if gi == 0 and d >= 2:
                    pe.wait_ge(gate_saved, d - 1)
                arrived(pe, n)
                wg = slot_view(n % FSLOTS, KT, 256)
                for k in range(KT):
                    ins = mm(bank[2 + d % 2][:, 256 * gi:256 * gi + 256], wg[:, k, P * (d % 2):P * (d % 2) + P],
                             uT[:, k, META:NT], k == 0, k == KT - 1)
                if gi:
                    ins.then_inc(gate_ready, 1)

            att_qk(0)
            half_units = iter(range(16))
            for _ in range(4):
                gate_half(next(half_units))
            pe.wait_ge(a_ready, 1)
            for i, m in enumerate((tri_le, tri_gt, ones)):
                ins = mm(bank[7][:, 96 * i:96 * i + 96], m, aa, True, True)
            ins.then_inc(cum_ready, 1)
            pe.wait_ge(decay_ready, 1)
            for _ in range(GATE_FIRST - 4):
                gate_half(next(half_units))
            for t in range(8):
                if t + 1 < 8:
                    att_qk(t + 1)
                for _ in range(gate_before[t]):
                    gate_half(next(half_units))
                att_transpose(t)
                gate_half(next(half_units))
                att_pv(t)

            pe.wait_ge(gate_saved, 8)

            def conv_transposes(i):
                if 4 <= i < 8:
                    return
                n = i if i < 4 else i - 4
                pe.wait_ge(xs_ready, i + 1)
                if n >= 2:
                    pe.wait_ge(tr_saved, n - 1)
                src = bT[:, i, :] if i < 4 else xs[:, i % 3, :]
                b = bank[4 + n % 2]
                tn.transpose(b[0:META, 0:P], src[:, 0:META], ident)
                ins = tn.transpose(b[:, P:2 * P], src[:, META:META + BLK], ident)
                if i >= 8:
                    ins = tn.transpose(b[:, 2 * P:3 * P], src[:, META + BLK:NT], ident)
                ins.then_inc(tr_ready, 1)

            def state0(g):
                pe.wait_ge(xdec0_ready, g + 1)
                if g:
                    pe.wait_ge(st0_saved, g)
                mm(bank[6][:, :], bTC[:, 0, P * g:P * g + P], xdec0, True, True).then_inc(st0_ready, 1)

            def z_tile(it):
                g, c = divmod(it, 2)
                t0 = META + BLK * c
                if it >= 1:
                    pe.wait_ge(z_saved, it)
                for h in range(2):
                    wz = slot_view(cz[g][h] % FSLOTS, 4, 512)
                    arrived(pe, cz[g][h])
                    for k in range(4):
                        kk = 4 * h + k
                        ins = mm(z_bank(it)[:, :], uT[:, kk, t0:t0 + BLK], wz[:, k, :], kk == 0, kk == KT - 1)
                ins.then_inc(z_ready, 1)

            def ssd_seg(it):
                g, c = divmod(it, 2)
                t0 = META + BLK * c
                pe.wait_ge(au_ready, it + 1)
                if it >= 1:
                    pe.wait_ge(e_ready, it)
                    pe.wait_ge(m_ready, it)
                mm(cb_bank(it)[:, 0:BLK], bT[:, g, t0:t0 + BLK], cT[:, g, t0:t0 + BLK], True, True)
                for j in range(2):
                    ins = mm(bank[j][:, :], tri_gt, au[:, it % 2, 4 * j:4 * j + 4, :], True, True)
                ins.then_inc(seg_ready, 1)

            for i in range(24 + 5):
                if i < 24:
                    n = cx[i // 2]
                    wx = slot_view(n % FSLOTS, KT, 256)
                    project(T_X + i, n, lambda k, wx=wx, i=i: wx[:, k, P * (i % 2):P * (i % 2) + P], NT)
                if i == 24:
                    pe.wait_ge(tile_saved, T_X + 21)
                    z_tile(0)
                if i == 2:
                    pe.wait_ge(ya_saved, 8)
                    pe.wait_ge(zeros_set, 2)
                if 0 <= i - 2 < 24:
                    conv_transposes(i - 2)
                if i == 25:
                    pe.wait_ge(tile_saved, T_Y)
                    ssd_seg(0)
                if i - 5 >= 11 and (i - 5 - 8) % 4 == 3:
                    state0((i - 5 - 8) // 4)

            def ssd_y(it):
                g, c = divmod(it, 2)
                t0 = META + BLK * c
                pe.wait_ge(m_ready, it + 1)
                if it >= 1:
                    pe.wait_ge(y_done, it)
                mm(bank[6][:, :], cT[:, g, t0:t0 + BLK], hst[:, g, :], True, True)
                for h in range(HPG):
                    q = h // 2
                    ins = mm(bank[2 + h // 4][:, P * (h % 4):P * (h % 4) + P], em[:, it % 2, h, :],
                             xdt[:, it % 2, 2 * q:2 * q + 2, :], True, True)
                if c == 0:
                    ins = mm(bank[7][:, :], bTC[:, 1, P * g:P * g + P], xdec, True, True)
                ins.then_inc(y_ready, 1)

            pe.wait_ge(tr_saved, 20)
            pe.wait_ge(st0_saved, 4)
            pe.wait_ge(z_saved, 1)
            for it in range(8):
                ssd_y(it)
                if it + 1 < 8:
                    ssd_seg(it + 1)
                    z_tile(it + 1)

            def branch(j, halves=(0, 1)):
                dp, bi = branch_order[j]
                arrived(pe, branch_chunk(j))
                wb = slot_view(branch_chunk(j) % FSLOTS, KT, 256)
                c0 = 0 if bi == 0 else 256
                for d in (2 * dp + h for h in halves):
                    if bi == 0 and d >= 4:
                        pe.wait_ge(m_done, d - 3)
                    for k in range(KT):
                        rhs = yaT[:, k, :] if bi == 0 else yT[:, 8 * (bi - 1) + k, :]
                        ins = mm(bank[d % 4][:, c0:c0 + 256], wb[:, k, P * (d % 2):P * (d % 2) + P], rhs,
                                 k == 0 and bi < 2, k == KT - 1 and bi != 1)
                if 1 in halves:
                    ins.then_inc(branch_used, 1)

            pe.wait_ge(e_ready, 8)
            branch(0)
            pe.wait_ge(y_done, 8)
            for i in range(16):
                pe.wait_ge(yn_ready, 4 if i < 8 else 8)
                if i >= 4:
                    pe.wait_ge(tile_saved, T_Y + i - 3)
                b = bank[4 + i % 4]
                for c in range(2):
                    ins = tn.transpose(b[:, P * c:P * c + P], zy[:, c, P * i:P * i + P], ident)
                ready(ins)
                if i in (3, 7):
                    branch(1, (i // 4,))
            for j in range(2, 12):
                if branch_order[j][1]:
                    pe.wait_ge(tile_saved, T_Y + 8 * branch_order[j][1])
                branch(j)


            def ffn_transposes(c):
                pe.wait_ge(un_ready, 4 + c)
                for k in range(KT):
                    ins = tn.transpose(bank[4 + 2 * c + k // 4][:, P * (k % 4):P * (k % 4) + P], un[:, c, P * k:P * k + P], ident)
                    if k % 4 == 3:
                        ins.then_inc(u2_ready, 1)

            def router(c):
                for k in range(KT):
                    if k % 4 == 0:
                        pe.wait_ge(u2_saved, 2 * c + k // 4 + 1)
                    ins = mm(bank[4][:, E * c:E * c + E], u2T[:, k, P * c:P * c + P], wrt[:, k, :], k == 0, k == KT - 1)
                return ins

            for c in range(2):
                for i in range(4):
                    arrived(pe, co[i])
                    if c == 0:
                        pe.wait_ge(m_done, max(6, 2 * i + 2))
                    wo = slot_view(co[i] % FSLOTS, 2, 1024)
                    for k in range(2):
                        for n in range(2):
                            ins = mm(bank[2 * c + n][:, :], mT[:, 2 * i + k, BLK * c:BLK * c + BLK],
                                     wo[:, k, 512 * n:512 * n + 512], i == 0 and k == 0, i == 3 and k == 1)
                    if i == 3:
                        ins.then_inc(h_ready, 1)
                    if c and i == 1:
                        ffn_transposes(0)
                    if c and i == 2:
                        router(0)

            ffn_transposes(1)
            router(1).then_inc(lg_ready, 1)
            pe.wait_ge(mask_ready, 1)
            mm(bank[6][:, 0:E], tri_lt_b, maskb[:, 0, :], True, True)
            mm(bank[6][:, E:2 * E], ones_b, maskb[:, 0, :], True, False)
            mm(bank[6][:, E:2 * E], tri_lt_b, maskb[:, 1, :], False, True)
            mm(bank[6][:, 2 * E:3 * E], ones_b, maskb[:, 0, :], True, False)
            mm(bank[6][:, 2 * E:3 * E], ones_b, maskb[:, 1, :], False, True).then_inc(rank_ready, 1)
            pe.wait_ge(wtok_ready, 2)
            for c in range(2):
                ins = tn.transpose(bank[5][0:E, P * c:P * c + P], wtok[:, c, 0:E], ident)
            ins.then_inc(wT_ready, 1)

            def scatter(s):
                for i in range(4):
                    c, n = divmod(i, 2)
                    if i < 2:
                        pe.wait_ge(sc_added, s * 4 + 1)
                    else:
                        pe.wait_ge(sc_added, s * 4 + i)
                    mm(bank[6 + n][:, :], s2[:, P * c:P * c + P], ysb[:, n, :], True, True).then_inc(sc_ready, 1)

            def expert(t, b, pair, odd):
                pe.wait_ge(g_ready, t + b + 1)
                for k in range(KT):
                    for part in range(3):
                        for c in range(2):
                            ins = mm(bank[4][:, CAP * k:CAP * k + CAP], upart[:, part, c, P * k:P * k + P],
                                     gsel[:, c, :], part == 0 and c == 0, part == 2 and c == 1)
                ins.then_inc(gat_ready, 1)
                for half in range(2):
                    for c in range(2):
                        c0 = 1024 * half + 512 * c
                        mm(bank[half][64 * c:64 * c + 64, :], bsel[0:3 * E, :], b1all[0:3 * E, c0:c0 + 512], True, False)
                pe.wait_ge(usel_ready, t + 1)
                for half in range(2):
                    for s_ in range(4):
                        i = 4 * half + s_
                        expert_arrived(pe, i, t, pair, odd)
                        w, _ = expert_slot(i, odd)
                        for kk in range(2):
                            for c in range(2):
                                k = 2 * s_ + kk
                                ins = mm(bank[half][64 * c:64 * c + 64, :], usel[:, k, :],
                                         w[:, kk, 512 * c:512 * c + 512], False, k == KT - 1)
                        ins.then_inc(slot_used, 1)
                    if half == 0:
                        pe.wait_ge(ye_saved, t * 2 + 2)
                        scatter(t)
                        for c in range(2):
                            ins = tn.transpose(bank[5][:, P * c:P * c + P], gwt[:, c, :], ident)
                        ins.then_inc(s2_ready, 1)
                pe.wait_ge(s2_saved, t + 1)
                for half in range(2):
                    pe.wait_ge(hs_ready, t * 2 + half + 1)
                    if half:
                        pe.wait_ge(hT_saved, t * 2 + 1)
                    for q in range(2):
                        ins = tn.transpose(bank[5][:, P * q:P * q + P], hsw[:, half, P * q:P * q + P], ident)
                    ins.then_inc(hT_ready, 1)
                    pe.wait_ge(hT_saved, t * 2 + half + 1)
                    for q in range(2):
                        i = 8 + 2 * half + q
                        expert_arrived(pe, i, t, pair, odd)
                        w, _ = expert_slot(i, odd)
                        for n in range(2):
                            for c in range(2):
                                ins = mm(bank[2 + n][64 * c:64 * c + 64, :], hT[:, half, q, 64 * c:64 * c + 64],
                                         w[:, c, 512 * n:512 * n + 512], half == 0 and q == 0, half == 1 and q == 1)
                        ins.then_inc(slot_used, 1)

            pe.wait_ge(b2_in, 16)
            pe.wait_ge(b1_spread, 32)
            with pe.Fori(0, E // 2) as pair:
                for odd in range(2):
                    expert(pair * 2 + odd, 0, pair, odd)
            more = pe.value_load(ofl[0:1, 0:1].bitcast(I32), min_val=0, max_val=1)
            with pe.If(more):
                with pe.Fori(0, PASSES - 1) as b:
                    with pe.Fori(0, E // 2) as pair:
                        for odd in range(2):
                            expert(b * E + pair * 2 + (E + odd), b + 1, b * (E // 2) + pair + E // 2, odd)
                pe.wait_ge(ye_saved, 2 * PASSES * E + 2)
                pe.wait_ge(sc_added, 4 * PASSES * E + 1)
            pe.wait_ge(ye_saved, 2 * E + 2)
            pe.wait_ge(sc_added, 4 * E + 1)
            for i in range(4):
                c, n = divmod(i, 2)
                if i >= 2:
                    pe.wait_ge(acc_final, i - 1)
                mm(bank[6 + n][:, :], s2[:, P * c:P * c + P], ysb[:, n, :], True, True).then_inc(last_sc_ready, 1)


def kernel(**inputs):
    import concourse.bacc as bacc
    from concourse.bass_utils import run_bass_kernel_spmd

    flat = {
        "x": inputs["x"].reshape(SEQ, D), "meta": inputs["meta_tokens"], "rel": inputs["rel_bias"],
        "g_mix": inputs["norm_mix_g"].reshape(D), "w_in": inputs["w_in"][0], "sinks": inputs["attn_sinks"].reshape(-1),
        "conv_w": inputs["conv_w"][0], "conv_b": inputs["conv_b"].reshape(-1), "dt_bias": inputs["dt_bias"].reshape(-1),
        "a_log": inputs["a_log"].reshape(-1), "d_skip": inputs["d_skip"].reshape(-1),
        "g_ssm": inputs["ssm_norm_g"].reshape(-1), "w_att": inputs["w_attn_br"][0], "w_ssm": inputs["w_ssm_br"][0],
        "w_out": inputs["w_out"][0], "g_ffn": inputs["norm_ffn_g"].reshape(-1), "w_rt": inputs["w_router"][0],
        "b_rt": inputs["b_router"].reshape(-1), "w1": inputs["w_exp_in"][0], "b1": inputs["b_exp_in"][0],
        "w2": inputs["w_exp_out"][0], "b2": inputs["b_exp_out"][0], "g_fin": inputs["norm_final_g"],
    }
    i = np.arange(P)
    squares = np.stack([i[:, None] == i[None, :], i[:, None] <= i[None, :], i[:, None] > i[None, :],
                        np.ones((P, P)), np.broadcast_to(i % CAP, (P, P))], axis=1).astype(np.float32)
    flat["c_sq"] = squares
    flat["c_oh"] = distance_one_hots()
    nc = bacc.Bacc("TRN2", target_bir_lowering=False, num_devices=1)
    arrays, args = {}, {}
    for name, a in flat.items():
        a = np.ascontiguousarray(a)
        arrays["in_" + name] = a
        args[name] = nc.dram_tensor("in_" + name, a.shape, mybir.dt.from_np(a.dtype), kind="ExternalInput").ap()
    args["out"] = nc.dram_tensor("out_0", (SEQ, D), F32, kind="ExternalOutput").ap()
    hybrid_layer(nc, **args)
    r = run_bass_kernel_spmd(nc, [arrays], core_ids=[0])
    return r.results[0]["out_0"].reshape(1, SEQ, D)
```
